# Optimizing a Trainium2 kernel written in Bass

```python
import jax, jax.numpy as jnp
from jax import lax
import numpy as np
import math

D_MODEL = 2048
BATCH = 1
SEQ = 256
DEPTH = 1

HEAD_DIM = 64
A_Q_HEADS = 12
A_KV_HEADS = 4
A_GROUP = A_Q_HEADS // A_KV_HEADS
WINDOW = 128
BLOCK = 128
B_HEADS = 12
C_HEADS = 4
C_HEAD_DIM = 128
MEM_TOKENS = 256
N_BRANCHES = 3
A_WIDTH = A_Q_HEADS * HEAD_DIM
A_KV_WIDTH = A_KV_HEADS * HEAD_DIM
B_WIDTH = B_HEADS * HEAD_DIM
C_WIDTH = C_HEADS * C_HEAD_DIM
EPS = 1e-6
NEG = -1e30

IN_SIZES = (A_WIDTH, A_KV_WIDTH, A_KV_WIDTH, A_WIDTH,
            B_WIDTH, B_WIDTH, B_WIDTH, B_WIDTH, B_HEADS,
            C_WIDTH, C_WIDTH,
            N_BRANCHES * D_MODEL)
IN_WIDTH = sum(IN_SIZES)
IN_OFFSETS = tuple(int(o) for o in np.cumsum(IN_SIZES)[:-1])


def rms_norm(x, gain):
    x32 = x.astype(jnp.float32)
    y = x32 * lax.rsqrt(jnp.mean(x32 * x32, axis=-1, keepdims=True) + EPS)
    return (y * gain.astype(jnp.float32)).astype(x.dtype)

def alibi_slopes(n_heads):
    h = jnp.arange(1, n_heads + 1, dtype=jnp.float32)
    return jnp.exp2(-8.0 * h / n_heads)

def sliding_window_attention(q, k, v, q_gain, k_gain, sinks):
    b, s, _, d = q.shape
    nb = s // BLOCK
    q = rms_norm(q, q_gain).astype(jnp.float32)
    k = rms_norm(k, k_gain).astype(jnp.float32)
    v = v.astype(jnp.float32)
    qb = q.reshape(b, nb, BLOCK, A_KV_HEADS, A_GROUP, d)
    pad = jnp.zeros((b, BLOCK, A_KV_HEADS, d), jnp.float32)
    kp = jnp.concatenate([pad, k], axis=1).reshape(b, nb + 1, BLOCK, A_KV_HEADS, d)
    vp = jnp.concatenate([pad, v], axis=1).reshape(b, nb + 1, BLOCK, A_KV_HEADS, d)
    kb = jnp.concatenate([kp[:, :-1], kp[:, 1:]], axis=2)
    vb = jnp.concatenate([vp[:, :-1], vp[:, 1:]], axis=2)
    scores = jnp.einsum('bnqkgd,bnskd->bnkgqs', qb, kb) * (d ** -0.5)
    qi = jnp.arange(BLOCK)[:, None]
    kj = jnp.arange(2 * BLOCK)[None, :]
    rel = qi + BLOCK - kj
    key_pos = jnp.arange(nb)[:, None, None] * BLOCK - BLOCK + kj[None]
    valid = (rel >= 0) & (rel < WINDOW) & (key_pos >= 0)
    slopes = alibi_slopes(A_Q_HEADS).reshape(A_KV_HEADS, A_GROUP)
    bias = -slopes[:, :, None, None] * rel.astype(jnp.float32)
    scores = jnp.where(valid[None, :, None, None], scores + bias[None, None], NEG)
    sink = sinks.astype(jnp.float32).reshape(A_KV_HEADS, A_GROUP)[None, None, :, :, None, None]
    m = jnp.maximum(jnp.max(scores, axis=-1, keepdims=True), sink)
    p = jnp.exp(scores - m)
    denom = jnp.sum(p, axis=-1, keepdims=True) + jnp.exp(sink - m)
    out = jnp.einsum('bnkgqs,bnskd->bnqkgd', p / denom, vb)
    return out.reshape(b, s, A_Q_HEADS * d)

def forgetting_attention(q, k, v, f_logit, q_gain, k_gain):
    b, s, h, d = q.shape
    nb = s // BLOCK
    q = rms_norm(q, q_gain).astype(jnp.float32)
    k = rms_norm(k, k_gain).astype(jnp.float32)
    v = v.astype(jnp.float32)
    log_f = jax.nn.log_sigmoid(f_logit.astype(jnp.float32))
    c = jnp.cumsum(log_f, axis=1).transpose(0, 2, 1)
    q_blocks = q.reshape(b, nb, BLOCK, h, d).transpose(1, 0, 2, 3, 4)
    cq_blocks = c.reshape(b, h, nb, BLOCK).transpose(2, 0, 1, 3)
    key_pos = jnp.arange(s)
    scale = d ** -0.5

    def block_fn(args):
        qb, cqb, n = args
        sc = jnp.einsum('bqhd,bshd->bhqs', qb, k) * scale + cqb[..., None] - c[:, :, None, :]
        qpos = n * BLOCK + jnp.arange(BLOCK)
        mask = key_pos[None, :] <= qpos[:, None]
        sc = jnp.where(mask[None, None], sc, NEG)
        p = jax.nn.softmax(sc, axis=-1)
        return jnp.einsum('bhqs,bshd->bqhd', p, v)

    out = lax.map(block_fn, (q_blocks, cq_blocks, jnp.arange(nb)))
    return out.transpose(1, 0, 2, 3, 4).reshape(b, s, h * d)

def memory_attention(q, mk, mv, q_gain, k_gain):
    b, s, h, d = q.shape
    q = rms_norm(q, q_gain).astype(jnp.float32)
    mk = rms_norm(mk, k_gain).astype(jnp.float32)
    sc = jnp.einsum('bthd,bmhd->bhtm', q, mk) * (d ** -0.5)
    p = jax.nn.softmax(sc, axis=-1)
    out = jnp.einsum('bhtm,bmhd->bthd', p, mv.astype(jnp.float32))
    return out.reshape(b, s, h * d)

def hybrid_layer(x, mem, norm_gain, mem_norm_gain, w_in, b_forget,
                 q_gain_a, k_gain_a, sinks_a, q_gain_b, k_gain_b, q_gain_c, k_gain_c,
                 w_mem_kv, w_branch_a, w_branch_b, w_branch_c, w_out):
    b, s, _ = x.shape
    hn = rms_norm(x, norm_gain)
    proj = hn @ w_in
    (qa, ka, va, za, qb, kb, vb, zb, fb, qc, zc, gate_logits) = jnp.split(proj, IN_OFFSETS, axis=-1)

    ya = sliding_window_attention(qa.reshape(b, s, A_Q_HEADS, HEAD_DIM),
                                  ka.reshape(b, s, A_KV_HEADS, HEAD_DIM),
                                  va.reshape(b, s, A_KV_HEADS, HEAD_DIM),
                                  q_gain_a, k_gain_a, sinks_a).astype(x.dtype)
    ua = (ya * jax.nn.silu(za)) @ w_branch_a

    yb = forgetting_attention(qb.reshape(b, s, B_HEADS, HEAD_DIM),
                              kb.reshape(b, s, B_HEADS, HEAD_DIM),
                              vb.reshape(b, s, B_HEADS, HEAD_DIM),
                              fb + b_forget, q_gain_b, k_gain_b).astype(x.dtype)
    ub = (yb * jax.nn.silu(zb)) @ w_branch_b

    mkv = rms_norm(mem, mem_norm_gain) @ w_mem_kv
    mk, mv = jnp.split(mkv, 2, axis=-1)
    mlen = mem.shape[1]
    yc = memory_attention(qc.reshape(b, s, C_HEADS, C_HEAD_DIM),
                          mk.reshape(b, mlen, C_HEADS, C_HEAD_DIM),
                          mv.reshape(b, mlen, C_HEADS, C_HEAD_DIM),
                          q_gain_c, k_gain_c).astype(x.dtype)
    uc = (yc * jax.nn.silu(zc)) @ w_branch_c

    g = jax.nn.sigmoid(gate_logits.reshape(b, s, N_BRANCHES, D_MODEL))
    y = g[:, :, 0] * ua + g[:, :, 1] * ub + g[:, :, 2] * uc
    return x + y @ w_out

def first_inputs(seed: int = 0) -> dict:
    key = jax.random.key(seed)
    ks = jax.random.split(key, 20)
    f32 = jnp.float32
    nrm = lambda k, shape: jax.random.normal(k, shape, f32)
    return {
        "x": nrm(ks[0], (BATCH, SEQ, D_MODEL)),
        "mem": nrm(ks[1], (BATCH, MEM_TOKENS, D_MODEL)),
        "norm_gain": 1.0 + 0.02 * nrm(ks[2], (DEPTH, D_MODEL)),
        "mem_norm_gain": 1.0 + 0.02 * nrm(ks[3], (DEPTH, D_MODEL)),
        "w_in": nrm(ks[4], (DEPTH, D_MODEL, IN_WIDTH)) * D_MODEL ** -0.5,
        "b_forget": 3.0 + 0.5 * nrm(ks[5], (DEPTH, B_HEADS)),
        "q_gain_a": 1.0 + 0.02 * nrm(ks[6], (DEPTH, HEAD_DIM)),
        "k_gain_a": 1.0 + 0.02 * nrm(ks[7], (DEPTH, HEAD_DIM)),
        "sinks_a": 0.5 * nrm(ks[8], (DEPTH, A_Q_HEADS)),
        "q_gain_b": 1.0 + 0.02 * nrm(ks[9], (DEPTH, HEAD_DIM)),
        "k_gain_b": 1.0 + 0.02 * nrm(ks[10], (DEPTH, HEAD_DIM)),
        "q_gain_c": 1.0 + 0.02 * nrm(ks[11], (DEPTH, C_HEAD_DIM)),
        "k_gain_c": 1.0 + 0.02 * nrm(ks[12], (DEPTH, C_HEAD_DIM)),
        "w_mem_kv": nrm(ks[13], (DEPTH, D_MODEL, 2 * C_WIDTH)) * D_MODEL ** -0.5,
        "w_branch_a": nrm(ks[14], (DEPTH, A_WIDTH, D_MODEL)) * A_WIDTH ** -0.5,
        "w_branch_b": nrm(ks[15], (DEPTH, B_WIDTH, D_MODEL)) * B_WIDTH ** -0.5,
        "w_branch_c": nrm(ks[16], (DEPTH, C_WIDTH, D_MODEL)) * C_WIDTH ** -0.5,
        "w_out": nrm(ks[17], (DEPTH, D_MODEL, D_MODEL)) * D_MODEL ** -0.5,
    }

def first_block(x, mem, norm_gain, mem_norm_gain, w_in, b_forget,
              q_gain_a, k_gain_a, sinks_a, q_gain_b, k_gain_b, q_gain_c, k_gain_c,
              w_mem_kv, w_branch_a, w_branch_b, w_branch_c, w_out):
    for layer in range(DEPTH):
        x = hybrid_layer(x, mem, norm_gain[layer], mem_norm_gain[layer], w_in[layer], b_forget[layer],
                         q_gain_a[layer], k_gain_a[layer], sinks_a[layer],
                         q_gain_b[layer], k_gain_b[layer], q_gain_c[layer], k_gain_c[layer],
                         w_mem_kv[layer], w_branch_a[layer], w_branch_b[layer], w_branch_c[layer],
                         w_out[layer])
    return x


N_MEM = 256
CONV_WIDTH = D_MODEL // 2
CONV_K = 3
HG_HEADS = 8
HG_KEY_DIM = 128
HG_VAL_DIM = D_MODEL // 2 // HG_HEADS
HG_FWIDTH = HG_HEADS * HG_KEY_DIM
HG_VWIDTH = HG_HEADS * HG_VAL_DIM
HG_CHUNK = 64
LOG_TINY = 1e-30
MEM_HEADS = 4
MEM_HEAD_DIM = D_MODEL // 2 // MEM_HEADS
MEM_WIDTH = MEM_HEADS * MEM_HEAD_DIM
BRANCH_WIDTH = D_MODEL // 2
N_BRANCH = 3
FFN_DIM = 256 * (-(-8 * D_MODEL // (3 * 256)))
RMS_EPS = 1e-6
IN_SPLITS = [CONV_WIDTH, CONV_WIDTH, CONV_WIDTH,
             HG_FWIDTH, HG_FWIDTH, HG_VWIDTH, HG_VWIDTH,
             MEM_WIDTH,
             D_MODEL, D_MODEL, D_MODEL]
N_IN = sum(IN_SPLITS)


def rms_norm_2(x, w):
    xf = x.astype(jnp.float32)
    y = xf * lax.rsqrt(jnp.mean(xf * xf, axis=-1, keepdims=True) + RMS_EPS)
    return (y * w.astype(jnp.float32)).astype(x.dtype)

def causal_dwconv3(u, w):
    s = u.shape[1]
    up = jnp.pad(u, ((0, 0), (CONV_K - 1, 0), (0, 0)))
    return up[:, :s] * w[0] + up[:, 1:s + 1] * w[1] + up[:, 2:] * w[2]

def hgrn2_chunked(q, k, v, log_f):
    bsz, s, h, dk = q.shape
    dv = v.shape[-1]
    n = s // HG_CHUNK

    def chunks(a):
        a = a.astype(jnp.float32).reshape(bsz, n, HG_CHUNK, h, a.shape[-1])
        return jnp.moveaxis(a, 1, 0)

    qc, kc, vc = chunks(q), chunks(k), chunks(v)
    bc = jnp.cumsum(chunks(log_f), axis=2)
    mask = jnp.tril(jnp.ones((HG_CHUNK, HG_CHUNK), dtype=bool))[None, :, :, None, None]

    def step(state, inp):
        qi, ki, vi, bi = inp
        o_inter = jnp.einsum('bchk,bhkv->bchv', qi * jnp.exp(bi), state)
        diff = bi[:, :, None] - bi[:, None, :]
        decay = jnp.where(mask, jnp.exp(jnp.minimum(diff, 0.0)), 0.0)
        scores = jnp.einsum('bihk,bijhk,bjhk->bhij', qi, decay, ki)
        o_intra = jnp.einsum('bhij,bjhv->bihv', scores, vi)
        b_last = bi[:, -1]
        k_to_end = ki * jnp.exp(b_last[:, None] - bi)
        state = jnp.exp(b_last)[..., None] * state + jnp.einsum('bjhk,bjhv->bhkv', k_to_end, vi)
        return state, o_inter + o_intra

    s0 = jnp.zeros((bsz, h, dk, dv), jnp.float32)
    _, o = lax.scan(step, s0, (qc, kc, vc, bc))
    return jnp.moveaxis(o, 0, 1).reshape(bsz, s, h, dv)

def second_inputs(seed: int = 0) -> dict:
    key = jax.random.key(seed)
    ks = jax.random.split(key, 20)

    def nrm(k, shape, scale):
        return jax.random.normal(k, shape, jnp.float32) * scale

    def gain(k):
        return 1.0 + nrm(k, (DEPTH, D_MODEL), 0.02)

    return {
        'x': nrm(ks[0], (BATCH, SEQ, D_MODEL), 1.0),
        'mem': nrm(ks[1], (BATCH, N_MEM, D_MODEL), 1.0),
        'w_in': nrm(ks[2], (DEPTH, D_MODEL, N_IN), D_MODEL ** -0.5),
        'conv_mix_w': nrm(ks[3], (DEPTH, CONV_K, CONV_WIDTH), CONV_K ** -0.5),
        'hg_lower_bounds': nrm(ks[4], (DEPTH, HG_FWIDTH), 0.1),
        'hg_norm_w': 1.0 + nrm(ks[5], (DEPTH, HG_VWIDTH), 0.02),
        'w_mem_kv': nrm(ks[6], (DEPTH, D_MODEL, 2 * MEM_WIDTH), D_MODEL ** -0.5),
        'w_branch': nrm(ks[7], (DEPTH, N_BRANCH, BRANCH_WIDTH, D_MODEL), BRANCH_WIDTH ** -0.5),
        'w_out': nrm(ks[8], (DEPTH, D_MODEL, D_MODEL), D_MODEL ** -0.5),
        'norm_mix_pre': gain(ks[9]),
        'norm_mix_post': gain(ks[10]),
        'norm_mem': gain(ks[11]),
        'norm_ffn_pre': gain(ks[12]),
        'norm_ffn_post': gain(ks[13]),
        'w_ffn_up': nrm(ks[14], (DEPTH, D_MODEL, 2 * FFN_DIM), D_MODEL ** -0.5),
        'conv_ffn_w': nrm(ks[15], (DEPTH, CONV_K, FFN_DIM), CONV_K ** -0.5),
        'conv_ffn_b': nrm(ks[16], (DEPTH, FFN_DIM), 0.01),
        'w_ffn_down': nrm(ks[17], (DEPTH, FFN_DIM, D_MODEL), FFN_DIM ** -0.5),
    }

def second_block(x, mem, w_in, conv_mix_w, hg_lower_bounds, hg_norm_w, w_mem_kv, w_branch, w_out,
              norm_mix_pre, norm_mix_post, norm_mem, norm_ffn_pre, norm_ffn_post,
              w_ffn_up, conv_ffn_w, conv_ffn_b, w_ffn_down):
    bsz, s, _ = x.shape
    dt = x.dtype
    lb_soft = jax.nn.softmax(hg_lower_bounds.astype(jnp.float32), axis=0)
    lb_all = jnp.cumsum(lb_soft, axis=0) - lb_soft[0]
    split_idx = list(np.cumsum(IN_SPLITS)[:-1])

    for l in range(DEPTH):
        h = rms_norm_2(x, norm_mix_pre[l])
        proj = jnp.einsum('bsd,dn->bsn', h, w_in[l])
        (cb, cc, cv, hq, hf, hi, hg, mq, ga, gb, gm) = jnp.split(proj, split_idx, axis=-1)

        y_a = cb * causal_dwconv3(cc * cv, conv_mix_w[l])

        q = jax.nn.silu(hq).reshape(bsz, s, HG_HEADS, HG_KEY_DIM) * (HG_KEY_DIM ** -0.5)
        lb = jnp.clip(lb_all[l], 0.0, 1.0).reshape(HG_HEADS, HG_KEY_DIM)
        zf = hf.astype(jnp.float32).reshape(bsz, s, HG_HEADS, HG_KEY_DIM)
        log_f = jnp.logaddexp(jnp.log(lb + LOG_TINY), jnp.log1p(-lb) + jax.nn.log_sigmoid(zf))
        k = -jnp.expm1(log_f)
        vin = hi.reshape(bsz, s, HG_HEADS, HG_VAL_DIM)
        o = hgrn2_chunked(q, k, vin, log_f)
        o = o * lax.rsqrt(jnp.mean(o * o, axis=-1, keepdims=True) + RMS_EPS)
        o = o * hg_norm_w[l].astype(jnp.float32).reshape(HG_HEADS, HG_VAL_DIM)
        y_b = (o.reshape(bsz, s, HG_VWIDTH) * jax.nn.silu(hg.astype(jnp.float32))).astype(dt)

        mh = rms_norm_2(mem, norm_mem[l])
        mk, mv = jnp.split(jnp.einsum('bmd,dn->bmn', mh, w_mem_kv[l]), 2, axis=-1)
        qh = mq.reshape(bsz, s, MEM_HEADS, MEM_HEAD_DIM)
        kh = mk.reshape(bsz, N_MEM, MEM_HEADS, MEM_HEAD_DIM)
        vh = mv.reshape(bsz, N_MEM, MEM_HEADS, MEM_HEAD_DIM)
        sc = jnp.einsum('bshd,bmhd->bhsm', qh, kh).astype(jnp.float32) * (MEM_HEAD_DIM ** -0.5)
        p = jax.nn.softmax(sc, axis=-1).astype(dt)
        y_m = jnp.einsum('bhsm,bmhd->bshd', p, vh).reshape(bsz, s, MEM_WIDTH)

        merged = (jax.nn.sigmoid(ga) * jnp.einsum('bsc,cd->bsd', y_a, w_branch[l, 0])
                  + jax.nn.sigmoid(gb) * jnp.einsum('bsc,cd->bsd', y_b, w_branch[l, 1])
                  + jax.nn.sigmoid(gm) * jnp.einsum('bsc,cd->bsd', y_m, w_branch[l, 2]))
        mix_out = jnp.einsum('bsd,de->bse', merged, w_out[l])
        x = x + rms_norm_2(mix_out, norm_mix_post[l])

        h2 = rms_norm_2(x, norm_ffn_pre[l])
        up_g, up_v = jnp.split(jnp.einsum('bsd,df->bsf', h2, w_ffn_up[l]), 2, axis=-1)
        act = jax.nn.gelu(causal_dwconv3(up_g, conv_ffn_w[l]) + conv_ffn_b[l], approximate=True) * up_v
        ffn_out = jnp.einsum('bsf,fd->bsd', act, w_ffn_down[l])
        x = x + rms_norm_2(ffn_out, norm_ffn_post[l])
    return x


def setup_inputs(seed=0):
    out = dict(first_inputs(seed))
    for name, value in second_inputs(seed + 1).items():
        if name != "x":
            out[name + "_2"] = value
    return out


def reference(
    x, mem, norm_gain, mem_norm_gain, w_in, b_forget, q_gain_a, k_gain_a, sinks_a, q_gain_b,
    k_gain_b, q_gain_c, k_gain_c, w_mem_kv, w_branch_a, w_branch_b, w_branch_c, w_out, mem_2,
    w_in_2, conv_mix_w_2, hg_lower_bounds_2, hg_norm_w_2, w_mem_kv_2, w_branch_2, w_out_2,
    norm_mix_pre_2, norm_mix_post_2, norm_mem_2, norm_ffn_pre_2, norm_ffn_post_2, w_ffn_up_2,
    conv_ffn_w_2, conv_ffn_b_2, w_ffn_down_2,
):
    x = first_block(
        x, mem, norm_gain, mem_norm_gain, w_in, b_forget, q_gain_a, k_gain_a, sinks_a, q_gain_b,
        k_gain_b, q_gain_c, k_gain_c, w_mem_kv, w_branch_a, w_branch_b, w_branch_c, w_out,
    )
    return second_block(
        x, mem_2, w_in_2, conv_mix_w_2, hg_lower_bounds_2, hg_norm_w_2, w_mem_kv_2, w_branch_2,
        w_out_2, norm_mix_pre_2, norm_mix_post_2, norm_mem_2, norm_ffn_pre_2, norm_ffn_post_2,
        w_ffn_up_2, conv_ffn_w_2, conv_ffn_b_2, w_ffn_down_2,
    )


_drawn_inputs = setup_inputs


def setup_inputs(seed=0):
    import zlib

    import numpy as np

    out = dict(_drawn_inputs(seed))
    spreads = {}
    factors = {'norm_gain': 6.48,
     'mem_norm_gain': 8.0,
     'q_gain_a': 8.0,
     'k_gain_a': 8.0,
     'sinks_a': 54.904,
     'q_gain_b': 8.0,
     'k_gain_b': 8.0,
     'q_gain_c': 8.0,
     'k_gain_c': 8.0,
     'hg_norm_w_2': 200.0,
     'norm_mix_post_2': 104.276,
     'norm_mem_2': 200.0,
     'norm_ffn_pre_2': 77.742,
     'norm_ffn_post_2': 165.503,
     'conv_ffn_b_2': 200.0,
     'conv_mix_w_2': 4.508,
     'norm_mix_pre_2': 8.0,
     'mem_2': 2.878,
     'w_mem_kv_2': 2.872}
    for name, (base, spread) in spreads.items():
        noise = np.random.default_rng([zlib.crc32(name.encode()), seed]).standard_normal(out[name].shape)
        drawn = base * np.exp(spread * noise) if base else spread * noise
        out[name] = __import__('jax').numpy.asarray(drawn.astype(out[name].dtype))
    for name, factor in factors.items():
        out[name] = (out[name] * factor).astype(out[name].dtype)
    return out
```

```python
from contextlib import ExitStack

import numpy as np

import concourse.bass as bass
from concourse import mybir

F32 = mybir.dt.float32
F32R = mybir.dt.float32r
U8 = mybir.dt.uint8
ALU = mybir.AluOpType
ACT = mybir.ActivationFunctionType
AX = mybir.AxisListType.X

P = 128
D = 2048
S = 256
T = S // P
KT = D // P
NB = 512
EPS = 1e-6
NEG = -1e30
RING = 4
LEAD = 3

HD = 64
AH, AKV, AG = 12, 4, 3
BH = 12
CH, CD = 4, 128
AW, AKW, BW, CW = AH * HD, AKV * HD, BH * HD, CH * CD
A_COLS = 2 * AW + 2 * AKW
B_AT = A_COLS
F_AT = B_AT + 4 * BW
C_AT = F_AT + BH
G_AT = C_AT + 2 * CW

BR = D // 2
HH, HK = 8, 128
MH, MD = 4, 256
FF = 5632
FT = FF // P
HQ_AT, MQ_AT, G2_AT = 3 * BR, 7 * BR, 8 * BR
LOG_TINY = float(np.log(np.float32(1e-30)))
LEVELS = [1, 2, 4, 8, 16, 32, 64]

V_NORM, V_MEM, V_MIX, V_MEM2, V_FFN = (0, 0), (0, 16), (0, 32), (0, 48), (0, 64)
V_CONV, V_HG = (0, 80), (0, 104)
V_FW = [(1, 0), (1, FT), (2, 0)]
V_FB = (2, FT)
V_QK = 2 * FT
V_ROWS = [112, V_QK + 6, 2 * FT]

K_ID, K_REL, K_MASK, K_TRI, K_ONE, K_SLOPE = 0, 128, 512, 640, 768, 896
K_COLS = K_SLOPE + AH


def shape_constants():
    p = np.arange(P)
    c = np.zeros((P, K_COLS), np.float32)
    c[:, K_ID:K_ID + P] = np.eye(P)
    own = p[:, None] - p[None, :]
    before = own + P
    far = np.float32(1e34)
    own_rel = np.where(own >= 0, own, far)
    c[:, K_REL:K_REL + P] = own_rel
    c[:, K_REL + P:K_REL + 2 * P] = np.where(before < P, before, far)
    c[:, K_REL + 2 * P:K_REL + 3 * P] = own_rel
    c[:, K_MASK:K_MASK + P] = np.where(own >= 0, 0, NEG)
    c[:, K_TRI:K_TRI + P] = p[:, None] <= p[None, :]
    c[:, K_ONE:K_ONE + P] = 1
    c[:, K_SLOPE:] = -np.exp2(-8.0 * np.arange(1, AH + 1) / AH).astype(np.float32)
    j, i = p[:, None], p[None, :]
    masks = [(j // (2 * s) == i // (2 * s)) & (j // s % 2 == 0) & (i // s % 2 == 1) for s in LEVELS]
    return c, np.concatenate(masks, 1).astype(np.float32)


class Stage:

    def __init__(self, sem, name, **steps):
        self.steps = steps
        self.sems = {e: sem(f"{name}_{e}") for e in steps}
        self.place = {e: 0 for e in steps}

    def after(self, engine, step, it=0):
        n = self.steps[engine]
        return self.sems[engine], it * len(n) + n.index(step) + 1

    def mark(self, engine, step):
        n = self.steps[engine]
        assert n[self.place[engine]] == step, (n[self.place[engine]], step)
        self.place[engine] = (self.place[engine] + 1) % len(n)
        return self.sems[engine], 1


class Phase:

    def __init__(self, name, times, sizes, before):
        self.name, self.times, self.sizes, self.n = name, times, sizes, len(sizes)
        self.c0 = before.c0 + before.n * before.times if before else 0
        self.b0 = before.b0 + before.blocks * before.times if before else 0
        self.blocks = 0

    def chunk(self, i, j):
        return i * self.n + (self.c0 + j)

    def use(self, i, block):
        return i * (self.blocks // 2) + (self.b0 + block) // 2


FULL = [2] * (KT // 2)


def plan():
    gate_a = FULL + [2, 2, 1, 1]
    gate_c = FULL + [1, 1, 1, 1]
    gate_2 = FULL + [2, 2, 2, 2]
    down = [2] * 20 + [1] * 4
    spec = [
        ("a_proj", 2, FULL * 2, 2), ("b_proj", 3, FULL * 2, 2), ("c_proj", 1, FULL * 4, 4),
        ("gate_a", 4, gate_a, 2), ("gate_b", 4, gate_a, 2), ("gate_c", 4, gate_c, 2),
        ("out", 1, FULL * 4, 4), ("mem_kv_2", 1, FULL * 4, 4),
        ("conv_proj", 3, FULL * 2, 2), ("mq_proj", 1, FULL * 2, 2), ("hg_proj", 4, FULL * 2, 2),
        ("gate_conv", 4, gate_2, 2), ("gate_mem", 4, gate_2, 2), ("gate_hg", 4, gate_2, 2),
        ("out_2", 1, FULL * 4, 4), ("ffn_first", 1, FULL * 2, 2), ("ffn_up", FT // 4 - 1, FULL * 2, 2),
        ("ffn_down", 2, down * 2, 2),
    ]
    phases, before = {}, None
    for name, times, sizes, blocks in spec:
        before = Phase(name, times, sizes, before)
        before.blocks = blocks
        phases[name] = before
    return phases, before.c0 + before.n * before.times


def two_blocks(
    nc, x, mem, norm_gain, mem_norm_gain, w_in, b_forget, q_gain_a, k_gain_a, sinks_a, q_gain_b, k_gain_b,
    q_gain_c, k_gain_c, w_mem_kv, w_branch_a, w_branch_b, w_branch_c, w_out, mem_2, w_in_2, conv_mix_w_2,
    hg_norm_w_2, w_mem_kv_2, w_branch_2, w_out_2, norm_mix_pre_2, norm_mix_post_2, norm_mem_2,
    norm_ffn_pre_2, norm_ffn_post_2, w_ffn_up_2, conv_ffn_w_2, conv_ffn_b_2, w_ffn_down_2,
    constants, level_masks, out,
):
    phases, chunks = plan()
    ctx = ExitStack()

    def sem(name):
        return ctx.enter_context(nc.semaphore(name))

    base = (nc.sbuf_base + 31) // 32 * 32
    names = set()

    def at(name, offset, shape, dt=F32):
        assert name not in names
        names.add(name)
        return nc.alloc_sbuf_tensor_at(name, [P, *shape], dt, offset=base + offset)

    CHUNK = 2 * NB * 4
    TK = S * 4
    RAW_AT, HI_AT, LO_AT = 0, RING * CHUNK, 2 * RING * CHUNK
    X_AT = 3 * RING * CHUNK
    CONST_AT = X_AT + 2 * KT * TK
    O_AT = CONST_AT + 11776
    W_AT = O_AT + 48 * TK

    raw = at("raw", RAW_AT, [RING, 2, NB])
    hi = at("hi", HI_AT, [RING, 2, NB], F32R)
    lo = at("lo", LO_AT, [RING, 2, NB], F32R)
    xh = at("xh", X_AT, [KT, S], F32R)
    xl = at("xl", X_AT + KT * TK, [KT, S], F32R)
    oh = at("oh", O_AT, [24, S], F32R)
    ol = at("ol", O_AT + 24 * TK, [24, S], F32R)
    m2h = at("m2h", W_AT + 16384, [KT, S], F32R)
    m2l = at("m2l", W_AT + 32768, [KT, S], F32R)
    fh = at("fh", O_AT, [FT, S], F32R)
    fl = at("fl", O_AT + FT * TK, [FT, S], F32R)

    cursor = [CONST_AT]

    def const(name, shape, dt=F32):
        size = int(np.prod(shape)) * (1 if dt == U8 else 4)
        t = at(name, cursor[0], shape, dt)
        cursor[0] += (size + 31) // 32 * 32
        assert cursor[0] <= O_AT
        return t

    kc = const("kc", [K_COLS])
    lmask = const("lmask", [len(LEVELS), P], U8)
    vcol = const("vcol", [3, P])
    gqk = const("gqk", [3])
    sinks = const("sinks", [AH])
    bfor = const("bfor", [BH])
    wf_raw = const("wf_raw", [KT, BH])
    wf_hi = const("wf_hi", [KT, BH], F32R)
    wf_lo = const("wf_lo", [KT, BH], F32R)
    ss4 = const("ss4", [T, 4])
    rn = const("rn", [T])
    ssh = const("ssh", [T, 2 * BH])
    nmax = const("nmax", [8])
    m3 = const("m3", [12])
    mm = const("mm", [4])
    es = const("es", [8])
    den = const("den", [8])
    rden = const("rden", [8])
    cq = const("cq", [T, BH])
    logf = const("logf", [T, BH])
    tf = const("tf", [T, BH])
    ssk = const("ssk", [8])
    ident = kc[:, K_ID:K_ID + P]

    pa = at("pa", W_AT, [T, A_COLS])
    pb = at("pb", W_AT + 16384, [T, 4 * BW])
    pc = at("pc", W_AT + 40960, [T, 2 * CW])
    mk1 = at("mk1", W_AT + 49152, [T, 2 * CW])
    x_in = at("x_in", W_AT + 16384, [T, D])
    mem_in = [at("mem_in0", O_AT + 16 * TK, [D]), at("mem_in1", O_AT + 40 * TK, [D])]
    vrow = at("vrow", W_AT + 57344, [3, P])
    y1 = at("y1", W_AT, [T, D])
    sig = at("sig", W_AT + 65536, [T, NB])
    lmask_in = at("lmask_in", W_AT + 65536, [len(LEVELS), P])
    a_qn = at("a_qn", W_AT + 40960, [T, AKV, HD])
    a_qt = at("a_qt", W_AT + 43008, [2, S])
    a_kt = at("a_kt", W_AT + 45056, [2, S])
    a_s = at("a_s", W_AT + 47104, [AKV, 3, P])
    a_pt = at("a_pt", W_AT + 53248, [2, 3, P])
    a_o = at("a_o", W_AT + 56320, [T, AKV, HD])
    a_sq = at("a_sq", W_AT + 47104, [T, AW + AKW])
    a_kn = at("a_kn", W_AT + 55296, [T, AKW])
    b_sq = at("b_sq", W_AT + 57344, [2 * BW])
    nck = at("nck", O_AT, [BH, S])
    ct = at("ct", W_AT + 63488, [S])
    B_AT_ = O_AT + 24 * TK
    b_qn = at("b_qn", B_AT_, [T, AG, HD])
    b_kn = at("b_kn", B_AT_ + 1536, [T, AG, HD])
    b_qt = at("b_qt", B_AT_ + 3072, [2, S])
    b_kt = at("b_kt", B_AT_ + 5120, [2, S])
    b_s = at("b_s", B_AT_ + 7168, [AG, 3, P])
    b_pt = at("b_pt", B_AT_ + 11776, [2, 3, P])
    b_o = at("b_o", B_AT_ + 14848, [T, AG, HD])
    c_qn = at("c_qn", W_AT + 57344, [T, CD])
    c_kn = at("c_kn", W_AT + 58368, [T, CD])
    c_qt = at("c_qt", W_AT + 59392, [S])
    c_kt = at("c_kt", W_AT + 60416, [S])
    c_p = at("c_p", W_AT + 61440, [T, S])
    c_pt = at("c_pt", W_AT + 63488, [T, S])
    me_sq = at("me_sq", W_AT + 57344, [T, CW])
    x_again = at("x_again", X_AT, [T, D])
    mem2_in = at("mem2_in", W_AT + 49152, [T, D])
    x1 = at("x1", W_AT, [T, D])
    x1n = at("x1n", W_AT + 49152, [T, D])
    mk2 = at("mk2", O_AT + 8 * TK, [T, BR])
    mv2 = at("mv2", O_AT + 32 * TK, [T, BR])
    hg = at("hg", W_AT, [4, T, BR])
    cv = at("cv", W_AT + 32768, [3, T, BR])
    mq = at("mq", W_AT + 57344, [T, BR])
    u_st = at("u_st", W_AT + 65536, [T, 2, P])
    cb_st = at("cb_st", W_AT + 67584, [T, 2, P])
    v_tm = at("v_tm", O_AT + 16 * TK, [2, S])
    d_q = at("d_q", O_AT + 18 * TK, [T, MD])
    d_k = at("d_k", O_AT + 20 * TK, [T, MD])
    d_qt = at("d_qt", O_AT + 22 * TK, [2, S])
    d_kt = at("d_kt", O_AT + 40 * TK, [2, S])
    d_p = at("d_p", O_AT + 42 * TK, [T, S])
    d_pt = at("d_pt", O_AT + 44 * TK, [T, S])
    qt = at("qt", W_AT + 32768, [HH, S])
    zt = at("zt", W_AT + 40960, [HH, S])
    H_AT = W_AT + 49152
    h_a = at("h_a", H_AT, [S])
    h_l = at("h_l", H_AT + 1024, [S])
    h_pre = at("h_pre", H_AT + 2048, [S])
    h_suf = at("h_suf", H_AT + 3072, [S])
    h_k = at("h_k", H_AT + 4096, [S])
    h_e = at("h_e", H_AT + 5120, [S])
    h_g = at("h_g", H_AT + 6144, [S])
    h_sc = at("h_sc", H_AT + 8192, [T, P])
    h_off = at("h_off", H_AT + 9216, [P])
    h_o = at("h_o", H_AT + 9728, [T, HK])
    h_ls = at("h_ls", H_AT + 10752, [S])
    h_d = at("h_d", H_AT + 11776, [S])
    y2 = at("y2", W_AT, [T, D])
    mix = at("mix", W_AT, [T, D])
    x2 = at("x2", W_AT + 16384, [T, D])
    gpost = at("gpost", W_AT + 32768, [D])
    x2n = at("x2n", W_AT + 49152, [T, D])
    F_W = W_AT + 40960
    f_g = at("f_g", F_W, [T, NB])
    f_v = at("f_v", F_W + 4096, [T, NB])
    f_c = at("f_c", F_W + 8192, [4, S])
    f_a = at("f_a", F_W + 12288, [4, S])
    ff = at("ff", F_W, [T, D])
    x2b = at("x2b", X_AT, [T, D])
    gpost2 = at("gpost2", X_AT + KT * TK, [D])

    acc = [[ctx.enter_context(nc.psum_tensor(f"acc{p}{t}", [P, NB], F32)) for t in range(T)] for p in range(2)]
    tp = [ctx.enter_context(nc.psum_tensor(f"tp{n}", [P, NB], F32)) for n in range(2)]
    sc = [ctx.enter_context(nc.psum_tensor(f"sc{n}", [P, NB], F32)) for n in range(2)]

    nck_d = nc.dram_tensor("nck_d", [BH, S], F32).ap()
    x1_d = nc.dram_tensor("x1_d", [S, D], F32).ap()
    x2_d = nc.dram_tensor("x2_d", [S, D], F32).ap()

    loaded = [sem(f"chunk_loaded{n}") for n in range(RING)]
    hi_ready = sem("hi_ready")
    lo_ready = sem("lo_ready")
    chunk_done = sem("chunk_done")
    acc_free = [sem(f"acc_free{n}") for n in range(2)]
    phase_end = sem("phase_end")
    in_const, in_x, in_mem, in_wf = sem("in_const"), sem("in_x"), sem("in_mem"), sem("in_wf")
    in_mem2, in_x_again, out_x1, in_x1 = sem("in_mem2"), sem("in_x_again"), sem("out_x1"), sem("in_x1")
    out_x2, in_x2, out_nck, in_nck, out_y = (sem(n) for n in ("out_x2", "in_x2", "out_nck", "in_nck", "out_y"))

    BANKS = KT // 2

    def split_steps(banks):
        return dict(pe=[f"t{n}" for n in range(banks)], act=[f"h{n}" for n in range(banks)],
                    dve=[f"l{n}" for n in range(banks)])

    def norm_stage(name):
        s = split_steps(BANKS)
        return Stage(sem, name, pe=s["pe"], act=[f"sq{n}" for n in range(4 * T)] + ["rt"] + s["act"], dve=["ms", "e", "r", "n0", "n1"] + s["dve"])

    setup = Stage(sem, "setup", pe=["v"], act=["wh"], dve=["v", "qk0", "qk1", "wl"])
    norm_x, norm_m, norm_m2, norm_x1, norm_x2 = (
        norm_stage(n) for n in ("norm_x", "norm_m", "norm_m2", "norm_x1", "norm_x2"))
    win_prep = Stage(sem, "win_prep", pe=["k"], act=["sq", "rt", "silu", "k"], dve=["ms", "e", "r", "kn"])
    G4 = range(AKV)
    G3 = range(AG)
    win = Stage(
        sem, "win",
        pe=["q"] + [f"s{g}" for g in G4] + [f"{k}{g}" for g in G4 for k in ("pt", "o")],
        act=["q", "p"] + ["es"] + [f"pt{g}" for g in G4],
        dve=["qn"] + [f"s{g}" for g in G4] + ["m3", "mm", "n0", "n1", "neg", "es", "den", "rd", "on", "u"])
    ua_split = Stage(sem, "ua_split", **split_steps(3))
    fg_prep = Stage(
        sem, "fg_prep", pe=["f", "c", "ct"], act=["sq0", "sq1", "rt", "silu", "e", "l"],
        dve=["ms0", "ms1", "e", "r", "z", "a", "lf", "c", "ct"])
    fg = Stage(
        sem, "fg",
        pe=["q", "k"] + [f"s{g}" for g in G3] + [f"{k}{g}" for g in G3 for k in ("pt", "o")],
        act=["q", "k", "p"] + [f"pt{g}" for g in G3],
        dve=["qn", "kn"] + [f"s{g}" for g in G3] + ["mask", "m3", "mm", "n0", "neg", "rd", "on", "u"])
    ub_split = Stage(sem, "ub_split", **split_steps(3))
    me_prep = Stage(sem, "me_prep", act=["sq0", "sq1", "rt", "silu"], dve=["ms0", "ms1", "e", "r"])
    me = Stage(sem, "me", pe=["qk", "s", "pt", "o"], act=["q", "k", "p", "pt"], dve=["qn", "kn", "m", "rd", "on", "u"])
    uc_split = Stage(sem, "uc_split", **split_steps(2))
    y1_split = Stage(sem, "y1_split", **split_steps(BANKS))
    y2_split = Stage(sem, "y2_split", **split_steps(BANKS))
    sig_free = sem("sig_free")
    GATES = ("gate_a", "gate_b", "gate_c", "gate_conv", "gate_mem", "gate_hg")
    out1 = Stage(sem, "out1", dve=[f"x{n}" for n in range(4)])
    conv = Stage(sem, "conv", pe=["u", "b"], act=["cb", "h"], dve=["u", "c0", "c1", "c2", "y", "l"])
    ma = Stage(sem, "ma", pe=["q", "k", "s", "pt", "o"], act=["sq", "sk", "q", "k", "p", "pt"], dve=["m", "rd", "u"])
    ym_split = Stage(sem, "ym_split", **split_steps(4))
    hg_prep = Stage(sem, "hg_prep", pe=[f"t{n}" for n in range(8)], act=[f"t{n}" for n in range(8)] + ["silu"])
    LV = range(len(LEVELS))
    hr_dve = ["a", "ls", "d0", "d", "lf", "lf0", "kz", "k", "dg"]
    for n in range(len(LEVELS) + 1):
        hr_dve += [f"gl{n}", f"gr{n}"]
        if n < len(LEVELS):
            hr_dve += [f"suf{n}", f"pre{n}"]
        if n > 0:
            hr_dve += [f"mk{n - 1}"]
    hr = Stage(
        sem, "hr", pe=["d"] + [f"s{n}" for n in LV] + ["s7", "o"],
        act=["e1", "l1", "e2", "l2", "k"] + [f"e{k}{n}" for n in range(8) for k in "lr"] + ["off", "sq0", "sq1", "rt"],
        dve=hr_dve + ["e", "r", "on", "u"])
    yb_split = Stage(sem, "yb_split", **split_steps(4))
    mixs = Stage(sem, "mixs", act=[f"m{n}" for n in range(4)])
    post1 = Stage(sem, "post1", act=["rt"], dve=["ms", "e", "r", "g0", "g1", "x0", "x1"])
    ffs = Stage(sem, "ffs", pe=["g0", "g1", "v0", "v1"], act=["ev", "gelu", "h"],
                dve=[f"{k}" for c in range(4) for k in (f"c{c}", f"b{c}1", f"b{c}2")] + ["y", "l"])
    ffe = Stage(sem, "ffe", act=["m"])
    post2 = Stage(sem, "post2", act=["rt"], dve=["ms", "e", "r", "g0", "g1", "x0", "x1"])

    def w3(w):
        return w.rearrange("(k p) n -> p k n", p=P)

    wi, wi2 = w3(w_in[0]), w3(w_in_2[0])
    w_up, w_down = w3(w_ffn_up_2[0]), w3(w_ffn_down_2[0])
    w_o, w_o2, w_m, w_m2 = w3(w_out[0]), w3(w_out_2[0]), w3(w_mem_kv[0]), w3(w_mem_kv_2[0])
    w_br = {"a": w3(w_branch_a[0]), "b": w3(w_branch_b[0]), "c": w3(w_branch_c[0])}
    w_br2 = [w3(w_branch_2[0, n]) for n in range(3)]

    def weights(name, i, n):
        two = lambda w, col: [(w, col), (w, col + NB)]
        if name == "a_proj":
            return two(wi, i * 2 * NB)
        if name == "b_proj":
            return two(wi, i * 2 * NB + B_AT)
        if name == "c_proj":
            return two(wi, C_AT) + two(w_m, 0)
        if name in ("gate_a", "gate_b", "gate_c"):
            return [(wi, i * NB + (G_AT + "abc".index(name[-1]) * D)), (w_br[name[-1]], n * NB - NB)]
        if name in ("out", "out_2", "mem_kv_2"):
            w = {"out": w_o, "out_2": w_o2, "mem_kv_2": w_m2}[name]
            return two(w, 0) + two(w, 2 * NB)
        if name == "conv_proj":
            return two(wi2, i * 2 * NB)
        if name == "mq_proj":
            return two(wi2, MQ_AT)
        if name == "hg_proj":
            return two(wi2, i * 2 * NB + HQ_AT)
        if name in ("gate_conv", "gate_hg", "gate_mem"):
            g = ("gate_conv", "gate_hg", "gate_mem").index(name)
            return [(wi2, i * NB + (G2_AT + g * D)), (w_br2[g], n * NB - NB)]
        if name == "ffn_first":
            return [(w_up, 0), (w_up, FF)]
        if name == "ffn_up":
            return [(w_up, i * NB + NB), (w_up, i * NB + (FF + NB))]
        if name == "ffn_down":
            return two(w_down, i * 2 * NB)

    def positions(ph):
        per = {"ffn_down": len(ph.sizes) // 2}.get(ph.name, KT // 2)
        res, k, block = [], 0, 0
        for j, size in enumerate(ph.sizes):
            new = j > 0 and (j % per == 0 if not ph.name.startswith("gate") else j == KT // 2)
            if new:
                block, k = block + 1, 0
            res.append([block, k, size, False])
            k += size
        for j, r in enumerate(res):
            r[3] = j + 1 == len(res) or res[j + 1][0] != r[0]
        return res

    OUT_SLOTS = [*range(10, 24), 0, 1]
    OUT2_SLOTS = [*range(0, 8), *range(16, 24)]

    def stationary(name, block):
        own = lambda k: k
        if name in ("a_proj", "b_proj", "conv_proj", "mq_proj", "hg_proj", "ffn_first", "ffn_up"):
            return xh, xl, own
        if name == "c_proj":
            return (xh, xl, own) if block < 2 else (oh, ol, own)
        if name.startswith("gate"):
            if block == 0:
                return xh, xl, own
            first = {"gate_a": 16, "gate_b": 0, "gate_c": 6, "gate_conv": 0, "gate_mem": 16, "gate_hg": 8}[name]
            return oh, ol, lambda k: first + k
        if name == "out":
            return oh, ol, lambda k: OUT_SLOTS[k]
        if name == "out_2":
            return oh, ol, lambda k: OUT2_SLOTS[k]
        if name == "mem_kv_2":
            return m2h, m2l, own
        return fh, fl, own

    block_ctx = ctx.enter_context(nc.Block())

    def run(engine, name, body):
        ph = phases[name]
        if ph.times == 1:
            body(ph, 0)
        elif ph.c0 == 0:
            body(ph, 0)
            with engine.Fori(1, ph.times) as i:
                body(ph, i)
        else:
            with engine.Fori(0, ph.times) as i:
                body(ph, i)

    ENDS = ["norm_x", "a_proj", "b_proj", "c_proj", "gate_a", "gate_b", "gate_c", "out", "mem_kv_2", "conv_proj",
            "mq_proj", "hg_proj", "hg_prep", "gate_conv", "gate_mem", "gate_hg", "out_2", "ffn_up"]

    def ended(name):
        return phase_end, 3 * (ENDS.index(name) + 1)

    def end_phase(engine, name):
        engine.drain().then_inc(phase_end, 1)
        engine.wait_ge(*ended(name))

    @block_ctx.sync
    def _(sp):
        sp.dma_start(x_in[:], x[0].rearrange("(t p) d -> p t d", p=P)).then_inc(in_x, 16)
        sp.dma_start(kc[:], constants).then_inc(in_const, 16)

        def rows(dst, vec, n):
            sp.dma_start(dst, vec.rearrange("(r c) -> r c", c=P) if n > 1 else vec).then_inc(in_const, 16)

        for (g, r), vec in ((V_NORM, norm_gain), (V_MEM, mem_norm_gain), (V_MIX, norm_mix_pre_2),
                            (V_MEM2, norm_mem_2), (V_FFN, norm_ffn_pre_2)):
            rows(vrow[r:r + KT, g], vec[0], KT)
        for k in range(3):
            rows(vrow[V_CONV[1] + 8 * k:V_CONV[1] + 8 * k + 8, 0], conv_mix_w_2[0, k], 8)
            g, r = V_FW[k]
            rows(vrow[r:r + FT, g], conv_ffn_w_2[0, k], FT)
        rows(vrow[V_HG[1]:V_HG[1] + HH, 0], hg_norm_w_2[0], HH)
        rows(vrow[V_FB[1]:V_FB[1] + FT, 2], conv_ffn_b_2[0], FT)
        for k, vec in enumerate((q_gain_a, k_gain_a, q_gain_b, k_gain_b)):
            for half in range(2):
                sp.dma_start(vrow[V_QK + k:V_QK + k + 1, 1, half * HD:half * HD + HD], vec).then_inc(in_const, 16)
        for k, vec in enumerate((q_gain_c, k_gain_c)):
            sp.dma_start(vrow[V_QK + 4 + k:V_QK + 5 + k, 1, :], vec).then_inc(in_const, 16)
        sp.dma_start(sinks[:], sinks_a.partition_broadcast(P)).then_inc(in_const, 16)
        sp.dma_start(bfor[:], b_forget.partition_broadcast(P)).then_inc(in_const, 16)
        sp.dma_start(lmask_in[:], level_masks.rearrange("p (l c) -> p l c", c=P)).then_inc(in_const, 16)

        def load(ph, i, n=1):
            spec = weights(ph.name, i, n)
            for j, (blk, k, size, _) in enumerate(positions(ph)):
                c = ph.chunk(i, j)
                slot = (ph.c0 + j) % RING
                w, col = spec[blk]
                source = w[:, k:k + size, bass.ds(col, NB)]
                if not (isinstance(c, int) and c < RING):
                    sp.wait_ge(lo_ready, c - (RING - 1))
                sp.dma_start(raw[:, slot, 0:size], source).then_inc(loaded[slot], 16)

        ph = phases["a_proj"]
        load(ph, 0)
        with sp.Fori(1, ph.times) as i:
            load(ph, i)
        for name in list(phases)[1:]:
            ph = phases[name]
            if ph.times == 1:
                load(ph, 0)
            else:
                with sp.Fori(1, ph.times + 1) as n:
                    load(ph, n - 1, n)
        for t in range(T):
            sp.wait_ge(*post2.after("dve", f"x{t}"))
            sp.dma_start(out[0].rearrange("(t p) d -> p t d", p=P)[:, t], x2b[:, t]).then_inc(out_y, 16)
        sp.wait_ge(out_y, 16 * T)

    N_CONST = 1 + 5 + 3 * 2 + 2 + 8 + 2 + 3

    @block_ctx.gpsimd
    def _(pool):
        pool.dma_start(wf_raw[:], wi[:, :, F_AT:F_AT + BH]).then_inc(in_wf, 16)
        for t in range(T):
            pool.dma_start(mem_in[t][:], mem[0, t * P:(t + 1) * P]).then_inc(in_mem, 16)
        pool.wait_ge(*fg_prep.after("dve", "ct"))
        pool.dma_start(nck_d, ct[0:BH, :]).then_inc(out_nck, 16)
        pool.wait_ge(out_nck, 16)
        pool.wait_ge(*ended("c_proj"))
        pool.dma_start(nck[:], nck_d.partition_broadcast(P)).then_inc(in_nck, 16)
        pool.wait_ge(*ended("gate_b"))
        pool.dma_start(mem2_in[:], mem_2[0].rearrange("(t p) d -> p t d", p=P)).then_inc(in_mem2, 16)
        pool.wait_ge(*ended("gate_c"))
        pool.dma_start(x_again[:], x[0].rearrange("(t p) d -> p t d", p=P)).then_inc(in_x_again, 16)
        pool.wait_ge(*out1.after("dve", "x3"))
        pool.dma_start(x1_d.rearrange("(t p) d -> p t d", p=P), x1[:]).then_inc(out_x1, 16)
        pool.wait_ge(out_x1, 16)
        pool.wait_ge(*ended("gate_hg"))
        pool.dma_start(x2[:], x1_d.rearrange("(t p) d -> p t d", p=P)).then_inc(in_x1, 16)
        pool.dma_start(gpost[:], norm_mix_post_2[0].partition_broadcast(P)).then_inc(in_x1, 16)
        pool.wait_ge(*post1.after("dve", "x1"))
        pool.dma_start(x2_d.rearrange("(t p) d -> p t d", p=P), x2[:]).then_inc(out_x2, 16)
        pool.wait_ge(out_x2, 16)
        pool.wait_ge(*ended("ffn_up"))
        pool.dma_start(x2b[:], x2_d.rearrange("(t p) d -> p t d", p=P)).then_inc(in_x2, 16)
        pool.dma_start(gpost2[:], norm_ffn_post_2[0].partition_broadcast(P)).then_inc(in_x2, 16)

    @block_ctx.tensor
    def _(pe):
        def mm(o, lhsT, rhs, start=True, stop=True):
            return nc.tensor.matmul(o, lhsT, rhs, start=start, stop=stop)

        def tr(o, in_):
            k = in_.shape[0]
            return nc.tensor.transpose(o, in_, ident[0:k, :])

        def chunk(ph, i, j, pos):
            blk, k0, size, last = pos
            pair = blk % 2
            slot = (ph.c0 + j) % RING
            ah, al, place = stationary(ph.name, blk)
            if k0 == 0 and not (isinstance(i, int) and ph.use(i, blk) == 0):
                pe.wait_ge(acc_free[pair], 2 * ph.use(i, blk))
            pe.wait_ge(lo_ready, ph.chunk(i, j) + 1)
            for kk in range(size):
                ks = place(k0 + kk)
                for t in range(T):
                    tok = slice(t * P, (t + 1) * P)
                    o = acc[pair][t][:]
                    end = last and kk == size - 1
                    mm(o, al[:, ks, tok], hi[:, slot, kk], start=(k0 + kk == 0), stop=False)
                    mm(o, ah[:, ks, tok], hi[:, slot, kk], start=False, stop=False)
                    ins = mm(o, ah[:, ks, tok], lo[:, slot, kk], start=False, stop=end)
            ins.then_inc(chunk_done, 1)

        def stream(side):
            def body(ph, i):
                for j, pos in enumerate(positions(ph)):
                    chunk(ph, i, j, pos)
                    side(i, j)
            return body

        nothing = lambda i, j: None

        def split(st, src, ready, n, kts=None):
            bank = tp[n % 2]
            if n >= 2:
                pe.wait_ge(*st.after("dve", f"l{n - 2}"))
            if ready:
                pe.wait_ge(*ready)
            for kk in range(2):
                for t in range(T):
                    ins = tr(bank[:, kk * S + t * P:kk * S + (t + 1) * P], src(t, (2 * n + kk) * P))
            ins.then_inc(*st.mark("pe", f"t{n}"))

        def norm_split(st, src, n):
            split(st, src, st.after("dve", "n1"), n)

        pe.wait_ge(in_const, 16 * N_CONST)
        for g in range(3):
            ins = nc.tensor.transpose(sc[0][:, g * P:g * P + V_ROWS[g]], vrow[0:V_ROWS[g], g], ident[0:V_ROWS[g], 0:V_ROWS[g]])
        ins.then_inc(*setup.mark("pe", "v"))
        for n in range(BANKS):
            norm_split(norm_x, lambda t, c: x_in[:, t, c:c + P], n)
        end_phase(pe, "norm_x")
        pe.wait_ge(*norm_x.after("dve", f"l{BANKS - 1}"))

        run(pe, "a_proj", stream(nothing))
        end_phase(pe, "a_proj")

        pe.wait_ge(*win_prep.after("dve", "kn"))
        for t in range(T):
            for pair in range(2):
                ins = tr(tp[0][:, pair * S + t * P:pair * S + (t + 1) * P], a_kn[:, t, pair * P:(pair + 1) * P])
        ins.then_inc(*win_prep.mark("pe", "k"))
        pe.wait_ge(*win_prep.after("act", "k"))

        def window(i, j):
            if j == 0:
                pe.wait_ge(*win.after("dve", "qn", i))
                for t in range(T):
                    for pair in range(2):
                        ins = tr(tp[0][:, pair * S + t * P:pair * S + (t + 1) * P], a_qn[:, t, 2 * pair:2 * pair + 2, :].rearrange("p h d -> p (h d)"))
                ins.then_inc(*win.mark("pe", "q"))
            if j in (1, 2):
                for g in (2 * j - 2, 2 * j - 1):
                    pe.wait_ge(*win.after("act", "q", i))
                    if g >= 2:
                        pe.wait_ge(*win.after("dve", f"s{g - 2}", i))
                    half = slice(64 * (g % 2), 64 * (g % 2) + 64)
                    o = sc[g % 2]
                    mm(o[:, 0:P], a_qt[half, g // 2, 0:P], a_kt[half, g // 2, 0:P])
                    mm(o[:, P:3 * P], a_qt[half, g // 2, P:S], a_kt[half, g // 2, :]).then_inc(*win.mark("pe", f"s{g}"))
            if 7 <= j < 11:
                g = j - 7
                pe.wait_ge(*win.after("act", f"pt{g}", i))
                v = lambda t: pa[:, t, AW + AKW + g * HD:AW + AKW + (g + 1) * HD]
                mm(sc[0][:, g * HD:(g + 1) * HD], a_pt[:, g % 2, 0], v(0))
                o = sc[0][:, S + g * HD:S + (g + 1) * HD]
                mm(o, a_pt[:, g % 2, 1], v(0), stop=False)
                mm(o, a_pt[:, g % 2, 2], v(1), start=False).then_inc(*win.mark("pe", f"o{g}"))
            if 6 <= j < 10:
                g = j - 6
                pe.wait_ge(*win.after("act", "p", i))
                if g >= 2:
                    pe.wait_ge(*win.after("act", f"pt{g - 2}", i))
                for b in range(3):
                    ins = tr(tp[g % 2][:, b * P:(b + 1) * P], a_s[:, g, b])
                ins.then_inc(*win.mark("pe", f"pt{g}"))

        run(pe, "b_proj", stream(window))
        end_phase(pe, "b_proj")

        def c_side(i, j):
            if j == 0:
                pe.wait_ge(*setup.after("dve", "wl"))
                for t in range(T):
                    for k in range(KT):
                        tok = slice(t * P, (t + 1) * P)
                        o = sc[1][:, t * BH:(t + 1) * BH]
                        mm(o, xl[:, k, tok], wf_hi[:, k], start=(k == 0), stop=False)
                        mm(o, xh[:, k, tok], wf_hi[:, k], start=False, stop=False)
                        ins = mm(o, xh[:, k, tok], wf_lo[:, k], start=False, stop=(k == KT - 1))
                ins.then_inc(*fg_prep.mark("pe", "f"))
            if 4 <= j < 12:
                norm_split(norm_m, lambda t, c: mem_in[t][:, c:c + P], j - 4)
            if j == 13:
                pe.wait_ge(*fg_prep.after("dve", "lf"))
                tri, one = kc[:, K_TRI:K_TRI + P], kc[:, K_ONE:K_ONE + P]
                mm(sc[0][:, 0:BH], tri, logf[:, 0])
                mm(sc[0][:, BH:2 * BH], one, logf[:, 0], stop=False)
                mm(sc[0][:, BH:2 * BH], tri, logf[:, 1], start=False).then_inc(*fg_prep.mark("pe", "c"))
                pe.wait_ge(*norm_m.after("dve", f"l{BANKS - 1}"))
            if j == 15:
                pe.wait_ge(*fg_prep.after("dve", "c"))
                for t in range(T):
                    ins = tr(sc[1][0:BH, t * P:(t + 1) * P], cq[:, t])
                ins.then_inc(*fg_prep.mark("pe", "ct"))
            if 18 <= j < 21:
                split(ua_split, lambda t, c: pa[:, t, AW + 2 * AKW + c:AW + 2 * AKW + c + P], None, j - 18)

        run(pe, "c_proj", stream(c_side))
        end_phase(pe, "c_proj")

        def forget(i, j):
            pairs = ((0, P), (1, HD))
            if j == 0:
                for what, src, bank in (("q", b_qn, tp[0]), ("k", b_kn, tp[1])):
                    pe.wait_ge(*fg.after("dve", f"{what}n", i))
                    for n, w in pairs:
                        for t in range(T):
                            ins = tr(bank[0:w, n * S + t * P:n * S + (t + 1) * P], src[:, t].rearrange("p h d -> p (h d)")[:, n * P:n * P + w])
                    ins.then_inc(*fg.mark("pe", what))
            if j in (1, 2):
                for g in ((0, 1) if j == 1 else (2,)):
                    pe.wait_ge(*fg.after("act", "k", i))
                    if g >= 2:
                        pe.wait_ge(*fg.after("dve", f"s{g - 2}", i))
                    half = slice(64 * (g % 2), 64 * (g % 2) + 64)
                    o = sc[g % 2]
                    mm(o[:, 0:P], b_qt[half, g // 2, 0:P], b_kt[half, g // 2, 0:P])
                    mm(o[:, P:3 * P], b_qt[half, g // 2, P:S], b_kt[half, g // 2, :]).then_inc(*fg.mark("pe", f"s{g}"))
            if 7 <= j < 10:
                g = j - 7
                pe.wait_ge(*fg.after("act", f"pt{g}", i))
                v = lambda t: pb[:, t, bass.ds(i * AG * HD + (2 * BW + g * HD), HD)]
                mm(sc[0][:, g * HD:(g + 1) * HD], b_pt[:, g % 2, 0], v(0))
                o = sc[0][:, S + g * HD:S + (g + 1) * HD]
                mm(o, b_pt[:, g % 2, 1], v(0), stop=False)
                mm(o, b_pt[:, g % 2, 2], v(1), start=False).then_inc(*fg.mark("pe", f"o{g}"))
            if 6 <= j < 9:
                g = j - 6
                pe.wait_ge(*fg.after("act", "p", i))
                if g >= 2:
                    pe.wait_ge(*fg.after("act", f"pt{g - 2}", i))
                for b in range(3):
                    ins = tr(tp[g % 2][:, b * P:(b + 1) * P], b_s[:, g, b])
                ins.then_inc(*fg.mark("pe", f"pt{g}"))

        pe.wait_ge(*ua_split.after("dve", "l2"))
        run(pe, "gate_a", stream(forget))
        end_phase(pe, "gate_a")
        for n in range(3):
            split(ub_split, lambda t, c: pb[:, t, 3 * BW + c:3 * BW + c + P], None, n)
        pe.wait_ge(*ub_split.after("dve", "l2"))

        def memory(i, j):
            if j == 0:
                pe.wait_ge(*me.after("dve", "kn", i))
                for n, src in enumerate((c_qn, c_kn)):
                    for t in range(T):
                        ins = tr(tp[0][:, n * S + t * P:n * S + (t + 1) * P], src[:, t])
                ins.then_inc(*me.mark("pe", "qk"))
            if j == 2:
                pe.wait_ge(*me.after("act", "k", i))
                for t in range(T):
                    ins = mm(sc[0][:, t * S:(t + 1) * S], c_qt[:, t * P:(t + 1) * P], c_kt[:])
                ins.then_inc(*me.mark("pe", "s"))
            if j == 5:
                pe.wait_ge(*me.after("act", "p", i))
                for m in range(T):
                    for t in range(T):
                        ins = tr(tp[1][:, m * S + t * P:m * S + (t + 1) * P], c_p[:, t, m * P:(m + 1) * P])
                ins.then_inc(*me.mark("pe", "pt"))
            if j == 7:
                pe.wait_ge(*me.after("act", "pt", i))
                for t in range(T):
                    for m in range(T):
                        ins = mm(sc[1][:, t * CD:(t + 1) * CD], c_pt[:, m, t * P:(t + 1) * P],
                                 mk1[:, m, bass.ds(i * CD + CW, CD)], start=(m == 0), stop=(m == T - 1))
                ins.then_inc(*me.mark("pe", "o"))

        run(pe, "gate_b", stream(memory))
        end_phase(pe, "gate_b")
        for n in range(2):
            split(uc_split, lambda t, c: pc[:, t, CW + c:CW + c + P], None, n)
        pe.wait_ge(*uc_split.after("dve", "l1"))
        run(pe, "gate_c", stream(nothing))
        end_phase(pe, "gate_c")

        for n in range(BANKS):
            split(y1_split, lambda t, c: y1[:, t, c:c + P], None, n)
        pe.wait_ge(*y1_split.after("dve", f"l{BANKS - 1}"))

        def out_side(i, j):
            if 4 <= j < 12:
                norm_split(norm_m2, lambda t, c: mem2_in[:, t, c:c + P], j - 4)

        run(pe, "out", stream(out_side))
        end_phase(pe, "out")

        def mem2_side(i, j):
            if 6 <= j < 14:
                norm_split(norm_x1, lambda t, c: x1n[:, t, c:c + P], j - 6)

        run(pe, "mem_kv_2", stream(mem2_side))
        end_phase(pe, "mem_kv_2")
        run(pe, "conv_proj", stream(nothing))
        end_phase(pe, "conv_proj")
        run(pe, "mq_proj", stream(nothing))
        end_phase(pe, "mq_proj")

        def hg_side(i, j):
            if j == 0:
                pe.wait_ge(*conv.after("act", "cb", i))
                pe.wait_ge(*conv.after("dve", "u", i))
                for what, src, bank in (("u", u_st, tp[0]), ("b", cb_st, tp[1])):
                    for n in range(2):
                        for t in range(T):
                            ins = tr(bank[:, n * S + t * P:n * S + (t + 1) * P], src[:, t, n])
                    ins.then_inc(*conv.mark("pe", what))
            if j == 5:
                pe.wait_ge(*conv.after("dve", "y", i))
                for what, src, bank in (("q", d_q, tp[0]), ("k", d_k, tp[1])):
                    pe.wait_ge(*ma.after("act", f"s{what}", i))
                    for n in range(2):
                        for t in range(T):
                            ins = tr(bank[:, n * S + t * P:n * S + (t + 1) * P], src[:, t, n * P:(n + 1) * P])
                    ins.then_inc(*ma.mark("pe", what))
            if j == 7:
                pe.wait_ge(*ma.after("act", "k", i))
                for t in range(T):
                    for n in range(2):
                        ins = mm(sc[0][:, t * S:(t + 1) * S], d_qt[:, n, t * P:(t + 1) * P], d_kt[:, n],
                                 start=(n == 0), stop=(n == 1))
                ins.then_inc(*ma.mark("pe", "s"))
            if j == 10:
                pe.wait_ge(*ma.after("act", "p", i))
                for m in range(T):
                    for t in range(T):
                        ins = tr(tp[0][:, m * S + t * P:m * S + (t + 1) * P], d_p[:, t, m * P:(m + 1) * P])
                ins.then_inc(*ma.mark("pe", "pt"))
            if j == 12:
                pe.wait_ge(*ma.after("act", "pt", i))
                for t in range(T):
                    for m in range(T):
                        ins = mm(sc[1][:, t * MD:(t + 1) * MD], d_pt[:, m, t * P:(t + 1) * P],
                                 mv2[:, m, bass.ds(i * MD, MD)], start=(m == 0), stop=(m == T - 1))
                ins.then_inc(*ma.mark("pe", "o"))

        run(pe, "hg_proj", stream(hg_side))
        end_phase(pe, "hg_proj")
        for n in range(4):
            split(ym_split, lambda t, c: mq[:, t, c:c + P], None, n)
        pe.wait_ge(*ym_split.after("dve", "l3"))
        for n in range(8):
            if n >= 2:
                pe.wait_ge(*hg_prep.after("act", f"t{n - 2}"))
            for h in range(2):
                for t in range(T):
                    c = (2 * (n % 4) + h) * HK
                    ins = tr(sc[n % 2][:, h * S + t * P:h * S + (t + 1) * P], hg[:, n // 4, t, c:c + P])
            ins.then_inc(*hg_prep.mark("pe", f"t{n}"))
        end_phase(pe, "hg_prep")

        def recur(first):
            def side(i, j):
                it = i + first
                if j == 1:
                    pe.wait_ge(*hr.after("dve", "k", it))
                    for t in range(T):
                        ins = mm(sc[0][:, t * P:(t + 1) * P], h_k[:, t * P:(t + 1) * P],
                                 qt[:, bass.ds(it, 1), t * P:(t + 1) * P].rearrange("p a b -> p (a b)"))
                    ins.then_inc(*hr.mark("pe", "d"))
                if 2 <= j < 9:
                    n = j - 2
                    pe.wait_ge(*hr.after("dve", f"gr{n}", it))
                    if n >= 1:
                        pe.wait_ge(*hr.after("dve", "dg" if n == 1 else f"mk{n - 2}", it))
                    for t in range(T):
                        g = h_g[:, t * P:(t + 1) * P]
                        ins = mm(sc[(n + 1) % 2][:, t * P:(t + 1) * P], g, g)
                    ins.then_inc(*hr.mark("pe", f"s{n}"))
                if j == 9:
                    pe.wait_ge(*hr.after("dve", "gr7", it))
                    pe.wait_ge(*hr.after("dve", "mk5", it))
                    mm(sc[0][:, 0:P], h_g[:, 0:P], h_g[:, P:S]).then_inc(*hr.mark("pe", "s7"))
                if j == 10:
                    pe.wait_ge(*hr.after("act", "off", it))
                    pe.wait_ge(*hr.after("dve", "mk6", it))
                    v = lambda t: hg[:, 2, t, bass.ds(it * HK, HK)]
                    mm(sc[1][:, 0:HK], h_sc[:, 0], v(0))
                    mm(sc[1][:, HK:2 * HK], h_off[:], v(0), stop=False)
                    mm(sc[1][:, HK:2 * HK], h_sc[:, 1], v(1), start=False).then_inc(*hr.mark("pe", "o"))
            return side

        run(pe, "gate_conv", stream(recur(0)))
        end_phase(pe, "gate_conv")
        run(pe, "gate_mem", stream(recur(4)))
        end_phase(pe, "gate_mem")
        for n in range(4):
            split(yb_split, lambda t, c: hg[:, 3, t, c:c + P], None, n)
        pe.wait_ge(*yb_split.after("dve", "l3"))
        run(pe, "gate_hg", stream(nothing))
        end_phase(pe, "gate_hg")
        for n in range(BANKS):
            split(y2_split, lambda t, c: y2[:, t, c:c + P], None, n)
        pe.wait_ge(*y2_split.after("dve", f"l{BANKS - 1}"))
        run(pe, "out_2", stream(nothing))
        for n in range(BANKS):
            norm_split(norm_x2, lambda t, c: x2n[:, t, c:c + P], n)
        pe.wait_ge(*norm_x2.after("dve", f"l{BANKS - 1}"))
        end_phase(pe, "out_2")

        def ffn(i, at_, step):
            st, n = ("g", f_g) if step < 2 else ("v", f_v)
            h = step % 2
            pe.wait_ge(*ffs.after("act", "ev", i))
            if step >= 2:
                pe.wait_ge(*ffs.after("dve", f"b{2 * h + 1}2", i))
            for c in range(2):
                for t in range(T):
                    ins = tr(tp[h][:, c * S + t * P:c * S + (t + 1) * P], n[:, t, (2 * h + c) * P:(2 * h + c + 1) * P])
            ins.then_inc(*ffs.mark("pe", f"{st}{h}"))

        def ffn_side(i, j):
            if j in (0, 1):
                ffn(i, j, j)
            if j in (3, 4):
                ffn(i, j, j - 1)

        run(pe, "ffn_first", stream(nothing))
        run(pe, "ffn_up", stream(ffn_side))
        for step in range(4):
            ffn(FT // 4 - 1, 0, step)
        end_phase(pe, "ffn_up")
        run(pe, "ffn_down", stream(nothing))

    @block_ctx.scalar
    def _(act):
        def go(o, in_, func=ACT.Copy, **kw):
            return nc.scalar.activation(o, in_, func, **kw)

        def convert(c, slot, size, uses):
            act.wait_ge(loaded[slot], 16 * uses)
            if not (isinstance(c, int) and c < RING):
                act.wait_ge(chunk_done, c - (RING - 1))
            go(hi[:, slot, 0:size], raw[:, slot, 0:size]).then_inc(hi_ready, 1)

        def stream(side, skip_last=False):
            def body(ph, i):
                for j in range(ph.n):
                    c = ph.chunk(i, j + LEAD)
                    if not (skip_last and j + LEAD >= ph.n):
                        slot = (ph.c0 + j + LEAD) % RING
                        size = ph.sizes[j + LEAD] if j + LEAD < ph.n else 2
                        convert(c, slot, size, i * (ph.n // RING) + ((ph.c0 + j + LEAD) // RING + 1))
                    side(i, j)
            return body

        def evacuate(ph, i, blk, dst, then=None):
            j = max(k for k, p in enumerate(positions(ph)) if p[0] == blk)
            act.wait_ge(chunk_done, ph.chunk(i, j) + 1)
            for t in range(T):
                go(dst(t), acc[blk % 2][t][:]).then_inc(acc_free[blk % 2], 1)

        def ends(ph, j):
            p = positions(ph)[j]
            return p[0] if p[3] else None

        def split_hi(st, dst, n, gain=None):
            act.wait_ge(*st.after("pe", f"t{n}"))
            for kk in range(2):
                k = 2 * n + kk
                kw = dict(func=ACT.Identity, scale=vcol[:, gain[0], gain[1] + k:gain[1] + k + 1]) if gain else {}
                ins = go(dst(k), tp[n % 2][:, kk * S:(kk + 1) * S], **kw)
            ins.then_inc(*st.mark("act", f"h{n}"))

        def norm_stats(st, src, bank):
            for n in range(4 * T):
                t, q = divmod(n, 4)
                if n > 0:
                    act.wait_ge(*st.after("act", f"sq{n - 1}"))
                go(bank[:], src(t)[:, q * NB:(q + 1) * NB], ACT.Square, accum_out=ss4[:, t, q:q + 1]).then_inc(*st.mark("act", f"sq{n}"))
            act.wait_ge(*st.after("dve", "e"))
            go(rn[:], rn[:], ACT.Sqrt).then_inc(*st.mark("act", "rt"))

        def head_root(st, n):
            act.wait_ge(*st.after("dve", "e"))
            go(ssh[:, :, 0:n], ssh[:, :, 0:n], ACT.Sqrt).then_inc(*st.mark("act", "rt"))

        act.wait_ge(in_x, 16)
        norm_stats(norm_x, lambda t: x_in[:, t], sc[1])
        act.wait_ge(in_wf, 16)
        go(wf_hi[:], wf_raw[:]).then_inc(*setup.mark("act", "wh"))
        act.wait_ge(*setup.after("dve", "v"))
        for n in range(BANKS):
            split_hi(norm_x, lambda k: xh[:, k], n, V_NORM)
        for c in range(LEAD):
            convert(c, c, 2, 1)
        end_phase(act, "norm_x")

        def into(dst):
            def side(i, j):
                blk = ends(ph_of[0], j)
                if blk is not None:
                    evacuate(ph_of[0], i, blk, lambda t: dst(t, i, blk))
            return side

        ph_of = [None]

        def go_phase(name, side=None, dst=None, skip_last=False):
            ph_of[0] = phases[name]
            both = into(dst) if dst else (lambda i, j: None)

            def all_(i, j):
                both(i, j)
                if side:
                    side(i, j)

            run(act, name, stream(all_, skip_last))

        go_phase("a_proj", dst=lambda t, i, b: pa[:, t, bass.ds(i * 2 * NB + b * NB, NB)])
        end_phase(act, "a_proj")

        go(a_sq[:], pa[:, :, 0:AW + AKW], ACT.Square).then_inc(*win_prep.mark("act", "sq"))
        head_root(win_prep, AH + AKV)
        z = pa[:, :, AW + 2 * AKW:A_COLS]
        go(z, z, ACT.Silu).then_inc(*win_prep.mark("act", "silu"))
        act.wait_ge(*win_prep.after("pe", "k"))
        go(a_kt[:].rearrange("p a b -> p (a b)"), tp[0][:]).then_inc(*win_prep.mark("act", "k"))

        def window(i, j):
            if j == 0:
                act.wait_ge(*win.after("pe", "q", i))
                go(a_qt[:].rearrange("p a b -> p (a b)"), tp[0][:], ACT.Identity, scale=gqk[:, 0:1]).then_inc(*win.mark("act", "q"))
            if j == 4:
                act.wait_ge(*win.after("dve", "neg", i))
                for g in G4:
                    for t in range(T):
                        n = 2 * g + t
                        part = a_s[:, g, t:2 * t + 1].rearrange("p b k -> p (b k)")
                        ins = go(part, part, ACT.Exp, bias=nmax[:, n:n + 1], accum_out=den[:, n:n + 1])
                ins.then_inc(*win.mark("act", "p"))
                act.wait_ge(*win.after("dve", "es", i))
                go(es[:], es[:], ACT.Exp).then_inc(*win.mark("act", "es"))
            if 6 <= j < 10:
                g = j - 6
                act.wait_ge(*win.after("pe", f"pt{g}", i))
                if g >= 2:
                    act.wait_ge(*win.after("pe", f"o{g - 2}", i))
                go(a_pt[:, g % 2].rearrange("p b k -> p (b k)"), tp[g % 2][:, 0:3 * P]).then_inc(*win.mark("act", f"pt{g}"))

        go_phase("b_proj", window, lambda t, i, b: pb[:, t, bass.ds(i * 2 * NB + b * NB, NB)])
        end_phase(act, "b_proj")

        def c_dst(t, i, b):
            return (pc if b < 2 else mk1)[:, t, (b % 2) * NB:(b % 2 + 1) * NB]

        def c_side(i, j):
            if j == 0:
                act.wait_ge(in_mem, 32)
                norm_stats(norm_m, lambda t: mem_in[t][:], sc[0])
            if 4 <= j < 12:
                split_hi(norm_m, lambda k: oh[:, k], j - 4, V_MEM)
            if j == 2:
                for t in range(T):
                    if t:
                        act.wait_ge(*fg_prep.after("dve", f"ms{t - 1}"))
                    go(b_sq[:], pb[:, t, 0:2 * BW], ACT.Square).then_inc(*fg_prep.mark("act", f"sq{t}"))
                act.wait_ge(*fg_prep.after("dve", "e"))
                go(ssh[:], ssh[:], ACT.Sqrt).then_inc(*fg_prep.mark("act", "rt"))
            if j == 10:
                zz = pb[:, :, 3 * BW:4 * BW]
                go(zz, zz, ACT.Silu).then_inc(*fg_prep.mark("act", "silu"))
            if j == 12:
                act.wait_ge(*fg_prep.after("dve", "a"))
                go(tf[:], tf[:], ACT.Exp, scale=-1.0).then_inc(*fg_prep.mark("act", "e"))
                act.wait_ge(*fg_prep.after("act", "e"))
                go(tf[:], tf[:], ACT.Ln, bias=1.0).then_inc(*fg_prep.mark("act", "l"))
            if 18 <= j < 21:
                split_hi(ua_split, lambda k: oh[:, 16 + k], j - 18)

        go_phase("c_proj", c_side, c_dst)
        end_phase(act, "c_proj")

        def gate_side(name, more=None):
            gates_before = GATES.index(name) * (D // NB)

            def side(i, j):
                ph = ph_of[0]
                if j == KT // 2 - 1:
                    act.wait_ge(chunk_done, ph.chunk(i, j) + 1)
                    act.wait_ge(sig_free, i * T + (1 + T * gates_before))
                    for t in range(T):
                        go(sig[:, t], acc[0][t][:], ACT.Sigmoid).then_inc(acc_free[0], 1)
                if more:
                    more(i, j)
            return side

        def forget(i, j):
            if j == 0:
                for what, dst, bank in (("q", b_qt, tp[0]), ("k", b_kt, tp[1])):
                    act.wait_ge(*fg.after("pe", what, i))
                    kw = lambda w: dict(func=ACT.Identity, scale=gqk[0:w, 1:2]) if what == "q" else {}
                    go(dst[:, 0], bank[:, 0:S], **kw(P))
                    go(dst[0:HD, 1], bank[0:HD, S:2 * S], **kw(HD)).then_inc(*fg.mark("act", what))
            if j == 4:
                act.wait_ge(*fg.after("dve", "neg", i))
                for g in G3:
                    for t in range(T):
                        n = 2 * g + t
                        part = b_s[:, g, t:2 * t + 1].rearrange("p b k -> p (b k)")
                        ins = go(part, part, ACT.Exp, bias=nmax[:, n:n + 1], accum_out=den[:, n:n + 1])
                ins.then_inc(*fg.mark("act", "p"))
            if 6 <= j < 9:
                g = j - 6
                act.wait_ge(*fg.after("pe", f"pt{g}", i))
                if g >= 2:
                    act.wait_ge(*fg.after("pe", f"o{g - 2}", i))
                go(b_pt[:, g % 2].rearrange("p b k -> p (b k)"), tp[g % 2][:, 0:3 * P]).then_inc(*fg.mark("act", f"pt{g}"))

        go_phase("gate_a", gate_side("gate_a", forget))
        end_phase(act, "gate_a")
        for n in range(3):
            split_hi(ub_split, lambda k: oh[:, k], n)
        for n, src in enumerate((pc, mk1)):
            if n:
                act.wait_ge(*me_prep.after("dve", "ms0"))
            go(me_sq[:], src[:, :, 0:CW], ACT.Square).then_inc(*me_prep.mark("act", f"sq{n}"))
        head_root(me_prep, 2 * CH)
        z3 = pc[:, :, CW:2 * CW]
        go(z3, z3, ACT.Silu).then_inc(*me_prep.mark("act", "silu"))

        def memory(i, j):
            if j == 0:
                act.wait_ge(*me.after("pe", "qk", i))
                go(c_qt[:], tp[0][:, 0:S], ACT.Identity, scale=gqk[:, 2:3]).then_inc(*me.mark("act", "q"))
                go(c_kt[:], tp[0][:, S:2 * S]).then_inc(*me.mark("act", "k"))
            if j == 3:
                act.wait_ge(*me.after("dve", "m", i))
                for t in range(T):
                    ins = go(c_p[:, t], sc[0][:, t * S:(t + 1) * S], ACT.Exp, bias=nmax[:, t:t + 1], accum_out=den[:, t:t + 1])
                ins.then_inc(*me.mark("act", "p"))
            if j == 5:
                act.wait_ge(*me.after("pe", "pt", i))
                go(c_pt[:].rearrange("p a b -> p (a b)"), tp[1][:]).then_inc(*me.mark("act", "pt"))

        go_phase("gate_b", gate_side("gate_b", memory))
        end_phase(act, "gate_b")
        for n in range(2):
            split_hi(uc_split, lambda k: oh[:, 6 + k], n)
        go_phase("gate_c", gate_side("gate_c"))
        end_phase(act, "gate_c")
        for n in range(BANKS):
            split_hi(y1_split, lambda k: oh[:, OUT_SLOTS[k]], n)

        def out_side(i, j):
            if j == 0:
                act.wait_ge(in_mem2, 16)
                norm_stats(norm_m2, lambda t: mem2_in[:, t], sc[0])
            if 4 <= j < 12:
                split_hi(norm_m2, lambda k: m2h[:, k], j - 4, V_MEM2)

        go_phase("out", out_side)
        end_phase(act, "out")

        def mem2_side(i, j):
            if j == 0:
                norm_stats(norm_x1, lambda t: x1[:, t], sc[0])
            if 6 <= j < 14:
                split_hi(norm_x1, lambda k: xh[:, k], j - 6, V_MIX)

        go_phase("mem_kv_2", mem2_side, lambda t, i, b: (mk2 if b < 2 else mv2)[:, t, (b % 2) * NB:(b % 2 + 1) * NB])
        end_phase(act, "mem_kv_2")
        go_phase("conv_proj", dst=lambda t, i, b: cv[:, i, t, b * NB:(b + 1) * NB])
        end_phase(act, "conv_proj")
        go_phase("mq_proj", dst=lambda t, i, b: mq[:, t, b * NB:(b + 1) * NB])
        end_phase(act, "mq_proj")

        def hg_side(i, j):
            if j == 0:
                go(cb_st[:], cv[:, 0, :, bass.ds(i * 2 * P, 2 * P)]).then_inc(*conv.mark("act", "cb"))
            if j == 4:
                act.wait_ge(*conv.after("dve", "y", i))
                for n in range(2):
                    ins = go(oh[:, bass.ds(i * 2 + n, 1)].rearrange("p a b -> p (a b)"), v_tm[:, n])
                ins.then_inc(*conv.mark("act", "h"))
                go(d_q[:], mq[:, :, bass.ds(i * MD, MD)], ACT.Copy, scale=MD ** -0.5).then_inc(*ma.mark("act", "sq"))
                go(d_k[:], mk2[:, :, bass.ds(i * MD, MD)]).then_inc(*ma.mark("act", "sk"))
            if j == 5:
                for what, dst, bank in (("q", d_qt, tp[0]), ("k", d_kt, tp[1])):
                    act.wait_ge(*ma.after("pe", what, i))
                    go(dst[:].rearrange("p a b -> p (a b)"), bank[:]).then_inc(*ma.mark("act", what))
            if j == 8:
                act.wait_ge(*ma.after("dve", "m", i))
                for t in range(T):
                    ins = go(d_p[:, t], sc[0][:, t * S:(t + 1) * S], ACT.Exp, bias=nmax[:, t:t + 1], accum_out=den[:, t:t + 1])
                ins.then_inc(*ma.mark("act", "p"))
            if j == 10:
                act.wait_ge(*ma.after("pe", "pt", i))
                go(d_pt[:].rearrange("p a b -> p (a b)"), tp[0][:]).then_inc(*ma.mark("act", "pt"))

        act.wait_ge(out_x1, 16)
        go_phase("hg_proj", hg_side, lambda t, i, b: hg[:, i, t, b * NB:(b + 1) * NB])
        end_phase(act, "hg_proj")
        for n in range(4):
            split_hi(ym_split, lambda k: oh[:, 16 + k], n)
        for n in range(8):
            act.wait_ge(*hg_prep.after("pe", f"t{n}"))
            dst = (qt if n < 4 else zt)[:, 2 * (n % 4):2 * (n % 4) + 2].rearrange("p a b -> p (a b)")
            go(dst, sc[n % 2][:], ACT.Silu if n < 4 else ACT.Copy).then_inc(*hg_prep.mark("act", f"t{n}"))
        go(hg[:, 3], hg[:, 3], ACT.Silu).then_inc(*hg_prep.mark("act", "silu"))
        end_phase(act, "hg_prep")

        def halves(tensor, s):
            v = tensor.rearrange("p (n two s) -> p n two s", two=2, s=s)
            return v[:, :, 0], v[:, :, 1]

        def recur(first):
            def side(i, j):
                it = i + first
                if j == 0:
                    act.wait_ge(*hr.after("dve", "a", it))
                    go(h_l[:], h_a[:], ACT.Exp, scale=-1.0).then_inc(*hr.mark("act", "e1"))
                    act.wait_ge(*hr.after("act", "e1", it))
                    go(h_l[:], h_l[:], ACT.Ln, bias=1.0).then_inc(*hr.mark("act", "l1"))
                    act.wait_ge(*hr.after("dve", "d", it))
                    go(h_d[:], h_d[:], ACT.Exp, scale=-1.0).then_inc(*hr.mark("act", "e2"))
                    act.wait_ge(*hr.after("act", "e2", it))
                    go(h_d[:], h_d[:], ACT.Ln, bias=1.0).then_inc(*hr.mark("act", "l2"))
                    act.wait_ge(*hr.after("dve", "kz", it))
                    go(h_k[:], h_k[:], ACT.Exp).then_inc(*hr.mark("act", "k"))
                if 1 <= j < 9:
                    n = j - 1
                    s = (LEVELS + [P])[n]
                    e, pre, suf = halves(h_e[:], s), halves(h_pre[:], s), halves(h_suf[:], s)
                    if n == 0:
                        act.wait_ge(*hr.after("dve", "lf0", it))
                    else:
                        act.wait_ge(*hr.after("dve", f"pre{n - 1}", it))
                    go(e[0], suf[0], ACT.Exp).then_inc(*hr.mark("act", f"el{n}"))
                    go(e[1], pre[1], ACT.Exp).then_inc(*hr.mark("act", f"er{n}"))
                if j == 9:
                    act.wait_ge(*hr.after("pe", "s7", it))
                    go(h_off[:], sc[0][:, 0:P]).then_inc(*hr.mark("act", "off"))
                if j == 10:
                    act.wait_ge(*hr.after("pe", "o", it))
                    for t in range(T):
                        go(h_e[:, 0:HK], sc[1][:, t * HK:(t + 1) * HK], ACT.Square, accum_out=ssk[:, t:t + 1]).then_inc(*hr.mark("act", f"sq{t}"))
                        act.wait_ge(*hr.after("act", f"sq{t}", it))
                    act.wait_ge(*hr.after("dve", "e", it))
                    go(ssk[:, 0:T], ssk[:, 0:T], ACT.Sqrt).then_inc(*hr.mark("act", "rt"))
            return side

        go_phase("gate_conv", gate_side("gate_conv", recur(0)))
        end_phase(act, "gate_conv")
        go_phase("gate_mem", gate_side("gate_mem", recur(4)))
        end_phase(act, "gate_mem")
        for n in range(4):
            split_hi(yb_split, lambda k: oh[:, 8 + k], n, V_HG)
        go_phase("gate_hg", gate_side("gate_hg"))
        end_phase(act, "gate_hg")
        for n in range(BANKS):
            split_hi(y2_split, lambda k: oh[:, OUT2_SLOTS[k]], n)

        def keep(st, dst, k):
            def side(i, j):
                ph = ph_of[0]
                blk = ends(ph, j)
                if blk is None:
                    return
                act.wait_ge(chunk_done, ph.chunk(i, j) + 1)
                if i or blk:
                    last = (i, blk - 1) if blk else (i - 1, ph.blocks - 1)
                    act.wait_ge(acc_free[last[1] % 2], 2 * ph.use(*last) + T)
                for t in range(T):
                    col = i * 2 + blk
                    go(dst[:, t, bass.ds(col * NB, NB)], acc[blk % 2][t][:])
                    if t:
                        act.wait_ge(acc_free[blk % 2], 2 * ph.use(i, blk) + t)
                    go(sc[0][:], acc[blk % 2][t][:], ACT.Square, accum_out=ss4[:, t, bass.ds(col, 1)]).then_inc(acc_free[blk % 2], 1)
                k(i, blk)
            return side

        go_phase("out_2", keep(mixs, mix, lambda i, b: act.drain().then_inc(*mixs.mark("act", f"m{b}"))))
        act.wait_ge(*post1.after("dve", "e"))
        go(rn[:], rn[:], ACT.Sqrt).then_inc(*post1.mark("act", "rt"))
        act.wait_ge(*post1.after("dve", "x1"))
        norm_stats(norm_x2, lambda t: x2[:, t], sc[0])
        for n in range(BANKS):
            split_hi(norm_x2, lambda k: xh[:, k], n, V_FFN)
        end_phase(act, "out_2")

        def ffn_ev(i, blk, ph):
            act.wait_ge(chunk_done, ph.chunk(i, KT // 2 * (blk + 1) - 1) + 1)
            for t in range(T):
                go((f_g, f_v)[blk][:, t], acc[blk][t][:]).then_inc(acc_free[blk], 1)

        def ffn_up(first, ph):
            def side(i, j):
                it = i + first
                if first and j == 2:
                    ffn_act(i)
                if first and j == 6:
                    ffn_hi(i)
                if j == 7:
                    ffn_ev(i, 0, ph)
                if j == 15:
                    ffn_ev(i, 1, ph)
                    act.drain().then_inc(*ffs.mark("act", "ev"))
            return side

        def ffn_act(i):
            act.wait_ge(*ffs.after("dve", "b32", i))
            for c in range(4):
                ins = go(f_a[:, c], f_c[:, c], ACT.Gelu_apprx_tanh, bias=vcol[:, V_FB[0], bass.ds(i * 4 + (V_FB[1] + c), 1)])
            ins.then_inc(*ffs.mark("act", "gelu"))

        def ffn_hi(i):
            act.wait_ge(*ffs.after("dve", "y", i))
            go(fh[:, bass.ds(i * 4, 4)], f_a[:]).then_inc(*ffs.mark("act", "h"))

        run(act, "ffn_first", stream(ffn_up(0, phases["ffn_first"])))
        act.wait_ge(out_x2, 16)
        run(act, "ffn_up", stream(ffn_up(1, phases["ffn_up"])))
        ffn_act(FT // 4 - 1)
        ffn_hi(FT // 4 - 1)
        end_phase(act, "ffn_up")
        ph_of[0] = ph = phases["ffn_down"]
        k = keep(ffe, ff, lambda i, b: None)
        stream(k)(ph, 0)
        stream(k, skip_last=True)(ph, 1)
        act.drain().then_inc(*ffe.mark("act", "m"))
        act.wait_ge(*post2.after("dve", "e"))
        go(rn[:], rn[:], ACT.Sqrt).then_inc(*post2.mark("act", "rt"))

    @block_ctx.vector
    def _(dve):
        v = nc.vector

        def convert(c, slot, size):
            dve.wait_ge(hi_ready, c + 1)
            v.tensor_tensor(lo[:, slot, 0:size], raw[:, slot, 0:size], hi[:, slot, 0:size].bitcast(F32),
                            ALU.subtract).then_inc(lo_ready, 1)

        def stream(side, skip_last=False):
            def body(ph, i):
                for j in range(ph.n):
                    if not (skip_last and j + LEAD >= ph.n):
                        size = ph.sizes[j + LEAD] if j + LEAD < ph.n else 2
                        convert(ph.chunk(i, j + LEAD), (ph.c0 + j + LEAD) % RING, size)
                    side(i, j)
            return body

        nothing = lambda i, j: None

        def split_lo(st, dst, hi_of, n, gain=None):
            dve.wait_ge(*st.after("act", f"h{n}"))
            for kk in range(2):
                k = 2 * n + kk
                src, h = tp[n % 2][:, kk * S:(kk + 1) * S], hi_of(k).bitcast(F32)
                if gain:
                    g = vcol[:, gain[0], gain[1] + k:gain[1] + k + 1]
                    ins = v.scalar_tensor_tensor(dst(k), src, g, h, ALU.mult, ALU.subtract)
                else:
                    ins = v.tensor_tensor(dst(k), src, h, ALU.subtract)
            ins.then_inc(*st.mark("dve", f"l{n}"))

        def root_mean(st, part, n, mean):
            v.tensor_scalar(part, part, 1.0 / mean, EPS, ALU.mult, ALU.add).then_inc(*st.mark("dve", "e"))
            dve.wait_ge(*st.after("act", "rt"))
            v.reciprocal(part, part).then_inc(*st.mark("dve", "r"))

        def norm_rest(st, src, dst):
            dve.wait_ge(*st.after("act", f"sq{4 * T - 1}"))
            v.tensor_reduce(rn[:], ss4[:], AX, ALU.add).then_inc(*st.mark("dve", "ms"))
            dve.wait_ge(*st.after("dve", "ms"))
            root_mean(st, rn[:], T, D)
            dve.wait_ge(*st.after("dve", "r"))
            for t in range(T):
                v.tensor_scalar(dst(t), src(t), rn[:, t:t + 1], None, ALU.mult).then_inc(*st.mark("dve", f"n{t}"))

        def over(ap, shape):
            return ap.unsqueeze(len(ap.shape)).to_broadcast(shape)

        norm_rest(norm_x, lambda t: x_in[:, t], lambda t: x_in[:, t])
        dve.wait_ge(*setup.after("pe", "v"))
        for g in range(3):
            ins = v.tensor_copy(vcol[:, g, 0:V_ROWS[g]], sc[0][:, g * P:g * P + V_ROWS[g]])
        ins.then_inc(*setup.mark("dve", "v"))
        dve.wait_ge(*setup.after("dve", "v"))
        v.tensor_tensor(gqk[:], vcol[:, 1, V_QK:V_QK + 6:2], vcol[:, 1, V_QK + 1:V_QK + 6:2], ALU.mult).then_inc(*setup.mark("dve", "qk0"))
        dve.wait_ge(*setup.after("dve", "qk0"))
        v.tensor_scalar(gqk[:, 0:2], gqk[:, 0:2], HD ** -0.5, None, ALU.mult)
        v.tensor_scalar(gqk[:, 2:3], gqk[:, 2:3], CD ** -0.5, None, ALU.mult).then_inc(*setup.mark("dve", "qk1"))
        dve.wait_ge(*setup.after("act", "wh"))
        v.tensor_tensor(wf_lo[:], wf_raw[:], wf_hi[:].bitcast(F32), ALU.subtract).then_inc(*setup.mark("dve", "wl"))
        dve.wait_ge(in_const, 16 * N_CONST)
        v.tensor_copy(lmask[:], lmask_in[:]).then_inc(sig_free, 1)
        for n in range(BANKS):
            split_lo(norm_x, lambda k: xl[:, k], lambda k: xh[:, k], n, V_NORM)
        for c in range(LEAD):
            convert(c, c, 2)
        end_phase(dve, "norm_x")
        run(dve, "a_proj", stream(nothing))
        end_phase(dve, "a_proj")

        dve.wait_ge(*win_prep.after("act", "sq"))
        heads = ssh[:, :, 0:AH + AKV]
        v.tensor_reduce(heads, a_sq[:].rearrange("p t (h d) -> p t h d", d=HD), AX, ALU.add).then_inc(*win_prep.mark("dve", "ms"))
        dve.wait_ge(*win_prep.after("dve", "ms"))
        root_mean(win_prep, heads, AH + AKV, HD)
        dve.wait_ge(*win_prep.after("dve", "r"))
        v.tensor_tensor(a_kn[:].rearrange("p t (h d) -> p t h d", d=HD),
                        pa[:, :, AW:AW + AKW].rearrange("p t (h d) -> p t h d", d=HD),
                        over(ssh[:, :, AH:AH + AKV], [P, T, AKV, HD]), ALU.mult).then_inc(*win_prep.mark("dve", "kn"))

        def window(i, j):
            by_g = lambda ap, n: ap.rearrange("p t (g n d) -> p t g n d", n=AG, d=n)[:, :, :, i, :]
            if j == 0:
                r = ssh[:, :, 0:AH].rearrange("p t (g n) -> p t g n", n=AG)[:, :, :, i]
                v.tensor_tensor(a_qn[:], by_g(pa[:, :, 0:AW], HD), over(r, [P, T, AKV, HD]), ALU.mult).then_inc(*win.mark("dve", "qn"))
            if j in (1, 2):
                for g in (2 * j - 2, 2 * j - 1):
                    dve.wait_ge(*win.after("pe", f"s{g}", i))
                    v.scalar_tensor_tensor(a_s[:, g].rearrange("p b k -> p (b k)"), kc[:, K_REL:K_REL + 3 * P],
                                           kc[:, bass.ds(i + (K_SLOPE + AG * g), 1)], sc[g % 2][:, 0:3 * P],
                                           ALU.mult, ALU.add).then_inc(*win.mark("dve", f"s{g}"))
            if j == 3:
                dve.wait_ge(*win.after("dve", "s3", i))
                v.tensor_reduce(m3[:], a_s[:].rearrange("p g b k -> p (g b) k"), AX, ALU.max).then_inc(*win.mark("dve", "m3"))
                dve.wait_ge(*win.after("dve", "m3", i))
                v.tensor_tensor(mm[:], m3[:, 1:12:3], m3[:, 2:12:3], ALU.max).then_inc(*win.mark("dve", "mm"))
                sink = sinks[:].rearrange("p (g n) -> p g n", n=AG)[:, :, i]
                v.tensor_tensor(nmax[:, 0:8:2], m3[:, 0:12:3], sink, ALU.max).then_inc(*win.mark("dve", "n0"))
                dve.wait_ge(*win.after("dve", "mm", i))
                v.tensor_tensor(nmax[:, 1:8:2], mm[:], sink, ALU.max).then_inc(*win.mark("dve", "n1"))
                dve.wait_ge(*win.after("dve", "n1", i))
                v.tensor_scalar(nmax[:], nmax[:], -1.0, None, ALU.mult).then_inc(*win.mark("dve", "neg"))
                dve.wait_ge(*win.after("dve", "neg", i))
                v.tensor_tensor(es[:].rearrange("p (g t) -> p g t", t=T), nmax[:].rearrange("p (g t) -> p g t", t=T),
                                over(sink, [P, AKV, T]), ALU.add).then_inc(*win.mark("dve", "es"))
            if j == 4:
                dve.wait_ge(*win.after("act", "es", i))
                v.tensor_tensor(den[:], den[:], es[:], ALU.add).then_inc(*win.mark("dve", "den"))
                dve.wait_ge(*win.after("dve", "den", i))
                v.reciprocal(rden[:], den[:]).then_inc(*win.mark("dve", "rd"))
            if j == 11:
                dve.wait_ge(*win.after("pe", "o3", i))
                r = rden[:].rearrange("p (g t) -> p t g", t=T)
                v.tensor_tensor(a_o[:], sc[0][:].rearrange("p (t g d) -> p t g d", t=T, g=AKV), over(r, [P, T, AKV, HD]),
                                ALU.mult).then_inc(*win.mark("dve", "on"))
                dve.wait_ge(*win.after("dve", "on", i))
                z = by_g(pa[:, :, AW + 2 * AKW:A_COLS], HD)
                v.tensor_tensor(z, a_o[:], z, ALU.mult).then_inc(*win.mark("dve", "u"))

        run(dve, "b_proj", stream(window))
        end_phase(dve, "b_proj")

        def c_side(i, j):
            if j == 0:
                norm_rest(norm_m, lambda t: mem_in[t][:], lambda t: mem_in[t][:])
            if 4 <= j < 12:
                split_lo(norm_m, lambda k: ol[:, k], lambda k: oh[:, k], j - 4, V_MEM)
            if j == 2:
                for t in range(T):
                    dve.wait_ge(*fg_prep.after("act", f"sq{t}"))
                    v.tensor_reduce(ssh[:, t], b_sq[:].rearrange("p (h d) -> p h d", d=HD), AX, ALU.add).then_inc(*fg_prep.mark("dve", f"ms{t}"))
                dve.wait_ge(*fg_prep.after("dve", "ms1"))
                root_mean(fg_prep, ssh[:], 2 * BH, HD)
                dve.wait_ge(*fg_prep.after("pe", "f"))
                v.tensor_tensor(logf[:], sc[1][:, 0:T * BH].rearrange("p (t h) -> p t h", t=T),
                                bfor[:].unsqueeze(1).to_broadcast([P, T, BH]), ALU.add).then_inc(*fg_prep.mark("dve", "z"))
                dve.wait_ge(*fg_prep.after("dve", "z"))
                v.scalar_tensor_tensor(tf[:], logf[:], -1.0, logf[:], ALU.mult, ALU.max).then_inc(*fg_prep.mark("dve", "a"))
            if j == 12:
                dve.wait_ge(*fg_prep.after("act", "l"))
                v.scalar_tensor_tensor(logf[:], logf[:], 0.0, tf[:], ALU.min, ALU.subtract).then_inc(*fg_prep.mark("dve", "lf"))
            if j == 14:
                dve.wait_ge(*fg_prep.after("pe", "c"))
                v.tensor_copy(cq[:].rearrange("p t h -> p (t h)"), sc[0][:, 0:T * BH]).then_inc(*fg_prep.mark("dve", "c"))
            if j == 16:
                dve.wait_ge(*fg_prep.after("pe", "ct"))
                v.tensor_scalar(ct[0:BH], sc[1][0:BH, 0:S], -1.0, None, ALU.mult).then_inc(*fg_prep.mark("dve", "ct"))
            if 18 <= j < 21:
                split_lo(ua_split, lambda k: ol[:, 16 + k], lambda k: oh[:, 16 + k], j - 18)

        run(dve, "c_proj", stream(c_side))
        end_phase(dve, "c_proj")

        def gate_side(ph, y, first, more=None):
            def side(i, j):
                if more:
                    more(i, j)
                if j != ph.n - 1:
                    return
                dve.wait_ge(acc_free[0], 2 * ph.use(i, 0) + T)
                dve.wait_ge(chunk_done, ph.chunk(i, j) + 1)
                for t in range(T):
                    v.tensor_tensor(sig[:, t], sig[:, t], acc[1][t][:], ALU.mult).then_inc(acc_free[1], 1)
                for t in range(T):
                    dve.wait_ge(acc_free[1], 2 * ph.use(i, 1) + t + 1)
                    col = y[:, t, bass.ds(i * NB, NB)]
                    if first:
                        v.tensor_copy(col, sig[:, t]).then_inc(sig_free, 1)
                    else:
                        v.tensor_tensor(col, col, sig[:, t], ALU.add).then_inc(sig_free, 1)
            return side

        def forget(i, j):
            if j == 0:
                for what, dst, col, h0 in (("qn", b_qn, 0, 0), ("kn", b_kn, BW, BH)):
                    src = pb[:, :, bass.ds(i * AG * HD + col, AG * HD)].rearrange("p t (h d) -> p t h d", d=HD)
                    v.tensor_tensor(dst[:], src, over(ssh[:, :, bass.ds(i * AG + h0, AG)], [P, T, AG, HD]), ALU.mult).then_inc(*fg.mark("dve", what))
            if j in (1, 2):
                dve.wait_ge(in_nck, 16)
                for g in ((0, 1) if j == 1 else (2,)):
                    dve.wait_ge(*fg.after("pe", f"s{g}", i))
                    h = bass.ds(i * AG + g, 1)
                    flat = lambda ap: ap.rearrange("p a b -> p (a b)")
                    v.scalar_tensor_tensor(b_s[:, g, 0], sc[g % 2][:, 0:P], cq[:, 0, h], flat(nck[:, h, 0:P]), ALU.add, ALU.add)
                    v.scalar_tensor_tensor(flat(b_s[:, g, 1:3]), sc[g % 2][:, P:3 * P], cq[:, 1, h], flat(nck[:, h, :]),
                                           ALU.add, ALU.add).then_inc(*fg.mark("dve", f"s{g}"))
            if j == 3:
                dve.wait_ge(*fg.after("dve", "s2", i))
                own = b_s[:, :, 0:3:2, :]
                mask = kc[:, K_MASK:K_MASK + P].unsqueeze(1).unsqueeze(1).to_broadcast([P, AG, 2, P])
                v.tensor_tensor(own, own, mask, ALU.add).then_inc(*fg.mark("dve", "mask"))
                dve.wait_ge(*fg.after("dve", "mask", i))
                v.tensor_reduce(m3[:, 0:9], b_s[:].rearrange("p g b k -> p (g b) k"), AX, ALU.max).then_inc(*fg.mark("dve", "m3"))
                dve.wait_ge(*fg.after("dve", "m3", i))
                v.tensor_tensor(mm[:, 0:3], m3[:, 1:9:3], m3[:, 2:9:3], ALU.max).then_inc(*fg.mark("dve", "mm"))
                v.tensor_scalar(nmax[:, 0:6:2], m3[:, 0:9:3], -1.0, None, ALU.mult).then_inc(*fg.mark("dve", "n0"))
                dve.wait_ge(*fg.after("dve", "mm", i))
                v.tensor_scalar(nmax[:, 1:6:2], mm[:, 0:3], -1.0, None, ALU.mult).then_inc(*fg.mark("dve", "neg"))
            if j == 5:
                dve.wait_ge(*fg.after("act", "p", i))
                v.reciprocal(rden[:, 0:6], den[:, 0:6]).then_inc(*fg.mark("dve", "rd"))
            if j == 10:
                dve.wait_ge(*fg.after("pe", "o2", i))
                dve.wait_ge(*fg.after("dve", "rd", i))
                o = sc[0][:].rearrange("p (t c) -> p t c", t=T)[:, :, 0:AG * HD].rearrange("p t (g d) -> p t g d", d=HD)
                r = rden[:, 0:6].rearrange("p (g t) -> p t g", t=T)
                v.tensor_tensor(b_o[:], o, over(r, [P, T, AG, HD]), ALU.mult).then_inc(*fg.mark("dve", "on"))
                dve.wait_ge(*fg.after("dve", "on", i))
                z = pb[:, :, bass.ds(i * AG * HD + 3 * BW, AG * HD)].rearrange("p t (h d) -> p t h d", d=HD)
                v.tensor_tensor(z, b_o[:], z, ALU.mult).then_inc(*fg.mark("dve", "u"))

        run(dve, "gate_a", stream(gate_side(phases["gate_a"], y1, True, forget)))
        end_phase(dve, "gate_a")
        for n in range(3):
            split_lo(ub_split, lambda k: ol[:, k], lambda k: oh[:, k], n)
        for n in range(2):
            dve.wait_ge(*me_prep.after("act", f"sq{n}"))
            v.tensor_reduce(ssh[:, :, n * CH:(n + 1) * CH], me_sq[:].rearrange("p t (h d) -> p t h d", d=CD), AX, ALU.add).then_inc(*me_prep.mark("dve", f"ms{n}"))
        dve.wait_ge(*me_prep.after("dve", "ms1"))
        root_mean(me_prep, ssh[:, :, 0:2 * CH], 2 * CH, CD)

        def memory(i, j):
            if j == 0:
                dve.wait_ge(*me_prep.after("dve", "r"))
                for what, dst, src, h0 in (("qn", c_qn, pc, 0), ("kn", c_kn, mk1, CH)):
                    r = ssh[:, :, bass.ds(i + h0, 1)].to_broadcast([P, T, CD])
                    v.tensor_tensor(dst[:], src[:, :, bass.ds(i * CD, CD)], r, ALU.mult).then_inc(*me.mark("dve", what))
            if j == 2:
                dve.wait_ge(*me.after("pe", "s", i))
                v.tensor_reduce(nmax[:, 0:T], sc[0][:].rearrange("p (t m) -> p t m", t=T), AX, ALU.max, negate=True).then_inc(*me.mark("dve", "m"))
            if j == 4:
                dve.wait_ge(*me.after("act", "p", i))
                v.reciprocal(rden[:, 0:T], den[:, 0:T]).then_inc(*me.mark("dve", "rd"))
            if j == 7:
                dve.wait_ge(*me.after("pe", "o", i))
                dve.wait_ge(*me.after("dve", "rd", i))
                o = sc[1][:, 0:T * CD].rearrange("p (t d) -> p t d", t=T)
                v.tensor_tensor(c_qn[:], o, over(rden[:, 0:T], [P, T, CD]), ALU.mult).then_inc(*me.mark("dve", "on"))
                dve.wait_ge(*me.after("dve", "on", i))
                z = pc[:, :, bass.ds(i * CD + CW, CD)]
                v.tensor_tensor(z, c_qn[:], z, ALU.mult).then_inc(*me.mark("dve", "u"))

        run(dve, "gate_b", stream(gate_side(phases["gate_b"], y1, False, memory)))
        end_phase(dve, "gate_b")
        for n in range(2):
            split_lo(uc_split, lambda k: ol[:, 6 + k], lambda k: oh[:, 6 + k], n)
        run(dve, "gate_c", stream(gate_side(phases["gate_c"], y1, False)))
        end_phase(dve, "gate_c")
        for n in range(BANKS):
            split_lo(y1_split, lambda k: ol[:, OUT_SLOTS[k]], lambda k: oh[:, OUT_SLOTS[k]], n)

        def out_side(i, j):
            ph = phases["out"]
            if j == 0:
                norm_rest(norm_m2, lambda t: mem2_in[:, t], lambda t: mem2_in[:, t])
            if 4 <= j < 12:
                split_lo(norm_m2, lambda k: m2l[:, k], lambda k: m2h[:, k], j - 4, V_MEM2)
            blk, _, _, last = positions(ph)[j]
            if last:
                dve.wait_ge(in_x_again, 16)
                dve.wait_ge(chunk_done, ph.chunk(i, j) + 1)
                for t in range(T):
                    cols = slice(blk * NB, (blk + 1) * NB)
                    v.tensor_tensor(x1[:, t, cols], acc[blk % 2][t][:], x_again[:, t, cols], ALU.add).then_inc(acc_free[blk % 2], 1)
                dve.drain().then_inc(*out1.mark("dve", f"x{blk}"))

        run(dve, "out", stream(out_side))
        end_phase(dve, "out")

        def mem2_side(i, j):
            if j == 0:
                norm_rest(norm_x1, lambda t: x1[:, t], lambda t: x1n[:, t])
            if 6 <= j < 14:
                split_lo(norm_x1, lambda k: xl[:, k], lambda k: xh[:, k], j - 6, V_MIX)

        run(dve, "mem_kv_2", stream(mem2_side))
        end_phase(dve, "mem_kv_2")
        run(dve, "conv_proj", stream(nothing))
        end_phase(dve, "conv_proj")
        run(dve, "mq_proj", stream(nothing))
        end_phase(dve, "mq_proj")

        def hg_side(i, j):
            if j == 0:
                part = lambda n: cv[:, n, :, bass.ds(i * 2 * P, 2 * P)]
                v.tensor_tensor(u_st[:].rearrange("p t a b -> p t (a b)"), part(1), part(2), ALU.mult).then_inc(*conv.mark("dve", "u"))
            if j == 1:
                dve.wait_ge(*conv.after("pe", "u", i))
                w = lambda k, n: vcol[:, V_CONV[0], bass.ds(i * 2 + (V_CONV[1] + 8 * k + n), 1)]
                u = lambda n: tp[0][:, n * S:(n + 1) * S]
                for n in range(2):
                    ins = v.tensor_scalar(v_tm[:, n], u(n), w(2, n), None, ALU.mult)
                ins.then_inc(*conv.mark("dve", "c0"))
                for back in (1, 2):
                    dve.wait_ge(*conv.after("dve", f"c{back - 1}", i))
                    for n in range(2):
                        ins = v.scalar_tensor_tensor(v_tm[:, n, back:S], u(n)[:, 0:S - back], w(2 - back, n), v_tm[:, n, back:S], ALU.mult, ALU.add)
                    ins.then_inc(*conv.mark("dve", f"c{back}"))
                dve.wait_ge(*conv.after("pe", "b", i))
                dve.wait_ge(*conv.after("dve", "c2", i))
                flat = v_tm[:].rearrange("p a b -> p (a b)")
                v.tensor_tensor(flat, flat, tp[1][:], ALU.mult).then_inc(*conv.mark("dve", "y"))
            if j == 4:
                dve.wait_ge(*conv.after("act", "h", i))
                k = bass.ds(i * 2, 2)
                v.tensor_tensor(ol[:, k], v_tm[:], oh[:, k].bitcast(F32), ALU.subtract).then_inc(*conv.mark("dve", "l"))
            if j == 7:
                dve.wait_ge(*ma.after("pe", "s", i))
                v.tensor_reduce(nmax[:, 0:T], sc[0][:].rearrange("p (t m) -> p t m", t=T), AX, ALU.max, negate=True).then_inc(*ma.mark("dve", "m"))
            if j == 9:
                dve.wait_ge(*ma.after("act", "p", i))
                v.reciprocal(rden[:, 0:T], den[:, 0:T]).then_inc(*ma.mark("dve", "rd"))
            if j == 12:
                dve.wait_ge(*ma.after("pe", "o", i))
                dve.wait_ge(*ma.after("dve", "rd", i))
                v.tensor_tensor(mq[:, :, bass.ds(i * MD, MD)], sc[1][:].rearrange("p (t d) -> p t d", t=T),
                                over(rden[:, 0:T], [P, T, MD]), ALU.mult).then_inc(*ma.mark("dve", "u"))

        run(dve, "hg_proj", stream(hg_side))
        end_phase(dve, "hg_proj")
        for n in range(4):
            split_lo(ym_split, lambda k: ol[:, 16 + k], lambda k: oh[:, 16 + k], n)
        end_phase(dve, "hg_prep")

        def halves(tensor, s):
            w = tensor.rearrange("p (n two s) -> p n two s", two=2, s=s)
            return w[:, :, 0], w[:, :, 1]

        def recur(first):
            def side(i, j):
                it = i + first
                z = zt[:, bass.ds(it, 1)].rearrange("p a b -> p (a b)")
                q = qt[:, bass.ds(it, 1)].rearrange("p a b -> p (a b)")
                if j == 0:
                    v.scalar_tensor_tensor(h_a[:], z, -1.0, z, ALU.mult, ALU.max).then_inc(*hr.mark("dve", "a"))
                    dve.wait_ge(*hr.after("act", "l1", it))
                    v.scalar_tensor_tensor(h_ls[:], z, 0.0, h_l[:], ALU.min, ALU.subtract).then_inc(*hr.mark("dve", "ls"))
                    dve.wait_ge(*hr.after("dve", "ls", it))
                    v.tensor_scalar(h_d[:], h_ls[:], LOG_TINY, None, ALU.subtract).then_inc(*hr.mark("dve", "d0"))
                    dve.wait_ge(*hr.after("dve", "d0", it))
                    v.scalar_tensor_tensor(h_d[:], h_d[:], -1.0, h_d[:], ALU.mult, ALU.max).then_inc(*hr.mark("dve", "d"))
                    dve.wait_ge(*hr.after("act", "l2", it))
                    v.scalar_tensor_tensor(h_pre[:], h_ls[:], LOG_TINY, h_d[:], ALU.max, ALU.add).then_inc(*hr.mark("dve", "lf"))
                    dve.wait_ge(*hr.after("dve", "lf", it))
                    v.memset(h_suf[:], 0.0)
                    v.tensor_scalar(h_pre[:], h_pre[:], 0.0, None, ALU.min).then_inc(*hr.mark("dve", "lf0"))
                    v.tensor_tensor(h_k[:], h_ls[:], z, ALU.subtract).then_inc(*hr.mark("dve", "kz"))
                    dve.wait_ge(*hr.after("act", "k", it))
                    v.tensor_scalar(h_k[:], h_k[:], 1e-30, HK ** -0.5, ALU.subtract, ALU.mult).then_inc(*hr.mark("dve", "k"))
                if j == 1:
                    dve.wait_ge(*hr.after("pe", "d", it))
                    v.tensor_tensor(h_sc[:], sc[0][:, 0:T * P].rearrange("p (t k) -> p t k", t=T),
                                    ident.unsqueeze(1).to_broadcast([P, T, P]), ALU.mult).then_inc(*hr.mark("dve", "dg"))
                if 1 <= j < 9:
                    n = j - 1
                    s = (LEVELS + [P])[n]
                    e, g, pre, suf = (halves(w[:], s) for w in (h_e, h_g, h_pre, h_suf))
                    dve.wait_ge(*hr.after("act", f"el{n}", it))
                    if n >= 1:
                        dve.wait_ge(*hr.after("pe", f"s{n - 1}", it))
                    if n == len(LEVELS):
                        dve.wait_ge(*hr.after("dve", f"mk{n - 2}", it))
                    v.tensor_tensor(g[0], e[0], halves(h_k[:], s)[0], ALU.mult).then_inc(*hr.mark("dve", f"gl{n}"))
                    dve.wait_ge(*hr.after("act", f"er{n}", it))
                    v.tensor_tensor(g[1], e[1], halves(q, s)[1], ALU.mult).then_inc(*hr.mark("dve", f"gr{n}"))
                    if n < len(LEVELS):
                        shape = [P, S // (2 * s), s]
                        v.tensor_tensor(suf[0], suf[0], pre[1][:, :, s - 1:s].to_broadcast(shape), ALU.add).then_inc(*hr.mark("dve", f"suf{n}"))
                        dve.wait_ge(*hr.after("dve", f"suf{n}", it))
                        v.tensor_tensor(pre[1], pre[1], pre[0][:, :, s - 1:s].to_broadcast(shape), ALU.add).then_inc(*hr.mark("dve", f"pre{n}"))
                if 2 <= j < 9:
                    n = j - 2
                    v.copy_predicated(h_sc[:], lmask[:, n].unsqueeze(1).to_broadcast([P, T, P]),
                                      sc[(n + 1) % 2][:, 0:T * P].rearrange("p (t k) -> p t k", t=T)).then_inc(*hr.mark("dve", f"mk{n}"))
                if j == 10:
                    dve.wait_ge(*hr.after("act", "sq1", it))
                    v.tensor_scalar(ssk[:, 0:T], ssk[:, 0:T], 1.0 / HK, EPS, ALU.mult, ALU.add).then_inc(*hr.mark("dve", "e"))
                    dve.wait_ge(*hr.after("act", "rt", it))
                    v.reciprocal(ssk[:, 0:T], ssk[:, 0:T]).then_inc(*hr.mark("dve", "r"))
                    dve.wait_ge(*hr.after("dve", "r", it))
                    o = sc[1][:, 0:T * HK].rearrange("p (t d) -> p t d", t=T)
                    v.tensor_tensor(h_o[:], o, over(ssk[:, 0:T], [P, T, HK]), ALU.mult).then_inc(*hr.mark("dve", "on"))
                    dve.wait_ge(*hr.after("dve", "on", it))
                    u = hg[:, 3, :, bass.ds(it * HK, HK)]
                    v.tensor_tensor(u, h_o[:], u, ALU.mult).then_inc(*hr.mark("dve", "u"))
            return side

        dve.wait_ge(sig_free, 1)
        run(dve, "gate_conv", stream(gate_side(phases["gate_conv"], y2, True, recur(0))))
        end_phase(dve, "gate_conv")
        run(dve, "gate_mem", stream(gate_side(phases["gate_mem"], y2, False, recur(4))))
        end_phase(dve, "gate_mem")
        for n in range(4):
            split_lo(yb_split, lambda k: ol[:, 8 + k], lambda k: oh[:, 8 + k], n, V_HG)
        run(dve, "gate_hg", stream(gate_side(phases["gate_hg"], y2, False)))
        end_phase(dve, "gate_hg")
        for n in range(BANKS):
            split_lo(y2_split, lambda k: ol[:, OUT2_SLOTS[k]], lambda k: oh[:, OUT2_SLOTS[k]], n)
        run(dve, "out_2", stream(nothing))

        def post(st, src, gain, res):
            v.tensor_reduce(rn[:], ss4[:], AX, ALU.add).then_inc(*st.mark("dve", "ms"))
            dve.wait_ge(*st.after("dve", "ms"))
            root_mean(st, rn[:], T, D)
            dve.wait_ge(*st.after("dve", "r"))
            for t in range(T):
                v.scalar_tensor_tensor(src[:, t], src[:, t], rn[:, t:t + 1], gain[:], ALU.mult, ALU.mult).then_inc(*st.mark("dve", f"g{t}"))
            for t in range(T):
                dve.wait_ge(*st.after("dve", f"g{t}"))
                v.tensor_tensor(res[:, t], src[:, t], res[:, t], ALU.add).then_inc(*st.mark("dve", f"x{t}"))

        dve.wait_ge(in_x1, 32)
        dve.wait_ge(*mixs.after("act", "m3"))
        post(post1, mix, gpost, x2)
        norm_rest(norm_x2, lambda t: x2[:, t], lambda t: x2n[:, t])
        for n in range(BANKS):
            split_lo(norm_x2, lambda k: xl[:, k], lambda k: xh[:, k], n, V_FFN)
        end_phase(dve, "out_2")

        def ffn_conv(i):
            for h in range(2):
                dve.wait_ge(*ffs.after("pe", f"g{h}", i))
                for c in (2 * h, 2 * h + 1):
                    w = lambda k: vcol[:, V_FW[k][0], bass.ds(i * 4 + (V_FW[k][1] + c), 1)]
                    u = tp[h][:, (c % 2) * S:(c % 2 + 1) * S]
                    v.tensor_scalar(f_c[:, c], u, w(2), None, ALU.mult).then_inc(*ffs.mark("dve", f"c{c}"))
                    dve.wait_ge(*ffs.after("dve", f"c{c}", i))
                    for back in (1, 2):
                        v.scalar_tensor_tensor(f_c[:, c, back:S], u[:, 0:S - back], w(2 - back), f_c[:, c, back:S],
                                               ALU.mult, ALU.add).then_inc(*ffs.mark("dve", f"b{c}{back}"))
                        dve.wait_ge(*ffs.after("dve", f"b{c}{back}", i))

        def ffn_mul(i):
            dve.wait_ge(*ffs.after("act", "gelu", i))
            for h in range(2):
                dve.wait_ge(*ffs.after("pe", f"v{h}", i))
                part = f_a[:, 2 * h:2 * h + 2].rearrange("p a b -> p (a b)")
                ins = v.tensor_tensor(part, part, tp[h][:], ALU.mult)
            ins.then_inc(*ffs.mark("dve", "y"))

        def ffn_lo(i):
            dve.wait_ge(*ffs.after("act", "h", i))
            k = bass.ds(i * 4, 4)
            v.tensor_tensor(fl[:, k], f_a[:], fh[:, k].bitcast(F32), ALU.subtract).then_inc(*ffs.mark("dve", "l"))

        def ffn_side(i, j):
            if j == 1:
                ffn_conv(i)
            if j == 5:
                ffn_mul(i)
            if j == 6:
                ffn_lo(i)

        run(dve, "ffn_first", stream(nothing))
        dve.wait_ge(out_x2, 16)
        run(dve, "ffn_up", stream(ffn_side))
        last = FT // 4 - 1
        ffn_conv(last)
        ffn_mul(last)
        ffn_lo(last)
        end_phase(dve, "ffn_up")
        ph = phases["ffn_down"]
        stream(nothing)(ph, 0)
        stream(nothing, skip_last=True)(ph, 1)
        dve.wait_ge(in_x2, 32)
        dve.wait_ge(*ffe.after("act", "m"))
        post(post2, ff, gpost2, x2b)

    ctx.close()


def kernel(**inputs):
    import numpy as _np
    import concourse.bacc as _bacc
    from concourse import mybir as _mybir
    from concourse.bass_utils import run_bass_kernel_spmd as _run

    nc = _bacc.Bacc("TRN2", target_bir_lowering=False, num_devices=1)
    constants, level_masks = shape_constants()
    arrays, args = {}, {}
    given = {n: _np.ascontiguousarray(a) for n, a in inputs.items() if n != "hg_lower_bounds_2"}
    for name, a in {**given, "constants": constants, "level_masks": level_masks}.items():
        arrays[f"in_{name}"] = a
        args[name] = nc.dram_tensor(f"in_{name}", a.shape, _mybir.dt.from_np(a.dtype), kind="ExternalInput").ap()
    out = nc.dram_tensor("out_x", (1, S, D), F32, kind="ExternalOutput").ap()
    two_blocks(nc, out=out, **args)
    r = _run(nc, [arrays], core_ids=[0])
    return r.results[0]["out_x"]
```

```python
from contextlib import ExitStack

import numpy as np

import concourse.bass as bass
from concourse import mybir

F32 = mybir.dt.float32
F32R = mybir.dt.float32r
U8 = mybir.dt.uint8
ALU = mybir.AluOpType
ACT = mybir.ActivationFunctionType
AX = mybir.AxisListType.X

P = 128
D = 2048
S = 256
T = S // P
KT = D // P
NB = 512
EPS = 1e-6
NEG = -1e30
RING = 4
LEAD = 3

HD = 64
AH, AKV, AG = 12, 4, 3
BH = 12
CH, CD = 4, 128
AW, AKW, BW, CW = AH * HD, AKV * HD, BH * HD, CH * CD
A_COLS = 2 * AW + 2 * AKW
B_AT = A_COLS
F_AT = B_AT + 4 * BW
C_AT = F_AT + BH
G_AT = C_AT + 2 * CW

BR = D // 2
HH, HK = 8, 128
MH, MD = 4, 256
FF = 5632
FT = FF // P
HQ_AT, MQ_AT, G2_AT = 3 * BR, 7 * BR, 8 * BR
LOG_TINY = float(np.log(np.float32(1e-30)))
LEVELS = [1, 2, 4, 8, 16, 32, 64]

V_NORM, V_MEM, V_MIX, V_MEM2, V_FFN = (0, 0), (0, 16), (0, 32), (0, 48), (0, 64)
V_CONV, V_HG = (0, 80), (0, 104)
V_FW = [(1, 0), (1, FT), (2, 0)]
V_FB = (2, FT)
V_QK = 2 * FT
V_ROWS = [112, V_QK + 6, 2 * FT]

K_ID, K_REL, K_MASK, K_TRI, K_ONE, K_SLOPE = 0, 128, 512, 640, 768, 896
K_COLS = K_SLOPE + AH


def shape_constants():
    p = np.arange(P)
    c = np.zeros((P, K_COLS), np.float32)
    c[:, K_ID:K_ID + P] = np.eye(P)
    own = p[:, None] - p[None, :]
    before = own + P
    far = np.float32(1e34)
    own_rel = np.where(own >= 0, own, far)
    c[:, K_REL:K_REL + P] = own_rel
    c[:, K_REL + P:K_REL + 2 * P] = np.where(before < P, before, far)
    c[:, K_REL + 2 * P:K_REL + 3 * P] = own_rel
    c[:, K_MASK:K_MASK + P] = np.where(own >= 0, 0, NEG)
    c[:, K_TRI:K_TRI + P] = p[:, None] <= p[None, :]
    c[:, K_ONE:K_ONE + P] = 1
    c[:, K_SLOPE:] = -np.exp2(-8.0 * np.arange(1, AH + 1) / AH).astype(np.float32)
    j, i = p[:, None], p[None, :]
    masks = [(j // (2 * s) == i // (2 * s)) & (j // s % 2 == 0) & (i // s % 2 == 1) for s in LEVELS]
    return c, np.concatenate(masks, 1).astype(np.float32)


class Stage:

    def __init__(self, sem, name, **steps):
        self.steps = steps
        self.sems = {e: sem(f"{name}_{e}") for e in steps}
        self.place = {e: 0 for e in steps}

    def after(self, engine, step, it=0):
        n = self.steps[engine]
        return self.sems[engine], it * len(n) + n.index(step) + 1

    def mark(self, engine, step):
        n = self.steps[engine]
        assert n[self.place[engine]] == step, (n[self.place[engine]], step)
        self.place[engine] = (self.place[engine] + 1) % len(n)
        return self.sems[engine], 1


class Phase:

    def __init__(self, name, times, sizes, before):
        self.name, self.times, self.sizes, self.n = name, times, sizes, len(sizes)
        self.c0 = before.c0 + before.n * before.times if before else 0
        self.b0 = before.b0 + before.blocks * before.times if before else 0
        self.blocks = 0

    def chunk(self, i, j):
        return i * self.n + (self.c0 + j)

    def use(self, i, block):
        return i * (self.blocks // 2) + (self.b0 + block) // 2


FULL = [2] * (KT // 2)


def plan():
    gate_a = FULL + [2, 2, 1, 1]
    gate_c = FULL + [1, 1, 1, 1]
    gate_2 = FULL + [2, 2, 2, 2]
    down = [2] * 20 + [1] * 4
    spec = [
        ("a_proj", 2, FULL * 2, 2), ("b_proj", 3, FULL * 2, 2), ("c_proj", 1, FULL * 4, 4),
        ("gate_a", 4, gate_a, 2), ("gate_b", 4, gate_a, 2), ("gate_c", 4, gate_c, 2),
        ("out", 1, FULL * 4, 4), ("mem_kv_2", 1, FULL * 4, 4),
        ("conv_proj", 3, FULL * 2, 2), ("mq_proj", 1, FULL * 2, 2), ("hg_proj", 4, FULL * 2, 2),
        ("gate_conv", 4, gate_2, 2), ("gate_mem", 4, gate_2, 2), ("gate_hg", 4, gate_2, 2),
        ("out_2", 1, FULL * 4, 4), ("ffn_first", 1, FULL * 2, 2), ("ffn_up", FT // 4 - 1, FULL * 2, 2),
        ("ffn_down", 2, down * 2, 2),
    ]
    phases, before = {}, None
    for name, times, sizes, blocks in spec:
        before = Phase(name, times, sizes, before)
        before.blocks = blocks
        phases[name] = before
    return phases, before.c0 + before.n * before.times


def two_blocks(
    nc, x, mem, norm_gain, mem_norm_gain, w_in, b_forget, q_gain_a, k_gain_a, sinks_a, q_gain_b, k_gain_b,
    q_gain_c, k_gain_c, w_mem_kv, w_branch_a, w_branch_b, w_branch_c, w_out, mem_2, w_in_2, conv_mix_w_2,
    hg_norm_w_2, w_mem_kv_2, w_branch_2, w_out_2, norm_mix_pre_2, norm_mix_post_2, norm_mem_2,
    norm_ffn_pre_2, norm_ffn_post_2, w_ffn_up_2, conv_ffn_w_2, conv_ffn_b_2, w_ffn_down_2,
    constants, level_masks, out,
):
    phases, chunks = plan()
    ctx = ExitStack()

    def sem(name):
        return ctx.enter_context(nc.semaphore(name))

    base = (nc.sbuf_base + 31) // 32 * 32
    names = set()

    def at(name, offset, shape, dt=F32):
        assert name not in names
        names.add(name)
        return nc.alloc_sbuf_tensor_at(name, [P, *shape], dt, offset=base + offset)

    CHUNK = 2 * NB * 4
    TK = S * 4
    RAW_AT, HI_AT, LO_AT = 0, RING * CHUNK, 2 * RING * CHUNK
    X_AT = 3 * RING * CHUNK
    CONST_AT = X_AT + 2 * KT * TK
    O_AT = CONST_AT + 11776
    W_AT = O_AT + 48 * TK

    raw = at("raw", RAW_AT, [RING, 2, NB])
    hi = at("hi", HI_AT, [RING, 2, NB], F32R)
    lo = at("lo", LO_AT, [RING, 2, NB], F32R)
    xh = at("xh", X_AT, [KT, S], F32R)
    xl = at("xl", X_AT + KT * TK, [KT, S], F32R)
    oh = at("oh", O_AT, [24, S], F32R)
    ol = at("ol", O_AT + 24 * TK, [24, S], F32R)
    m2h = at("m2h", W_AT + 16384, [KT, S], F32R)
    m2l = at("m2l", W_AT + 32768, [KT, S], F32R)
    fh = at("fh", O_AT, [FT, S], F32R)
    fl = at("fl", O_AT + FT * TK, [FT, S], F32R)

    cursor = [CONST_AT]

    def const(name, shape, dt=F32):
        size = int(np.prod(shape)) * (1 if dt == U8 else 4)
        t = at(name, cursor[0], shape, dt)
        cursor[0] += (size + 31) // 32 * 32
        assert cursor[0] <= O_AT
        return t

    kc = const("kc", [K_COLS])
    lmask = const("lmask", [len(LEVELS), P], U8)
    vcol = const("vcol", [3, P])
    gqk = const("gqk", [3])
    sinks = const("sinks", [AH])
    bfor = const("bfor", [BH])
    wf_raw = const("wf_raw", [KT, BH])
    wf_hi = const("wf_hi", [KT, BH], F32R)
    wf_lo = const("wf_lo", [KT, BH], F32R)
    ss4 = const("ss4", [T, 4])
    rnf = const("rnf", [T])
    rn = const("rn", [T])
    rnx = const("rnx", [T])
    ssh = const("ssh", [T, 2 * BH])
    nmax = const("nmax", [8])
    m3 = const("m3", [12])
    mm = const("mm", [4])
    es = const("es", [8])
    den = const("den", [8])
    rden = const("rden", [8])
    cq = const("cq", [T, BH])
    logf = const("logf", [T, BH])
    tf = const("tf", [T, BH])
    ssk = const("ssk", [8])
    ident = kc[:, K_ID:K_ID + P]

    pa = at("pa", W_AT, [T, A_COLS])
    pb = at("pb", W_AT + 16384, [T, 4 * BW])
    pc = at("pc", W_AT + 40960, [T, 2 * CW])
    mk1 = at("mk1", W_AT + 49152, [T, 2 * CW])
    x_in = at("x_in", W_AT + 16384, [T, D])
    mem_in = [at("mem_in0", O_AT + 16 * TK, [D]), at("mem_in1", O_AT + 40 * TK, [D])]
    vrow = at("vrow", W_AT + 57344, [3, P])
    y1 = at("y1", W_AT, [T, D])
    sig = at("sig", W_AT + 65536, [T, NB])
    lmask_in = at("lmask_in", W_AT + 65536, [len(LEVELS), P])
    a_qn = at("a_qn", W_AT + 40960, [T, AKV, HD])
    a_qt = at("a_qt", W_AT + 43008, [2, S])
    a_kt = at("a_kt", W_AT + 45056, [2, S])
    a_s = at("a_s", W_AT + 47104, [AKV, 3, P])
    a_pt = at("a_pt", W_AT + 53248, [2, 3, P])
    a_o = at("a_o", W_AT + 56320, [T, AKV, HD])
    a_sq = at("a_sq", W_AT + 47104, [T, AW + AKW])
    a_kn = at("a_kn", W_AT + 55296, [T, AKW])
    b_sq = at("b_sq", W_AT + 57344, [2 * BW])
    nck = at("nck", O_AT, [BH, S])
    ct = at("ct", W_AT + 63488, [S])
    B_AT_ = O_AT + 24 * TK
    b_qn = at("b_qn", B_AT_, [T, AG, HD])
    b_kn = at("b_kn", B_AT_ + 1536, [T, AG, HD])
    b_qt = at("b_qt", B_AT_ + 3072, [2, S])
    b_kt = at("b_kt", B_AT_ + 5120, [2, S])
    b_s = at("b_s", B_AT_ + 7168, [AG, 3, P])
    b_pt = at("b_pt", B_AT_ + 11776, [2, 3, P])
    b_o = at("b_o", B_AT_ + 14848, [T, AG, HD])
    c_qn = at("c_qn", W_AT + 57344, [T, CD])
    c_kn = at("c_kn", W_AT + 58368, [T, CD])
    c_qt = at("c_qt", W_AT + 59392, [S])
    c_kt = at("c_kt", W_AT + 60416, [S])
    c_p = at("c_p", W_AT + 61440, [T, S])
    c_pt = at("c_pt", W_AT + 63488, [T, S])
    me_sq = at("me_sq", W_AT + 57344, [T, CW])
    x_again = at("x_again", X_AT, [T, D])
    mem2_in = at("mem2_in", W_AT + 49152, [T, D])
    x1 = at("x1", W_AT, [T, D])
    x1n = at("x1n", W_AT + 49152, [T, D])
    mk2 = at("mk2", O_AT + 8 * TK, [T, BR])
    mv2 = at("mv2", O_AT + 32 * TK, [T, BR])
    hg = at("hg", W_AT, [4, T, BR])
    cv = at("cv", W_AT + 32768, [3, T, BR])
    mq = at("mq", W_AT + 57344, [T, BR])
    u_st = at("u_st", W_AT + 65536, [T, 2, P])
    cb_st = at("cb_st", W_AT + 67584, [T, 2, P])
    v_tm = at("v_tm", O_AT + 16 * TK, [2, S])
    d_q = at("d_q", O_AT + 18 * TK, [T, MD])
    d_k = at("d_k", O_AT + 20 * TK, [T, MD])
    d_qt = at("d_qt", O_AT + 22 * TK, [2, S])
    d_kt = at("d_kt", O_AT + 40 * TK, [2, S])
    d_p = at("d_p", O_AT + 42 * TK, [T, S])
    d_pt = at("d_pt", O_AT + 44 * TK, [T, S])
    qt = at("qt", W_AT + 32768, [HH, S])
    zt = at("zt", W_AT + 40960, [HH, S])
    H_AT, H2_AT = O_AT + 8 * TK, O_AT + 32 * TK
    h_a = at("h_a", H_AT, [S])
    h_l = at("h_l", H_AT + 1024, [S])
    h_pre = at("h_pre", H_AT + 2048, [S])
    h_suf = at("h_suf", H_AT + 3072, [S])
    h_k = at("h_k", H_AT + 4096, [S])
    h_e = at("h_e", H_AT + 5120, [S])
    h_g = at("h_g", H_AT + 6144, [S])
    h_sc = at("h_sc", H2_AT, [T, P])
    h_off = at("h_off", H2_AT + 1024, [P])
    h_o = at("h_o", H2_AT + 1536, [T, HK])
    h_ls = at("h_ls", H2_AT + 2560, [S])
    h_d = at("h_d", H2_AT + 3584, [S])
    y2 = at("y2", W_AT, [T, D])
    mix = at("mix", W_AT, [T, D])
    x2 = at("x2", W_AT + 16384, [T, D])
    gpost = at("gpost", W_AT + 32768, [D])
    F_W = W_AT + 40960
    f_g = at("f_g", F_W, [T, NB])
    f_v = at("f_v", F_W + 4096, [T, NB])
    f_c = at("f_c", F_W + 8192, [4, S])
    f_a = at("f_a", F_W + 12288, [4, S])
    ff = at("ff", F_W, [T, D])
    x2b = at("x2b", X_AT, [T, D])
    gpost2 = at("gpost2", X_AT + KT * TK, [D])

    acc = [[ctx.enter_context(nc.psum_tensor(f"acc{p}{t}", [P, NB], F32)) for t in range(T)] for p in range(2)]
    tp = [ctx.enter_context(nc.psum_tensor(f"tp{n}", [P, NB], F32)) for n in range(2)]
    sc = [ctx.enter_context(nc.psum_tensor(f"sc{n}", [P, NB], F32)) for n in range(2)]

    nck_d = nc.dram_tensor("nck_d", [BH, S], F32).ap()
    x1_d = nc.dram_tensor("x1_d", [S, D], F32).ap()
    x2_d = nc.dram_tensor("x2_d", [S, D], F32).ap()

    loaded = [sem(f"chunk_loaded{n}") for n in range(RING)]
    hi_ready = sem("hi_ready")
    lo_ready = sem("lo_ready")
    chunk_done = sem("chunk_done")
    acc_free = [sem(f"acc_free{n}") for n in range(2)]
    phase_end = sem("phase_end")
    in_first, in_const, in_mem, in_wf = (sem(n) for n in ("in_first", "in_const", "in_mem", "in_wf"))
    in_x = [sem(f"in_x_half{half}") for half in range(2)]
    in_mem2, in_x_again, out_x1, in_x1 = sem("in_mem2"), sem("in_x_again"), sem("out_x1"), sem("in_x1")
    out_x2, in_x2, out_nck, in_nck, out_y = (sem(n) for n in ("out_x2", "in_x2", "out_nck", "in_nck", "out_y"))

    BANKS = KT // 2

    def split_steps(banks):
        return dict(pe=[f"t{n}" for n in range(banks)], act=[f"h{n}" for n in range(banks)],
                    dve=[f"l{n}" for n in range(banks)])

    def norm_stage(name):
        s = split_steps(BANKS)
        return Stage(sem, name, pe=s["pe"], act=[f"sq{n}" for n in range(4 * T)] + ["rt"] + s["act"], dve=["ms", "e", "r", "n0", "n1"] + s["dve"])

    setup = Stage(sem, "setup", pe=["vn", "v"], act=["wh"], dve=["vn", "v", "qk0", "qk1", "wl"])
    norm_m, norm_m2, norm_x1 = (norm_stage(n) for n in ("norm_m", "norm_m2", "norm_x1"))
    x_split, x2_split = (Stage(sem, n, **split_steps(BANKS)) for n in ("x_split", "x2_split"))
    x_norm, x2_norm = (Stage(sem, n, act=[f"sq{k}" for k in range(4 * T)] + ["rt"], dve=["ms", "e", "r"])
                       for n in ("x_norm", "x2_norm"))
    win_prep = Stage(sem, "win_prep", pe=["k"], act=["sq", "rt", "silu", "k"], dve=["ms", "e", "r", "kn"])
    G4 = range(AKV)
    G3 = range(AG)
    win = Stage(
        sem, "win",
        pe=["q"] + [f"s{g}" for g in G4] + [f"{k}{g}" for g in G4 for k in ("pt", "o")],
        act=["q", "p"] + ["es"] + [f"pt{g}" for g in G4],
        dve=["qn"] + [f"s{g}" for g in G4] + ["m3", "mm", "n0", "n1", "neg", "es", "den", "rd", "on", "u"])
    ua_split = Stage(sem, "ua_split", **split_steps(3))
    fg_prep = Stage(
        sem, "fg_prep", pe=["f", "c", "ct"], act=["sq0", "sq1", "rt", "silu", "e", "l"],
        dve=["ms0", "ms1", "e", "r", "z", "a", "lf", "c", "ct"])
    fg = Stage(
        sem, "fg",
        pe=["q", "k"] + [f"s{g}" for g in G3] + [f"{k}{g}" for g in G3 for k in ("pt", "o")],
        act=["q", "k", "p"] + [f"pt{g}" for g in G3],
        dve=["qn", "kn"] + [f"s{g}" for g in G3] + ["mask", "m3", "mm", "n0", "neg", "rd", "on", "u"])
    ub_split = Stage(sem, "ub_split", **split_steps(3))
    me_prep = Stage(sem, "me_prep", act=["sq0", "sq1", "rt", "silu"], dve=["ms0", "ms1", "e", "r"])
    me = Stage(sem, "me", pe=["qk", "s", "pt", "o"], act=["q", "k", "p", "pt"], dve=["qn", "kn", "m", "rd", "on", "u"])
    uc_split = Stage(sem, "uc_split", **split_steps(2))
    y1_split = Stage(sem, "y1_split", **split_steps(BANKS))
    y2_split = Stage(sem, "y2_split", **split_steps(BANKS))
    sig_free = sem("sig_free")
    GATES = ("gate_a", "gate_b", "gate_c", "gate_conv", "gate_mem", "gate_hg")
    out1 = Stage(sem, "out1", dve=[f"x{n}" for n in range(4)])
    conv = Stage(sem, "conv", pe=["u", "b"], act=["cb", "h"], dve=["u", "c0", "c1", "c2", "y", "l"])
    ma = Stage(sem, "ma", pe=["q", "k", "s", "pt", "o"], act=["sq", "sk", "q", "k", "p", "pt"], dve=["m", "rd", "u"])
    ym_split = Stage(sem, "ym_split", **split_steps(4))
    hg_prep = Stage(sem, "hg_prep", pe=[f"t{n}" for n in range(8)], act=[f"t{n}" for n in range(8)] + ["silu"])
    LV = range(len(LEVELS))
    hp = Stage(sem, "hp", act=["e1", "l1", "e2", "l2", "k"], dve=["a", "ls", "d0", "d", "lf", "lf0", "kz", "k"])
    hr_dve = ["dg"]
    for n in range(len(LEVELS) + 1):
        hr_dve += [f"gl{n}", f"gr{n}"]
        if n < len(LEVELS):
            hr_dve += [f"suf{n}", f"pre{n}"]
        if n > 0:
            hr_dve += [f"mk{n - 1}"]
    hr = Stage(
        sem, "hr", pe=["d"] + [f"s{n}" for n in LV] + ["s7", "o"],
        act=[f"e{k}{n}" for n in range(8) for k in "lr"] + ["off", "sq0", "sq1", "rt"],
        dve=hr_dve + ["e", "r", "on", "u"])
    yb_split = Stage(sem, "yb_split", **split_steps(4))
    mixs, ffe = (Stage(sem, n, act=[f"m{b}{t}" for b in range(4) for t in range(T)]) for n in ("mixs", "ffe"))
    post1 = Stage(sem, "post1", act=["rt"], dve=[f"w{q}" for q in range(4)] + ["ms", "e", "r"] + [f"x{q}" for q in range(4)])
    ffs = Stage(sem, "ffs", pe=["g0", "g1", "v0", "v1"], act=["ev", "gelu", "h"],
                dve=[f"{k}" for c in range(4) for k in (f"c{c}", f"b{c}1", f"b{c}2")] + ["y", "l"])
    post2 = Stage(sem, "post2", act=["rt"], dve=[f"w{q}" for q in range(4)] + ["ms", "e", "r"] + [f"x{q}" for q in range(4)])

    def w3(w):
        return w.rearrange("(k p) n -> p k n", p=P)

    wi, wi2 = w3(w_in[0]), w3(w_in_2[0])
    w_up, w_down = w3(w_ffn_up_2[0]), w3(w_ffn_down_2[0])
    w_o, w_o2, w_m, w_m2 = w3(w_out[0]), w3(w_out_2[0]), w3(w_mem_kv[0]), w3(w_mem_kv_2[0])
    w_br = {"a": w3(w_branch_a[0]), "b": w3(w_branch_b[0]), "c": w3(w_branch_c[0])}
    w_br2 = [w3(w_branch_2[0, n]) for n in range(3)]

    def weights(name, i, n):
        two = lambda w, col: [(w, col), (w, col + NB)]
        if name == "a_proj":
            return two(wi, i * 2 * NB)
        if name == "b_proj":
            return two(wi, i * 2 * NB + B_AT)
        if name == "c_proj":
            return two(wi, C_AT) + two(w_m, 0)
        if name in ("gate_a", "gate_b", "gate_c"):
            return [(wi, i * NB + (G_AT + "abc".index(name[-1]) * D)), (w_br[name[-1]], n * NB - NB)]
        if name in ("out", "out_2", "mem_kv_2"):
            w = {"out": w_o, "out_2": w_o2, "mem_kv_2": w_m2}[name]
            return two(w, 0) + two(w, 2 * NB)
        if name == "conv_proj":
            return two(wi2, i * 2 * NB)
        if name == "mq_proj":
            return two(wi2, MQ_AT)
        if name == "hg_proj":
            return two(wi2, i * 2 * NB + HQ_AT)
        if name in ("gate_conv", "gate_hg", "gate_mem"):
            g = ("gate_conv", "gate_hg", "gate_mem").index(name)
            return [(wi2, i * NB + (G2_AT + g * D)), (w_br2[g], n * NB - NB)]
        if name == "ffn_first":
            return [(w_up, 0), (w_up, FF)]
        if name == "ffn_up":
            return [(w_up, i * NB + NB), (w_up, i * NB + (FF + NB))]
        if name == "ffn_down":
            return two(w_down, i * 2 * NB)

    def positions(ph):
        per = {"ffn_down": len(ph.sizes) // 2}.get(ph.name, KT // 2)
        res, k, block = [], 0, 0
        for j, size in enumerate(ph.sizes):
            new = j > 0 and (j % per == 0 if not ph.name.startswith("gate") else j == KT // 2)
            if new:
                block, k = block + 1, 0
            res.append([block, k, size, False])
            k += size
        for j, r in enumerate(res):
            r[3] = j + 1 == len(res) or res[j + 1][0] != r[0]
        return res

    OUT_SLOTS = [*range(10, 24), 0, 1]
    OUT2_SLOTS = [*range(0, 8), *range(16, 24)]

    def stationary(name, block):
        own = lambda k: k
        if name in ("a_proj", "b_proj", "conv_proj", "mq_proj", "hg_proj", "ffn_first", "ffn_up"):
            return xh, xl, own
        if name == "c_proj":
            return (xh, xl, own) if block < 2 else (oh, ol, own)
        if name.startswith("gate"):
            if block == 0:
                return xh, xl, own
            first = {"gate_a": 16, "gate_b": 0, "gate_c": 6, "gate_conv": 0, "gate_mem": 16, "gate_hg": 8}[name]
            return oh, ol, lambda k: first + k
        if name == "out":
            return oh, ol, lambda k: OUT_SLOTS[k]
        if name == "out_2":
            return oh, ol, lambda k: OUT2_SLOTS[k]
        if name == "mem_kv_2":
            return m2h, m2l, own
        return fh, fl, own

    block_ctx = ctx.enter_context(nc.Block())

    def run(engine, name, body, first=None, last=None):
        ph = phases[name]
        begin, end = 0, ph.times
        if first or ph.c0 == 0:
            (first or body)(ph, 0)
            begin = 1
        if last:
            end -= 1
        if end - begin == 1:
            body(ph, begin)
        elif end > begin:
            with engine.Fori(begin, end) as i:
                body(ph, i)
        if last:
            last(ph, end)

    def late(side):
        return lambda i, j: side(i, j - 1)

    ENDS = ["a_proj", "b_proj", "c_proj", "gate_a", "gate_b", "gate_c", "out", "mem_kv_2", "conv_proj",
            "mq_proj", "hg_proj", "hg_prep", "gate_conv", "gate_mem", "gate_hg", "out_2", "ffn_up"]

    def ended(name):
        return phase_end, 3 * (ENDS.index(name) + 1)

    def end_phase(engine, name, wait=True):
        engine.drain().then_inc(phase_end, 1)
        if wait:
            engine.wait_ge(*ended(name))

    def gate_used(name, i):
        return sig_free, 1 + T * (GATES.index(name) * (D // NB) + i + 1)

    @block_ctx.sync
    def _(sp):
        def rows(dst, vec, n, landed=in_const):
            sp.dma_start(dst, vec.rearrange("(r c) -> r c", c=P) if n > 1 else vec).then_inc(landed, 16)

        sp.dma_start(kc[:], constants).then_inc(in_first, 16)
        rows(vrow[V_NORM[1]:V_NORM[1] + KT, V_NORM[0]], norm_gain[0], KT, in_first)
        for half in range(2):
            cols = slice(half * D // 2, (half + 1) * D // 2)
            sp.dma_start(x_in[:, :, cols], x[0].rearrange("(t p) d -> p t d", p=P)[:, :, cols]).then_inc(in_x[half], 16)

        def vectors():
            for (g, r), vec in ((V_MEM, mem_norm_gain), (V_MIX, norm_mix_pre_2),
                                (V_MEM2, norm_mem_2), (V_FFN, norm_ffn_pre_2)):
                rows(vrow[r:r + KT, g], vec[0], KT)
            for k in range(3):
                rows(vrow[V_CONV[1] + 8 * k:V_CONV[1] + 8 * k + 8, 0], conv_mix_w_2[0, k], 8)
                g, r = V_FW[k]
                rows(vrow[r:r + FT, g], conv_ffn_w_2[0, k], FT)
            rows(vrow[V_HG[1]:V_HG[1] + HH, 0], hg_norm_w_2[0], HH)
            rows(vrow[V_FB[1]:V_FB[1] + FT, 2], conv_ffn_b_2[0], FT)
            for k, vec in enumerate((q_gain_a, k_gain_a, q_gain_b, k_gain_b)):
                for half in range(2):
                    sp.dma_start(vrow[V_QK + k:V_QK + k + 1, 1, half * HD:half * HD + HD], vec).then_inc(in_const, 16)
            for k, vec in enumerate((q_gain_c, k_gain_c)):
                sp.dma_start(vrow[V_QK + 4 + k:V_QK + 5 + k, 1, :], vec).then_inc(in_const, 16)
            sp.dma_start(sinks[:], sinks_a.partition_broadcast(P)).then_inc(in_const, 16)
            sp.dma_start(bfor[:], b_forget.partition_broadcast(P)).then_inc(in_const, 16)
            sp.dma_start(lmask_in[:], level_masks.rearrange("p (l c) -> p l c", c=P)).then_inc(in_const, 16)

        def load(ph, i, n=1):
            spec = weights(ph.name, i, n)
            for j, (blk, k, size, _) in enumerate(positions(ph)):
                c = ph.chunk(i, j)
                slot = (ph.c0 + j) % RING
                w, col = spec[blk]
                source = w[:, k:k + size, bass.ds(col, NB)]
                if not (isinstance(c, int) and c < RING):
                    sp.wait_ge(lo_ready, c - (RING - 1))
                sp.dma_start(raw[:, slot, 0:size], source).then_inc(loaded[slot], 16)
                if isinstance(c, int) and c == LEAD - 1:
                    vectors()

        ph = phases["a_proj"]
        load(ph, 0)
        load(ph, 1)
        for name in list(phases)[1:]:
            ph = phases[name]
            if ph.times == 1:
                load(ph, 0)
            else:
                with sp.Fori(1, ph.times + 1) as n:
                    load(ph, n - 1, n)
        for q in range(4):
            cols = slice(q * NB, (q + 1) * NB)
            sp.wait_ge(*post2.after("dve", f"x{q}"))
            sp.dma_start(out[0].rearrange("(t p) d -> p t d", p=P)[:, :, cols], x2b[:, :, cols]).then_inc(out_y, 16)
        sp.wait_ge(out_y, 16 * 4)

    N_CONST = 4 + 3 * 2 + 2 + 8 + 2 + 3

    @block_ctx.gpsimd
    def _(pool):
        pool.wait_ge(in_x[1], 16)
        pool.dma_start(wf_raw[:], wi[:, :, F_AT:F_AT + BH]).then_inc(in_wf, 16)
        for t in range(T):
            pool.dma_start(mem_in[t][:], mem[0, t * P:(t + 1) * P]).then_inc(in_mem, 16)
        pool.wait_ge(*fg_prep.after("dve", "ct"))
        pool.dma_start(nck_d, ct[0:BH, :]).then_inc(out_nck, 16)
        pool.wait_ge(out_nck, 16)
        pool.wait_ge(*ended("c_proj"))
        pool.dma_start(nck[:], nck_d.partition_broadcast(P)).then_inc(in_nck, 16)
        pool.wait_ge(*ended("gate_b"))
        pool.dma_start(mem2_in[:], mem_2[0].rearrange("(t p) d -> p t d", p=P)).then_inc(in_mem2, 16)
        pool.wait_ge(*ended("gate_c"))
        pool.dma_start(x_again[:], x[0].rearrange("(t p) d -> p t d", p=P)).then_inc(in_x_again, 16)
        pool.wait_ge(*out1.after("dve", "x3"))
        pool.dma_start(x1_d.rearrange("(t p) d -> p t d", p=P), x1[:]).then_inc(out_x1, 16)
        pool.wait_ge(out_x1, 16)
        pool.wait_ge(*ended("gate_hg"))
        pool.dma_start(x2[:], x1_d.rearrange("(t p) d -> p t d", p=P)).then_inc(in_x1, 16)
        pool.dma_start(gpost[:], norm_mix_post_2[0].partition_broadcast(P)).then_inc(in_x1, 16)
        pool.wait_ge(*post1.after("dve", "x3"))
        pool.dma_start(x2_d.rearrange("(t p) d -> p t d", p=P), x2[:]).then_inc(out_x2, 16)
        pool.wait_ge(out_x2, 16)
        pool.wait_ge(*ended("ffn_up"))
        pool.dma_start(x2b[:], x2_d.rearrange("(t p) d -> p t d", p=P)).then_inc(in_x2, 16)
        pool.dma_start(gpost2[:], norm_ffn_post_2[0].partition_broadcast(P)).then_inc(in_x2, 16)

    @block_ctx.tensor
    def _(pe):
        def mm(o, lhsT, rhs, start=True, stop=True):
            return nc.tensor.matmul(o, lhsT, rhs, start=start, stop=stop)

        def tr(o, in_):
            k = in_.shape[0]
            return nc.tensor.transpose(o, in_, ident[0:k, :])

        def chunk(ph, i, j, pos):
            blk, k0, size, last = pos
            pair = blk % 2
            slot = (ph.c0 + j) % RING
            ah, al, place = stationary(ph.name, blk)
            if k0 == 0 and not (isinstance(i, int) and ph.use(i, blk) == 0):
                pe.wait_ge(acc_free[pair], 2 * ph.use(i, blk))
            pe.wait_ge(lo_ready, ph.chunk(i, j) + 1)
            for kk in range(size):
                ks = place(k0 + kk)
                for t in range(T):
                    tok = slice(t * P, (t + 1) * P)
                    o = acc[pair][t][:]
                    end = last and kk == size - 1
                    mm(o, al[:, ks, tok], hi[:, slot, kk], start=(k0 + kk == 0), stop=False)
                    mm(o, ah[:, ks, tok], hi[:, slot, kk], start=False, stop=False)
                    ins = mm(o, ah[:, ks, tok], lo[:, slot, kk], start=False, stop=end)
            ins.then_inc(chunk_done, 1)

        def stream(side, ready=None):
            def body(ph, i):
                for j, pos in enumerate(positions(ph)):
                    if ready:
                        ready(i, j)
                    chunk(ph, i, j, pos)
                    side(i, j)
            return body

        nothing = lambda i, j: None

        def split(st, src, ready, n, kts=None):
            bank = tp[n % 2]
            if n >= 2:
                pe.wait_ge(*st.after("dve", f"l{n - 2}"))
            if ready:
                pe.wait_ge(*ready)
            for kk in range(2):
                for t in range(T):
                    ins = tr(bank[:, kk * S + t * P:kk * S + (t + 1) * P], src(t, (2 * n + kk) * P))
            ins.then_inc(*st.mark("pe", f"t{n}"))

        def norm_split(st, src, n):
            split(st, src, st.after("dve", "n1"), n)

        def stepwise(st, src, ready, side):
            for n in range(2):
                split(st, src, ready(n), n)

            def ahead(i, j):
                if i == 0 and j + 2 < BANKS:
                    split(st, src, ready(j + 2), j + 2)
                side(i, j)

            def have(i, j):
                if i == 0 and j < BANKS:
                    pe.wait_ge(*st.after("dve", f"l{j}"))
            return stream(ahead, have)

        pe.wait_ge(in_first, 16 * 2)
        nc.tensor.transpose(sc[0][:, 0:KT], vrow[0:KT, V_NORM[0]], ident[0:KT, 0:KT]).then_inc(*setup.mark("pe", "vn"))

        def vectors(i, j):
            if i == 1 and j == 0:
                pe.wait_ge(in_const, 16 * N_CONST)
                pe.wait_ge(*setup.after("dve", "vn"))
                for g in range(3):
                    ins = nc.tensor.transpose(sc[0][:, g * P:g * P + V_ROWS[g]], vrow[0:V_ROWS[g], g], ident[0:V_ROWS[g], 0:V_ROWS[g]])
                ins.then_inc(*setup.mark("pe", "v"))

        run(pe, "a_proj", stepwise(x_split, lambda t, c: x_in[:, t, c:c + P], lambda n: (in_x[n // 4], 16), vectors))
        end_phase(pe, "a_proj", wait=False)

        def window(i, j):
            if isinstance(i, int) and j == -1:
                pe.wait_ge(*win_prep.after("dve", "kn"))
                for t in range(T):
                    for pair in range(2):
                        ins = tr(tp[0][:, pair * S + t * P:pair * S + (t + 1) * P], a_kn[:, t, pair * P:(pair + 1) * P])
                ins.then_inc(*win_prep.mark("pe", "k"))
            if j == 0:
                if isinstance(i, int):
                    pe.wait_ge(*win_prep.after("act", "k"))
                pe.wait_ge(*win.after("dve", "qn", i))
                for t in range(T):
                    for pair in range(2):
                        ins = tr(tp[0][:, pair * S + t * P:pair * S + (t + 1) * P], a_qn[:, t, 2 * pair:2 * pair + 2, :].rearrange("p h d -> p (h d)"))
                ins.then_inc(*win.mark("pe", "q"))
            if j in (1, 2):
                for g in (2 * j - 2, 2 * j - 1):
                    pe.wait_ge(*win.after("act", "q", i))
                    if g >= 2:
                        pe.wait_ge(*win.after("dve", f"s{g - 2}", i))
                    half = slice(64 * (g % 2), 64 * (g % 2) + 64)
                    o = sc[g % 2]
                    mm(o[:, 0:P], a_qt[half, g // 2, 0:P], a_kt[half, g // 2, 0:P])
                    mm(o[:, P:3 * P], a_qt[half, g // 2, P:S], a_kt[half, g // 2, :]).then_inc(*win.mark("pe", f"s{g}"))
            if 7 <= j < 11:
                g = j - 7
                pe.wait_ge(*win.after("act", f"pt{g}", i))
                v = lambda t: pa[:, t, AW + AKW + g * HD:AW + AKW + (g + 1) * HD]
                mm(sc[0][:, g * HD:(g + 1) * HD], a_pt[:, g % 2, 0], v(0))
                o = sc[0][:, S + g * HD:S + (g + 1) * HD]
                mm(o, a_pt[:, g % 2, 1], v(0), stop=False)
                mm(o, a_pt[:, g % 2, 2], v(1), start=False).then_inc(*win.mark("pe", f"o{g}"))
            if 6 <= j < 10:
                g = j - 6
                pe.wait_ge(*win.after("act", "p", i))
                if g >= 2:
                    pe.wait_ge(*win.after("act", f"pt{g - 2}", i))
                for b in range(3):
                    ins = tr(tp[g % 2][:, b * P:(b + 1) * P], a_s[:, g, b])
                ins.then_inc(*win.mark("pe", f"pt{g}"))

        run(pe, "b_proj", stream(late(window)), first=stream(late(window)))
        end_phase(pe, "b_proj", wait=False)

        def c_side(i, j):
            if j == 0:
                pe.wait_ge(*setup.after("dve", "wl"))
                for t in range(T):
                    for k in range(KT):
                        tok = slice(t * P, (t + 1) * P)
                        o = sc[1][:, t * BH:(t + 1) * BH]
                        mm(o, xl[:, k, tok], wf_hi[:, k], start=(k == 0), stop=False)
                        mm(o, xh[:, k, tok], wf_hi[:, k], start=False, stop=False)
                        ins = mm(o, xh[:, k, tok], wf_lo[:, k], start=False, stop=(k == KT - 1))
                ins.then_inc(*fg_prep.mark("pe", "f"))
            if 4 <= j < 12:
                norm_split(norm_m, lambda t, c: mem_in[t][:, c:c + P], j - 4)
            if j == 13:
                pe.wait_ge(*fg_prep.after("dve", "lf"))
                tri, one = kc[:, K_TRI:K_TRI + P], kc[:, K_ONE:K_ONE + P]
                mm(sc[0][:, 0:BH], tri, logf[:, 0])
                mm(sc[0][:, BH:2 * BH], one, logf[:, 0], stop=False)
                mm(sc[0][:, BH:2 * BH], tri, logf[:, 1], start=False).then_inc(*fg_prep.mark("pe", "c"))
                pe.wait_ge(*norm_m.after("dve", f"l{BANKS - 1}"))
            if j == 15:
                pe.wait_ge(*fg_prep.after("dve", "c"))
                for t in range(T):
                    ins = tr(sc[1][0:BH, t * P:(t + 1) * P], cq[:, t])
                ins.then_inc(*fg_prep.mark("pe", "ct"))
            if 18 <= j < 21:
                split(ua_split, lambda t, c: pa[:, t, AW + 2 * AKW + c:AW + 2 * AKW + c + P], None, j - 18)

        run(pe, "c_proj", stream(c_side))
        end_phase(pe, "c_proj", wait=False)

        def forget(i, j):
            pairs = ((0, P), (1, HD))
            if j == 0:
                for what, src, bank in (("q", b_qn, tp[0]), ("k", b_kn, tp[1])):
                    pe.wait_ge(*fg.after("dve", f"{what}n", i))
                    for n, w in pairs:
                        for t in range(T):
                            ins = tr(bank[0:w, n * S + t * P:n * S + (t + 1) * P], src[:, t].rearrange("p h d -> p (h d)")[:, n * P:n * P + w])
                    ins.then_inc(*fg.mark("pe", what))
            if j in (1, 2):
                for g in ((0, 1) if j == 1 else (2,)):
                    pe.wait_ge(*fg.after("act", "k", i))
                    if g >= 2:
                        pe.wait_ge(*fg.after("dve", f"s{g - 2}", i))
                    half = slice(64 * (g % 2), 64 * (g % 2) + 64)
                    o = sc[g % 2]
                    mm(o[:, 0:P], b_qt[half, g // 2, 0:P], b_kt[half, g // 2, 0:P])
                    mm(o[:, P:3 * P], b_qt[half, g // 2, P:S], b_kt[half, g // 2, :]).then_inc(*fg.mark("pe", f"s{g}"))
            if 7 <= j < 10:
                g = j - 7
                pe.wait_ge(*fg.after("act", f"pt{g}", i))
                v = lambda t: pb[:, t, bass.ds(i * AG * HD + (2 * BW + g * HD), HD)]
                mm(sc[0][:, g * HD:(g + 1) * HD], b_pt[:, g % 2, 0], v(0))
                o = sc[0][:, S + g * HD:S + (g + 1) * HD]
                mm(o, b_pt[:, g % 2, 1], v(0), stop=False)
                mm(o, b_pt[:, g % 2, 2], v(1), start=False).then_inc(*fg.mark("pe", f"o{g}"))
            if 6 <= j < 9:
                g = j - 6
                pe.wait_ge(*fg.after("act", "p", i))
                if g >= 2:
                    pe.wait_ge(*fg.after("act", f"pt{g - 2}", i))
                for b in range(3):
                    ins = tr(tp[g % 2][:, b * P:(b + 1) * P], b_s[:, g, b])
                ins.then_inc(*fg.mark("pe", f"pt{g}"))

        def for_branch(st, src, ready, at_, side):
            def both(i, j):
                if j in at_:
                    for n in (n for n, k in enumerate(at_) if k == j):
                        split(st, src, ready, n)
                side(i, j)

            def have(i, j):
                if j == KT // 2:
                    pe.wait_ge(*st.after("dve", f"l{len(at_) - 1}"))
            return stream(both, have)

        pe.wait_ge(*ua_split.after("dve", "l2"))
        run(pe, "gate_a", stream(late(forget)))
        end_phase(pe, "gate_a", wait=False)

        def memory(i, j):
            if j == 0:
                pe.wait_ge(*me.after("dve", "kn", i))
                for n, src in enumerate((c_qn, c_kn)):
                    for t in range(T):
                        ins = tr(tp[0][:, n * S + t * P:n * S + (t + 1) * P], src[:, t])
                ins.then_inc(*me.mark("pe", "qk"))
            if j == 2:
                pe.wait_ge(*me.after("act", "k", i))
                for t in range(T):
                    ins = mm(sc[0][:, t * S:(t + 1) * S], c_qt[:, t * P:(t + 1) * P], c_kt[:])
                ins.then_inc(*me.mark("pe", "s"))
            if j == 5:
                pe.wait_ge(*me.after("act", "p", i))
                for m in range(T):
                    for t in range(T):
                        ins = tr(tp[1][:, m * S + t * P:m * S + (t + 1) * P], c_p[:, t, m * P:(m + 1) * P])
                ins.then_inc(*me.mark("pe", "pt"))
            if j == 7:
                pe.wait_ge(*me.after("act", "pt", i))
                for t in range(T):
                    for m in range(T):
                        ins = mm(sc[1][:, t * CD:(t + 1) * CD], c_pt[:, m, t * P:(t + 1) * P],
                                 mk1[:, m, bass.ds(i * CD + CW, CD)], start=(m == 0), stop=(m == T - 1))
                ins.then_inc(*me.mark("pe", "o"))

        def memory_first(i, j):
            if j == 1:
                pe.wait_ge(*ub_split.after("dve", "l0"))
            if j == 6:
                pe.wait_ge(*ub_split.after("dve", "l1"))
            memory(i, j - 1)

        run(pe, "gate_b", stream(late(memory)),
            first=for_branch(ub_split, lambda t, c: pb[:, t, 3 * BW + c:3 * BW + c + P], fg.after("dve", "u", D // NB - 1),
                             [0, 0, 4], memory_first))
        end_phase(pe, "gate_b", wait=False)
        run(pe, "gate_c", stream(nothing),
            first=for_branch(uc_split, lambda t, c: pc[:, t, CW + c:CW + c + P], me.after("dve", "u", D // NB - 1), [0, 1], nothing))
        end_phase(pe, "gate_c", wait=False)

        def out_side(i, j):
            if 8 <= j < 16:
                norm_split(norm_m2, lambda t, c: mem2_in[:, t, c:c + P], j - 8)

        run(pe, "out", stepwise(y1_split, lambda t, c: y1[:, t, c:c + P], lambda n: gate_used("gate_c", n // 2), out_side))
        end_phase(pe, "out", wait=False)

        def mem2_side(i, j):
            if 6 <= j < 14:
                norm_split(norm_x1, lambda t, c: x1n[:, t, c:c + P], j - 6)

        run(pe, "mem_kv_2", stream(mem2_side))
        end_phase(pe, "mem_kv_2", wait=False)
        run(pe, "conv_proj", stream(nothing))
        end_phase(pe, "conv_proj", wait=False)
        run(pe, "mq_proj", stream(nothing))
        end_phase(pe, "mq_proj", wait=False)

        def hg_side(i, j):
            if j == 0:
                pe.wait_ge(*conv.after("act", "cb", i))
                pe.wait_ge(*conv.after("dve", "u", i))
                for what, src, bank in (("u", u_st, tp[0]), ("b", cb_st, tp[1])):
                    for n in range(2):
                        for t in range(T):
                            ins = tr(bank[:, n * S + t * P:n * S + (t + 1) * P], src[:, t, n])
                    ins.then_inc(*conv.mark("pe", what))
            if j == 5:
                pe.wait_ge(*conv.after("dve", "y", i))
                for what, src, bank in (("q", d_q, tp[0]), ("k", d_k, tp[1])):
                    pe.wait_ge(*ma.after("act", f"s{what}", i))
                    for n in range(2):
                        for t in range(T):
                            ins = tr(bank[:, n * S + t * P:n * S + (t + 1) * P], src[:, t, n * P:(n + 1) * P])
                    ins.then_inc(*ma.mark("pe", what))
            if j == 7:
                pe.wait_ge(*ma.after("act", "k", i))
                for t in range(T):
                    for n in range(2):
                        ins = mm(sc[0][:, t * S:(t + 1) * S], d_qt[:, n, t * P:(t + 1) * P], d_kt[:, n],
                                 start=(n == 0), stop=(n == 1))
                ins.then_inc(*ma.mark("pe", "s"))
            if j == 10:
                pe.wait_ge(*ma.after("act", "p", i))
                for m in range(T):
                    for t in range(T):
                        ins = tr(tp[0][:, m * S + t * P:m * S + (t + 1) * P], d_p[:, t, m * P:(m + 1) * P])
                ins.then_inc(*ma.mark("pe", "pt"))
            if j == 12:
                pe.wait_ge(*ma.after("act", "pt", i))
                for t in range(T):
                    for m in range(T):
                        ins = mm(sc[1][:, t * MD:(t + 1) * MD], d_pt[:, m, t * P:(t + 1) * P],
                                 mv2[:, m, bass.ds(i * MD, MD)], start=(m == 0), stop=(m == T - 1))
                ins.then_inc(*ma.mark("pe", "o"))

        run(pe, "hg_proj", stream(late(hg_side)))
        end_phase(pe, "hg_proj", wait=False)
        pe.wait_ge(*ma.after("dve", "u", HH // 2 - 1))
        for n in range(8):
            if n >= 2:
                pe.wait_ge(*hg_prep.after("act", f"t{n - 2}"))
            for h in range(2):
                for t in range(T):
                    c = (2 * (n % 4) + h) * HK
                    ins = tr(sc[n % 2][:, h * S + t * P:h * S + (t + 1) * P], hg[:, n // 4, t, c:c + P])
            ins.then_inc(*hg_prep.mark("pe", f"t{n}"))
        end_phase(pe, "hg_prep", wait=False)

        def recur(first):
            def side(i, j):
                it = i + first
                if j == 0:
                    pe.wait_ge(*hp.after("dve", "k", it))
                    for t in range(T):
                        ins = mm(sc[0][:, t * P:(t + 1) * P], h_k[:, t * P:(t + 1) * P],
                                 qt[:, bass.ds(it, 1), t * P:(t + 1) * P].rearrange("p a b -> p (a b)"))
                    ins.then_inc(*hr.mark("pe", "d"))
                if 1 <= j < 8:
                    n = j - 1
                    pe.wait_ge(*hr.after("dve", f"gr{n}", it))
                    if n >= 1:
                        pe.wait_ge(*hr.after("dve", "dg" if n == 1 else f"mk{n - 2}", it))
                    for t in range(T):
                        g = h_g[:, t * P:(t + 1) * P]
                        ins = mm(sc[(n + 1) % 2][:, t * P:(t + 1) * P], g, g)
                    ins.then_inc(*hr.mark("pe", f"s{n}"))
                if j == 8:
                    pe.wait_ge(*hr.after("dve", "gr7", it))
                    pe.wait_ge(*hr.after("dve", "mk5", it))
                    mm(sc[0][:, 0:P], h_g[:, 0:P], h_g[:, P:S]).then_inc(*hr.mark("pe", "s7"))
                if j == 9:
                    pe.wait_ge(*hr.after("act", "off", it))
                    pe.wait_ge(*hr.after("dve", "mk6", it))
                    v = lambda t: hg[:, 2, t, bass.ds(it * HK, HK)]
                    mm(sc[1][:, 0:HK], h_sc[:, 0], v(0))
                    mm(sc[1][:, HK:2 * HK], h_off[:], v(0), stop=False)
                    mm(sc[1][:, HK:2 * HK], h_sc[:, 1], v(1), start=False).then_inc(*hr.mark("pe", "o"))
            return side

        run(pe, "gate_conv", stream(recur(0)))
        end_phase(pe, "gate_conv", wait=False)
        run(pe, "gate_mem", stream(recur(4)), last=stream(recur(4)),
            first=for_branch(ym_split, lambda t, c: mq[:, t, c:c + P], ma.after("dve", "u", HH // 2 - 1), [0, 1, 2, 3], recur(4)))
        end_phase(pe, "gate_mem", wait=False)
        run(pe, "gate_hg", stream(nothing),
            first=for_branch(yb_split, lambda t, c: hg[:, 3, t, c:c + P], hr.after("dve", "u", HH - 1), [0, 1, 2, 3], nothing))
        end_phase(pe, "gate_hg", wait=False)
        run(pe, "out_2", stepwise(y2_split, lambda t, c: y2[:, t, c:c + P], lambda n: gate_used("gate_hg", n // 2), nothing))
        end_phase(pe, "out_2", wait=False)

        def ffn(i, at_, step):
            st, n = ("g", f_g) if step < 2 else ("v", f_v)
            h = step % 2
            pe.wait_ge(*ffs.after("act", "ev", i))
            if step >= 2:
                pe.wait_ge(*ffs.after("dve", f"b{2 * h + 1}2", i))
            for c in range(2):
                for t in range(T):
                    ins = tr(tp[h][:, c * S + t * P:c * S + (t + 1) * P], n[:, t, (2 * h + c) * P:(2 * h + c + 1) * P])
            ins.then_inc(*ffs.mark("pe", f"{st}{h}"))

        def ffn_side(i, j):
            if j in (0, 1):
                ffn(i, j, j)
            if j in (3, 4):
                ffn(i, j, j - 1)

        run(pe, "ffn_first", stepwise(x2_split, lambda t, c: x2[:, t, c:c + P], lambda n: post1.after("dve", f"x{n // 2}"), nothing))
        run(pe, "ffn_up", stream(ffn_side))
        for step in range(4):
            ffn(FT // 4 - 1, 0, step)
        end_phase(pe, "ffn_up", wait=False)
        run(pe, "ffn_down", stream(nothing))

    @block_ctx.scalar
    def _(act):
        def go(o, in_, func=ACT.Copy, **kw):
            return nc.scalar.activation(o, in_, func, **kw)

        def convert(c, slot, size, uses):
            act.wait_ge(loaded[slot], 16 * uses)
            if not (isinstance(c, int) and c < RING):
                act.wait_ge(chunk_done, c - (RING - 1))
            go(hi[:, slot, 0:size], raw[:, slot, 0:size]).then_inc(hi_ready, 1)

        def stream(side, skip_last=False):
            def body(ph, i):
                for j in range(ph.n):
                    c = ph.chunk(i, j + LEAD)
                    if not (skip_last and j + LEAD >= ph.n):
                        slot = (ph.c0 + j + LEAD) % RING
                        size = ph.sizes[j + LEAD] if j + LEAD < ph.n else 2
                        convert(c, slot, size, i * (ph.n // RING) + ((ph.c0 + j + LEAD) // RING + 1))
                    side(i, j)
            return body

        def evacuate(ph, i, blk, dst, scale=None):
            j = max(k for k, p in enumerate(positions(ph)) if p[0] == blk)
            act.wait_ge(chunk_done, ph.chunk(i, j) + 1)
            for t in range(T):
                kw = dict(func=ACT.Identity, scale=scale[:, t:t + 1]) if scale is not None else {}
                go(dst(t), acc[blk % 2][t][:], **kw).then_inc(acc_free[blk % 2], 1)

        def ends(ph, j):
            p = positions(ph)[j]
            return p[0] if p[3] else None

        def split_hi(st, dst, n, gain=None):
            act.wait_ge(*st.after("pe", f"t{n}"))
            for kk in range(2):
                k = 2 * n + kk
                kw = dict(func=ACT.Identity, scale=vcol[:, gain[0], gain[1] + k:gain[1] + k + 1]) if gain else {}
                ins = go(dst(k), tp[n % 2][:, kk * S:(kk + 1) * S], **kw)
            ins.then_inc(*st.mark("act", f"h{n}"))

        def square(st, src, bank, n):
            t, q = n % T, n // T
            if n > 0:
                act.wait_ge(*st.after("act", f"sq{n - 1}"))
            go(bank[:], src(t)[:, q * NB:(q + 1) * NB], ACT.Square, accum_out=ss4[:, t, q:q + 1]).then_inc(*st.mark("act", f"sq{n}"))

        def scales(st, src, bank, r):
            def side(i, j):
                if i == 0 and 3 <= j < 7:
                    for n in (2 * j - 6, 2 * j - 5):
                        square(st, src, bank, n)
                if i == 0 and j == 7:
                    act.wait_ge(*st.after("dve", "e"))
                    go(r[:], r[:], ACT.Sqrt).then_inc(*st.mark("act", "rt"))
                    act.wait_ge(*st.after("dve", "r"))
            return side

        def stepwise(st, dst, gain=None):
            for n in range(2):
                split_hi(st, dst, n, gain)

            def side(i, j):
                if i == 0 and j + 2 < BANKS:
                    split_hi(st, dst, j + 2, gain)
            return side

        def norm_stats(st, src, bank):
            for n in range(4 * T):
                square(st, src, bank, n)
            act.wait_ge(*st.after("dve", "e"))
            go(rn[:], rn[:], ACT.Sqrt).then_inc(*st.mark("act", "rt"))

        def head_root(st, n):
            act.wait_ge(*st.after("dve", "e"))
            go(ssh[:, :, 0:n], ssh[:, :, 0:n], ACT.Sqrt).then_inc(*st.mark("act", "rt"))

        def into(dst, scale):
            def side(i, j):
                blk = ends(ph_of[0], j)
                if blk is not None:
                    evacuate(ph_of[0], i, blk, lambda t: dst(t, i, blk), scale(blk))
            return side

        ph_of = [None]

        def go_phase(name, side=None, dst=None, skip_last=False, peel_first=False, peel_last=False, before=None, scale=lambda b: None):
            ph_of[0] = phases[name]
            both = into(dst, scale) if dst else (lambda i, j: None)

            def all_(i, j):
                if before:
                    before(i, j)
                both(i, j)
                if side:
                    side(i, j)

            body = stream(all_, skip_last)
            run(act, name, body, first=body if peel_first else None, last=body if peel_last else None)

        act.wait_ge(*setup.after("dve", "vn"))
        x_hi = stepwise(x_split, lambda k: xh[:, k], V_NORM)
        for c in range(LEAD):
            convert(c, c, 2, 1)

        def a_side(i, j):
            x_hi(i, j)
            if i == 1 and j == 0:
                act.wait_ge(in_wf, 16)
                go(wf_hi[:], wf_raw[:]).then_inc(*setup.mark("act", "wh"))

        go_phase("a_proj", a_side, lambda t, i, b: pa[:, t, bass.ds(i * 2 * NB + b * NB, NB)],
                 before=scales(x_norm, lambda t: x_in[:, t], sc[1], rnx), scale=lambda b: rnx)
        end_phase(act, "a_proj")

        go(a_sq[:], pa[:, :, 0:AW + AKW], ACT.Square).then_inc(*win_prep.mark("act", "sq"))
        head_root(win_prep, AH + AKV)
        z = pa[:, :, AW + 2 * AKW:A_COLS]
        go(z, z, ACT.Silu).then_inc(*win_prep.mark("act", "silu"))

        def window(i, j):
            if isinstance(i, int) and j == -1:
                act.wait_ge(*win_prep.after("pe", "k"))
                go(a_kt[:].rearrange("p a b -> p (a b)"), tp[0][:]).then_inc(*win_prep.mark("act", "k"))
            if j == 0:
                act.wait_ge(*win.after("pe", "q", i))
                go(a_qt[:].rearrange("p a b -> p (a b)"), tp[0][:], ACT.Identity, scale=gqk[:, 0:1]).then_inc(*win.mark("act", "q"))
            if j == 4:
                act.wait_ge(*win.after("dve", "neg", i))
                for g in G4:
                    for t in range(T):
                        n = 2 * g + t
                        part = a_s[:, g, t:2 * t + 1].rearrange("p b k -> p (b k)")
                        ins = go(part, part, ACT.Exp, bias=nmax[:, n:n + 1], accum_out=den[:, n:n + 1])
                ins.then_inc(*win.mark("act", "p"))
                act.wait_ge(*win.after("dve", "es", i))
                go(es[:], es[:], ACT.Exp).then_inc(*win.mark("act", "es"))
            if 6 <= j < 10:
                g = j - 6
                act.wait_ge(*win.after("pe", f"pt{g}", i))
                if g >= 2:
                    act.wait_ge(*win.after("pe", f"o{g - 2}", i))
                go(a_pt[:, g % 2].rearrange("p b k -> p (b k)"), tp[g % 2][:, 0:3 * P]).then_inc(*win.mark("act", f"pt{g}"))

        go_phase("b_proj", late(window), lambda t, i, b: pb[:, t, bass.ds(i * 2 * NB + b * NB, NB)], scale=lambda b: rnx,
                 peel_first=True)
        end_phase(act, "b_proj")

        def c_dst(t, i, b):
            return (pc if b < 2 else mk1)[:, t, (b % 2) * NB:(b % 2 + 1) * NB]

        def c_side(i, j):
            if j == 0:
                act.wait_ge(in_mem, 32)
                norm_stats(norm_m, lambda t: mem_in[t][:], sc[0])
            if 4 <= j < 12:
                split_hi(norm_m, lambda k: oh[:, k], j - 4, V_MEM)
            if j == 2:
                for t in range(T):
                    if t:
                        act.wait_ge(*fg_prep.after("dve", f"ms{t - 1}"))
                    go(b_sq[:], pb[:, t, 0:2 * BW], ACT.Square).then_inc(*fg_prep.mark("act", f"sq{t}"))
                act.wait_ge(*fg_prep.after("dve", "e"))
                go(ssh[:], ssh[:], ACT.Sqrt).then_inc(*fg_prep.mark("act", "rt"))
            if j == 10:
                zz = pb[:, :, 3 * BW:4 * BW]
                go(zz, zz, ACT.Silu).then_inc(*fg_prep.mark("act", "silu"))
            if j == 12:
                act.wait_ge(*fg_prep.after("dve", "a"))
                go(tf[:], tf[:], ACT.Exp, scale=-1.0).then_inc(*fg_prep.mark("act", "e"))
                act.wait_ge(*fg_prep.after("act", "e"))
                go(tf[:], tf[:], ACT.Ln, bias=1.0).then_inc(*fg_prep.mark("act", "l"))
            if 18 <= j < 21:
                split_hi(ua_split, lambda k: oh[:, 16 + k], j - 18)

        go_phase("c_proj", c_side, c_dst, scale=lambda b: rnx if b < 2 else None)
        end_phase(act, "c_proj")

        def for_branch(st, dst, at_, side, gain=None):
            def both(i, j):
                if isinstance(i, int) and i == 0 and j in at_:
                    for n in (n for n, k in enumerate(at_) if k == j):
                        split_hi(st, dst, n, gain)
                if side:
                    side(i, j)
            return both

        def gate_side(name, more=None):
            gates_before = GATES.index(name) * (D // NB)

            def side(i, j):
                ph = ph_of[0]
                if j == KT // 2 - 1:
                    act.wait_ge(chunk_done, ph.chunk(i, j) + 1)
                    act.wait_ge(sig_free, i * T + (1 + T * gates_before))
                    for t in range(T):
                        kw = dict(scale=rnx[:, t:t + 1]) if name in ("gate_a", "gate_b", "gate_c") else {}
                        go(sig[:, t], acc[0][t][:], ACT.Sigmoid, **kw).then_inc(acc_free[0], 1)
                if more:
                    more(i, j)
            return side

        def forget(i, j):
            if j == 0:
                for what, dst, bank in (("q", b_qt, tp[0]), ("k", b_kt, tp[1])):
                    act.wait_ge(*fg.after("pe", what, i))
                    kw = lambda w: dict(func=ACT.Identity, scale=gqk[0:w, 1:2]) if what == "q" else {}
                    go(dst[:, 0], bank[:, 0:S], **kw(P))
                    go(dst[0:HD, 1], bank[0:HD, S:2 * S], **kw(HD)).then_inc(*fg.mark("act", what))
            if j == 4:
                act.wait_ge(*fg.after("dve", "neg", i))
                for g in G3:
                    for t in range(T):
                        n = 2 * g + t
                        part = b_s[:, g, t:2 * t + 1].rearrange("p b k -> p (b k)")
                        ins = go(part, part, ACT.Exp, bias=nmax[:, n:n + 1], accum_out=den[:, n:n + 1])
                ins.then_inc(*fg.mark("act", "p"))
            if 6 <= j < 9:
                g = j - 6
                act.wait_ge(*fg.after("pe", f"pt{g}", i))
                if g >= 2:
                    act.wait_ge(*fg.after("pe", f"o{g - 2}", i))
                go(b_pt[:, g % 2].rearrange("p b k -> p (b k)"), tp[g % 2][:, 0:3 * P]).then_inc(*fg.mark("act", f"pt{g}"))

        go_phase("gate_a", gate_side("gate_a", late(forget)))
        end_phase(act, "gate_a")
        for n, src in enumerate((pc, mk1)):
            if n:
                act.wait_ge(*me_prep.after("dve", "ms0"))
            go(me_sq[:], src[:, :, 0:CW], ACT.Square).then_inc(*me_prep.mark("act", f"sq{n}"))
        head_root(me_prep, 2 * CH)
        z3 = pc[:, :, CW:2 * CW]
        go(z3, z3, ACT.Silu).then_inc(*me_prep.mark("act", "silu"))

        def memory(i, j):
            if j == 0:
                act.wait_ge(*me.after("pe", "qk", i))
                go(c_qt[:], tp[0][:, 0:S], ACT.Identity, scale=gqk[:, 2:3]).then_inc(*me.mark("act", "q"))
                go(c_kt[:], tp[0][:, S:2 * S]).then_inc(*me.mark("act", "k"))
            if j == 3:
                act.wait_ge(*me.after("dve", "m", i))
                for t in range(T):
                    ins = go(c_p[:, t], sc[0][:, t * S:(t + 1) * S], ACT.Exp, bias=nmax[:, t:t + 1], accum_out=den[:, t:t + 1])
                ins.then_inc(*me.mark("act", "p"))
            if j == 5:
                act.wait_ge(*me.after("pe", "pt", i))
                go(c_pt[:].rearrange("p a b -> p (a b)"), tp[1][:]).then_inc(*me.mark("act", "pt"))

        go_phase("gate_b", gate_side("gate_b", for_branch(ub_split, lambda k: oh[:, k], [0, 0, 4], late(memory))), peel_first=True)
        end_phase(act, "gate_b")
        go_phase("gate_c", gate_side("gate_c", for_branch(uc_split, lambda k: oh[:, 6 + k], [0, 1], None)), peel_first=True)
        end_phase(act, "gate_c", wait=False)
        y1_hi = stepwise(y1_split, lambda k: oh[:, OUT_SLOTS[k]])

        def out_side(i, j):
            y1_hi(i, j)
            if j == 4:
                act.wait_ge(in_mem2, 16)
                norm_stats(norm_m2, lambda t: mem2_in[:, t], sc[0])
            if 8 <= j < 16:
                split_hi(norm_m2, lambda k: m2h[:, k], j - 8, V_MEM2)

        go_phase("out", out_side)
        end_phase(act, "out")

        def mem2_side(i, j):
            if j == 0:
                norm_stats(norm_x1, lambda t: x1[:, t], sc[0])
            if 6 <= j < 14:
                split_hi(norm_x1, lambda k: xh[:, k], j - 6, V_MIX)

        go_phase("mem_kv_2", mem2_side, lambda t, i, b: (mk2 if b < 2 else mv2)[:, t, (b % 2) * NB:(b % 2 + 1) * NB])
        end_phase(act, "mem_kv_2")
        go_phase("conv_proj", dst=lambda t, i, b: cv[:, i, t, b * NB:(b + 1) * NB])
        end_phase(act, "conv_proj")
        go_phase("mq_proj", dst=lambda t, i, b: mq[:, t, b * NB:(b + 1) * NB])
        end_phase(act, "mq_proj")

        def hg_side(i, j):
            if j == -1:
                go(cb_st[:], cv[:, 0, :, bass.ds(i * 2 * P, 2 * P)]).then_inc(*conv.mark("act", "cb"))
            if j == 4:
                act.wait_ge(*conv.after("dve", "y", i))
                for n in range(2):
                    ins = go(oh[:, bass.ds(i * 2 + n, 1)].rearrange("p a b -> p (a b)"), v_tm[:, n])
                ins.then_inc(*conv.mark("act", "h"))
                go(d_q[:], mq[:, :, bass.ds(i * MD, MD)], ACT.Copy, scale=MD ** -0.5).then_inc(*ma.mark("act", "sq"))
                go(d_k[:], mk2[:, :, bass.ds(i * MD, MD)]).then_inc(*ma.mark("act", "sk"))
            if j == 5:
                for what, dst, bank in (("q", d_qt, tp[0]), ("k", d_kt, tp[1])):
                    act.wait_ge(*ma.after("pe", what, i))
                    go(dst[:].rearrange("p a b -> p (a b)"), bank[:]).then_inc(*ma.mark("act", what))
            if j == 8:
                act.wait_ge(*ma.after("dve", "m", i))
                for t in range(T):
                    ins = go(d_p[:, t], sc[0][:, t * S:(t + 1) * S], ACT.Exp, bias=nmax[:, t:t + 1], accum_out=den[:, t:t + 1])
                ins.then_inc(*ma.mark("act", "p"))
            if j == 10:
                act.wait_ge(*ma.after("pe", "pt", i))
                go(d_pt[:].rearrange("p a b -> p (a b)"), tp[0][:]).then_inc(*ma.mark("act", "pt"))

        act.wait_ge(out_x1, 16)
        go_phase("hg_proj", late(hg_side), lambda t, i, b: hg[:, i, t, b * NB:(b + 1) * NB])
        end_phase(act, "hg_proj")
        for n in range(8):
            act.wait_ge(*hg_prep.after("pe", f"t{n}"))
            dst = (qt if n < 4 else zt)[:, 2 * (n % 4):2 * (n % 4) + 2].rearrange("p a b -> p (a b)")
            go(dst, sc[n % 2][:], ACT.Silu if n < 4 else ACT.Copy).then_inc(*hg_prep.mark("act", f"t{n}"))
        go(hg[:, 3], hg[:, 3], ACT.Silu).then_inc(*hg_prep.mark("act", "silu"))
        end_phase(act, "hg_prep")

        def halves(tensor, s):
            v = tensor.rearrange("p (n two s) -> p n two s", two=2, s=s)
            return v[:, :, 0], v[:, :, 1]

        def gates_of(it, j):
            if j == 8:
                act.wait_ge(*hp.after("dve", "a", it))
                go(h_l[:], h_a[:], ACT.Exp, scale=-1.0).then_inc(*hp.mark("act", "e1"))
                act.wait_ge(*hp.after("act", "e1", it))
                go(h_l[:], h_l[:], ACT.Ln, bias=1.0).then_inc(*hp.mark("act", "l1"))
            if j == 9:
                act.wait_ge(*hp.after("dve", "d", it))
                go(h_d[:], h_d[:], ACT.Exp, scale=-1.0).then_inc(*hp.mark("act", "e2"))
                act.wait_ge(*hp.after("act", "e2", it))
                go(h_d[:], h_d[:], ACT.Ln, bias=1.0).then_inc(*hp.mark("act", "l2"))
            if j == 10:
                act.wait_ge(*hp.after("dve", "kz", it))
                go(h_k[:], h_k[:], ACT.Exp).then_inc(*hp.mark("act", "k"))

        def recur(first):
            def side(i, j):
                it = i + first
                if j < 8:
                    n = j
                    s = (LEVELS + [P])[n]
                    e, pre, suf = halves(h_e[:], s), halves(h_pre[:], s), halves(h_suf[:], s)
                    if n == 0:
                        act.wait_ge(*hp.after("dve", "lf0", it))
                    else:
                        act.wait_ge(*hr.after("dve", f"pre{n - 1}", it))
                    go(e[0], suf[0], ACT.Exp).then_inc(*hr.mark("act", f"el{n}"))
                    go(e[1], pre[1], ACT.Exp).then_inc(*hr.mark("act", f"er{n}"))
                if j == 8:
                    act.wait_ge(*hr.after("pe", "s7", it))
                    go(h_off[:], sc[0][:, 0:P]).then_inc(*hr.mark("act", "off"))
                if j == 9:
                    act.wait_ge(*hr.after("pe", "o", it))
                    for t in range(T):
                        go(h_e[:, 0:HK], sc[1][:, t * HK:(t + 1) * HK], ACT.Square, accum_out=ssk[:, t:t + 1]).then_inc(*hr.mark("act", f"sq{t}"))
                        act.wait_ge(*hr.after("act", f"sq{t}", it))
                    act.wait_ge(*hr.after("dve", "e", it))
                    go(ssk[:, 0:T], ssk[:, 0:T], ACT.Sqrt).then_inc(*hr.mark("act", "rt"))
                if not (isinstance(it, int) and it == HH - 1):
                    gates_of(it + 1, j)
            return side

        for j in range(8, 11):
            gates_of(0, j)
        go_phase("gate_conv", gate_side("gate_conv", recur(0)))
        end_phase(act, "gate_conv")
        go_phase("gate_mem", gate_side("gate_mem", for_branch(ym_split, lambda k: oh[:, 16 + k], [0, 1, 2, 3], recur(4))),
                 peel_first=True, peel_last=True)
        end_phase(act, "gate_mem")
        go_phase("gate_hg", gate_side("gate_hg", for_branch(yb_split, lambda k: oh[:, 8 + k], [0, 1, 2, 3], None, V_HG)), peel_first=True)
        end_phase(act, "gate_hg", wait=False)
        y2_hi = stepwise(y2_split, lambda k: oh[:, OUT2_SLOTS[k]])

        def keep(st, dst):
            def side(i, j):
                ph = ph_of[0]
                blk = ends(ph, j)
                if blk is None:
                    return
                act.wait_ge(chunk_done, ph.chunk(i, j) + 1)
                if i or blk:
                    last = (i, blk - 1) if blk else (i - 1, ph.blocks - 1)
                    act.wait_ge(acc_free[last[1] % 2], 2 * ph.use(*last) + T)
                for t in range(T):
                    col = i * 2 + blk
                    go(dst[:, t, bass.ds(col * NB, NB)], acc[blk % 2][t][:]).then_inc(*st.mark("act", f"m{col}{t}"))
                    if t:
                        act.wait_ge(acc_free[blk % 2], 2 * ph.use(i, blk) + t)
                    go(sc[0][:], acc[blk % 2][t][:], ACT.Square, accum_out=ss4[:, t, bass.ds(col, 1)]).then_inc(acc_free[blk % 2], 1)
            return side

        go_phase("out_2", keep(mixs, mix), before=y2_hi)
        act.wait_ge(*post1.after("dve", "e"))
        go(rn[:], rn[:], ACT.Sqrt).then_inc(*post1.mark("act", "rt"))
        x2_hi = stepwise(x2_split, lambda k: xh[:, k], V_FFN)
        x2_scales = scales(x2_norm, lambda t: x2[:, t], sc[0], rnf)
        end_phase(act, "out_2", wait=False)

        def ffn_ev(i, blk, ph):
            act.wait_ge(chunk_done, ph.chunk(i, KT // 2 * (blk + 1) - 1) + 1)
            for t in range(T):
                go((f_g, f_v)[blk][:, t], acc[blk][t][:], ACT.Identity, scale=rnf[:, t:t + 1]).then_inc(acc_free[blk], 1)

        def ffn_up(first, ph):
            def side(i, j):
                if not first:
                    x2_scales(i, j)
                    x2_hi(i, j)
                if first and j == 3:
                    ffn_act(i)
                if first and j == 6:
                    ffn_hi(i)
                if j == 7:
                    ffn_ev(i, 0, ph)
                if j == 15:
                    ffn_ev(i, 1, ph)
                    act.drain().then_inc(*ffs.mark("act", "ev"))
            return side

        def ffn_act(i):
            act.wait_ge(*ffs.after("dve", "b32", i))
            for c in range(4):
                ins = go(f_a[:, c], f_c[:, c], ACT.Gelu_apprx_tanh, bias=vcol[:, V_FB[0], bass.ds(i * 4 + (V_FB[1] + c), 1)])
            ins.then_inc(*ffs.mark("act", "gelu"))

        def ffn_hi(i):
            act.wait_ge(*ffs.after("dve", "y", i))
            go(fh[:, bass.ds(i * 4, 4)], f_a[:]).then_inc(*ffs.mark("act", "h"))

        run(act, "ffn_first", stream(ffn_up(0, phases["ffn_first"])))
        act.wait_ge(out_x2, 16)
        run(act, "ffn_up", stream(ffn_up(1, phases["ffn_up"])))
        ffn_act(FT // 4 - 1)
        ffn_hi(FT // 4 - 1)
        end_phase(act, "ffn_up")
        ph_of[0] = ph = phases["ffn_down"]
        k = keep(ffe, ff)
        stream(k)(ph, 0)
        stream(k, skip_last=True)(ph, 1)
        act.wait_ge(*post2.after("dve", "e"))
        go(rn[:], rn[:], ACT.Sqrt).then_inc(*post2.mark("act", "rt"))

    @block_ctx.vector
    def _(dve):
        v = nc.vector

        def convert(c, slot, size):
            dve.wait_ge(hi_ready, c + 1)
            v.tensor_tensor(lo[:, slot, 0:size], raw[:, slot, 0:size], hi[:, slot, 0:size].bitcast(F32),
                            ALU.subtract).then_inc(lo_ready, 1)

        def stream(side, skip_last=False):
            def body(ph, i):
                for j in range(ph.n):
                    if not (skip_last and j + LEAD >= ph.n):
                        size = ph.sizes[j + LEAD] if j + LEAD < ph.n else 2
                        convert(ph.chunk(i, j + LEAD), (ph.c0 + j + LEAD) % RING, size)
                    side(i, j)
            return body

        nothing = lambda i, j: None

        def split_lo(st, dst, hi_of, n, gain=None):
            dve.wait_ge(*st.after("act", f"h{n}"))
            for kk in range(2):
                k = 2 * n + kk
                src, h = tp[n % 2][:, kk * S:(kk + 1) * S], hi_of(k).bitcast(F32)
                if gain:
                    g = vcol[:, gain[0], gain[1] + k:gain[1] + k + 1]
                    ins = v.scalar_tensor_tensor(dst(k), src, g, h, ALU.mult, ALU.subtract)
                else:
                    ins = v.tensor_tensor(dst(k), src, h, ALU.subtract)
            ins.then_inc(*st.mark("dve", f"l{n}"))

        def root_mean(st, part, n, mean):
            v.tensor_scalar(part, part, 1.0 / mean, EPS, ALU.mult, ALU.add).then_inc(*st.mark("dve", "e"))
            dve.wait_ge(*st.after("act", "rt"))
            v.reciprocal(part, part).then_inc(*st.mark("dve", "r"))

        def norm_rest(st, src, dst):
            dve.wait_ge(*st.after("act", f"sq{4 * T - 1}"))
            v.tensor_reduce(rn[:], ss4[:], AX, ALU.add).then_inc(*st.mark("dve", "ms"))
            dve.wait_ge(*st.after("dve", "ms"))
            root_mean(st, rn[:], T, D)
            dve.wait_ge(*st.after("dve", "r"))
            for t in range(T):
                v.tensor_scalar(dst(t), src(t), rn[:, t:t + 1], None, ALU.mult).then_inc(*st.mark("dve", f"n{t}"))

        def over(ap, shape):
            return ap.unsqueeze(len(ap.shape)).to_broadcast(shape)

        def scales(st, r):
            def side(i, j):
                if i == 0 and j == 6:
                    dve.wait_ge(*st.after("act", f"sq{4 * T - 1}"))
                    v.tensor_reduce(r[:], ss4[:], AX, ALU.add).then_inc(*st.mark("dve", "ms"))
                    dve.wait_ge(*st.after("dve", "ms"))
                    v.tensor_scalar(r[:], r[:], 1.0 / D, EPS, ALU.mult, ALU.add).then_inc(*st.mark("dve", "e"))
                if i == 0 and j == 7:
                    dve.wait_ge(*st.after("act", "rt"))
                    v.reciprocal(r[:], r[:]).then_inc(*st.mark("dve", "r"))
            return side

        def stepwise(st, dst, hi_of, gain=None):
            for n in range(2):
                split_lo(st, dst, hi_of, n, gain)

            def side(i, j):
                if i == 0 and j + 2 < BANKS:
                    split_lo(st, dst, hi_of, j + 2, gain)
            return side

        dve.wait_ge(*setup.after("pe", "vn"))
        v.tensor_copy(vcol[:, V_NORM[0], 0:KT], sc[0][:, 0:KT]).then_inc(*setup.mark("dve", "vn"))
        x_lo = stepwise(x_split, lambda k: xl[:, k], lambda k: xh[:, k], V_NORM)
        x_scales = scales(x_norm, rnx)
        for c in range(LEAD):
            convert(c, c, 2)

        def a_side(i, j):
            x_lo(i, j)
            x_scales(i, j)
            if i == 1 and j == 1:
                vectors()

        def vectors():
            dve.wait_ge(*setup.after("pe", "v"))
            for g in range(3):
                ins = v.tensor_copy(vcol[:, g, 0:V_ROWS[g]], sc[0][:, g * P:g * P + V_ROWS[g]])
            ins.then_inc(*setup.mark("dve", "v"))
            dve.wait_ge(*setup.after("dve", "v"))
            v.tensor_tensor(gqk[:], vcol[:, 1, V_QK:V_QK + 6:2], vcol[:, 1, V_QK + 1:V_QK + 6:2], ALU.mult).then_inc(*setup.mark("dve", "qk0"))
            dve.wait_ge(*setup.after("dve", "qk0"))
            v.tensor_scalar(gqk[:, 0:2], gqk[:, 0:2], HD ** -0.5, None, ALU.mult)
            v.tensor_scalar(gqk[:, 2:3], gqk[:, 2:3], CD ** -0.5, None, ALU.mult).then_inc(*setup.mark("dve", "qk1"))
            dve.wait_ge(*setup.after("act", "wh"))
            v.tensor_tensor(wf_lo[:], wf_raw[:], wf_hi[:].bitcast(F32), ALU.subtract).then_inc(*setup.mark("dve", "wl"))
            dve.wait_ge(in_const, 16 * N_CONST)
            v.tensor_copy(lmask[:], lmask_in[:]).then_inc(sig_free, 1)

        run(dve, "a_proj", stream(a_side))
        end_phase(dve, "a_proj")

        dve.wait_ge(*win_prep.after("act", "sq"))
        heads = ssh[:, :, 0:AH + AKV]
        v.tensor_reduce(heads, a_sq[:].rearrange("p t (h d) -> p t h d", d=HD), AX, ALU.add).then_inc(*win_prep.mark("dve", "ms"))
        dve.wait_ge(*win_prep.after("dve", "ms"))
        root_mean(win_prep, heads, AH + AKV, HD)
        dve.wait_ge(*win_prep.after("dve", "r"))
        v.tensor_tensor(a_kn[:].rearrange("p t (h d) -> p t h d", d=HD),
                        pa[:, :, AW:AW + AKW].rearrange("p t (h d) -> p t h d", d=HD),
                        over(ssh[:, :, AH:AH + AKV], [P, T, AKV, HD]), ALU.mult).then_inc(*win_prep.mark("dve", "kn"))

        def window(i, j):
            by_g = lambda ap, n: ap.rearrange("p t (g n d) -> p t g n d", n=AG, d=n)[:, :, :, i, :]
            if j == -1:
                r = ssh[:, :, 0:AH].rearrange("p t (g n) -> p t g n", n=AG)[:, :, :, i]
                v.tensor_tensor(a_qn[:], by_g(pa[:, :, 0:AW], HD), over(r, [P, T, AKV, HD]), ALU.mult).then_inc(*win.mark("dve", "qn"))
            if j in (1, 2):
                for g in (2 * j - 2, 2 * j - 1):
                    dve.wait_ge(*win.after("pe", f"s{g}", i))
                    v.scalar_tensor_tensor(a_s[:, g].rearrange("p b k -> p (b k)"), kc[:, K_REL:K_REL + 3 * P],
                                           kc[:, bass.ds(i + (K_SLOPE + AG * g), 1)], sc[g % 2][:, 0:3 * P],
                                           ALU.mult, ALU.add).then_inc(*win.mark("dve", f"s{g}"))
            if j == 3:
                dve.wait_ge(*win.after("dve", "s3", i))
                v.tensor_reduce(m3[:], a_s[:].rearrange("p g b k -> p (g b) k"), AX, ALU.max).then_inc(*win.mark("dve", "m3"))
                dve.wait_ge(*win.after("dve", "m3", i))
                v.tensor_tensor(mm[:], m3[:, 1:12:3], m3[:, 2:12:3], ALU.max).then_inc(*win.mark("dve", "mm"))
                sink = sinks[:].rearrange("p (g n) -> p g n", n=AG)[:, :, i]
                v.tensor_tensor(nmax[:, 0:8:2], m3[:, 0:12:3], sink, ALU.max).then_inc(*win.mark("dve", "n0"))
                dve.wait_ge(*win.after("dve", "mm", i))
                v.tensor_tensor(nmax[:, 1:8:2], mm[:], sink, ALU.max).then_inc(*win.mark("dve", "n1"))
                dve.wait_ge(*win.after("dve", "n1", i))
                v.tensor_scalar(nmax[:], nmax[:], -1.0, None, ALU.mult).then_inc(*win.mark("dve", "neg"))
                dve.wait_ge(*win.after("dve", "neg", i))
                v.tensor_tensor(es[:].rearrange("p (g t) -> p g t", t=T), nmax[:].rearrange("p (g t) -> p g t", t=T),
                                over(sink, [P, AKV, T]), ALU.add).then_inc(*win.mark("dve", "es"))
            if j == 4:
                dve.wait_ge(*win.after("act", "es", i))
                v.tensor_tensor(den[:], den[:], es[:], ALU.add).then_inc(*win.mark("dve", "den"))
                dve.wait_ge(*win.after("dve", "den", i))
                v.reciprocal(rden[:], den[:]).then_inc(*win.mark("dve", "rd"))
            if j == 11:
                dve.wait_ge(*win.after("pe", "o3", i))
                r = rden[:].rearrange("p (g t) -> p t g", t=T)
                v.tensor_tensor(a_o[:], sc[0][:].rearrange("p (t g d) -> p t g d", t=T, g=AKV), over(r, [P, T, AKV, HD]),
                                ALU.mult).then_inc(*win.mark("dve", "on"))
                dve.wait_ge(*win.after("dve", "on", i))
                z = by_g(pa[:, :, AW + 2 * AKW:A_COLS], HD)
                v.tensor_tensor(z, a_o[:], z, ALU.mult).then_inc(*win.mark("dve", "u"))

        run(dve, "b_proj", stream(late(window)))
        end_phase(dve, "b_proj")

        def c_side(i, j):
            if j == 0:
                norm_rest(norm_m, lambda t: mem_in[t][:], lambda t: mem_in[t][:])
            if 4 <= j < 12:
                split_lo(norm_m, lambda k: ol[:, k], lambda k: oh[:, k], j - 4, V_MEM)
            if j == 2:
                for t in range(T):
                    dve.wait_ge(*fg_prep.after("act", f"sq{t}"))
                    v.tensor_reduce(ssh[:, t], b_sq[:].rearrange("p (h d) -> p h d", d=HD), AX, ALU.add).then_inc(*fg_prep.mark("dve", f"ms{t}"))
                dve.wait_ge(*fg_prep.after("dve", "ms1"))
                root_mean(fg_prep, ssh[:], 2 * BH, HD)
                dve.wait_ge(*fg_prep.after("pe", "f"))
                for t in range(T):
                    ins = v.scalar_tensor_tensor(logf[:, t], sc[1][:, t * BH:(t + 1) * BH], rnx[:, t:t + 1], bfor[:], ALU.mult, ALU.add)
                ins.then_inc(*fg_prep.mark("dve", "z"))
                dve.wait_ge(*fg_prep.after("dve", "z"))
                v.scalar_tensor_tensor(tf[:], logf[:], -1.0, logf[:], ALU.mult, ALU.max).then_inc(*fg_prep.mark("dve", "a"))
            if j == 12:
                dve.wait_ge(*fg_prep.after("act", "l"))
                v.scalar_tensor_tensor(logf[:], logf[:], 0.0, tf[:], ALU.min, ALU.subtract).then_inc(*fg_prep.mark("dve", "lf"))
            if j == 14:
                dve.wait_ge(*fg_prep.after("pe", "c"))
                v.tensor_copy(cq[:].rearrange("p t h -> p (t h)"), sc[0][:, 0:T * BH]).then_inc(*fg_prep.mark("dve", "c"))
            if j == 16:
                dve.wait_ge(*fg_prep.after("pe", "ct"))
                v.tensor_scalar(ct[0:BH], sc[1][0:BH, 0:S], -1.0, None, ALU.mult).then_inc(*fg_prep.mark("dve", "ct"))
            if 18 <= j < 21:
                split_lo(ua_split, lambda k: ol[:, 16 + k], lambda k: oh[:, 16 + k], j - 18)

        run(dve, "c_proj", stream(c_side))
        end_phase(dve, "c_proj")

        def for_branch(st, dst, hi_of, at_, side, gain=None):
            def both(i, j):
                if isinstance(i, int) and i == 0 and j in at_:
                    for n in (n for n, k in enumerate(at_) if k == j):
                        split_lo(st, dst, hi_of, n, gain)
                if side:
                    side(i, j)
            return both

        def gate_side(ph, y, first, more=None):
            def side(i, j):
                if more:
                    more(i, j)
                if j != ph.n - 1:
                    return
                dve.wait_ge(acc_free[0], 2 * ph.use(i, 0) + T)
                dve.wait_ge(chunk_done, ph.chunk(i, j) + 1)
                for t in range(T):
                    v.tensor_tensor(sig[:, t], sig[:, t], acc[1][t][:], ALU.mult).then_inc(acc_free[1], 1)
                for t in range(T):
                    dve.wait_ge(acc_free[1], 2 * ph.use(i, 1) + t + 1)
                    col = y[:, t, bass.ds(i * NB, NB)]
                    if first:
                        v.tensor_copy(col, sig[:, t]).then_inc(sig_free, 1)
                    else:
                        v.tensor_tensor(col, col, sig[:, t], ALU.add).then_inc(sig_free, 1)
            return side

        def forget(i, j):
            if j == -1:
                for what, dst, col, h0 in (("qn", b_qn, 0, 0), ("kn", b_kn, BW, BH)):
                    src = pb[:, :, bass.ds(i * AG * HD + col, AG * HD)].rearrange("p t (h d) -> p t h d", d=HD)
                    v.tensor_tensor(dst[:], src, over(ssh[:, :, bass.ds(i * AG + h0, AG)], [P, T, AG, HD]), ALU.mult).then_inc(*fg.mark("dve", what))
            if j in (1, 2):
                dve.wait_ge(in_nck, 16)
                for g in ((0, 1) if j == 1 else (2,)):
                    dve.wait_ge(*fg.after("pe", f"s{g}", i))
                    h = bass.ds(i * AG + g, 1)
                    flat = lambda ap: ap.rearrange("p a b -> p (a b)")
                    v.scalar_tensor_tensor(b_s[:, g, 0], sc[g % 2][:, 0:P], cq[:, 0, h], flat(nck[:, h, 0:P]), ALU.add, ALU.add)
                    v.scalar_tensor_tensor(flat(b_s[:, g, 1:3]), sc[g % 2][:, P:3 * P], cq[:, 1, h], flat(nck[:, h, :]),
                                           ALU.add, ALU.add).then_inc(*fg.mark("dve", f"s{g}"))
            if j == 3:
                dve.wait_ge(*fg.after("dve", "s2", i))
                own = b_s[:, :, 0:3:2, :]
                mask = kc[:, K_MASK:K_MASK + P].unsqueeze(1).unsqueeze(1).to_broadcast([P, AG, 2, P])
                v.tensor_tensor(own, own, mask, ALU.add).then_inc(*fg.mark("dve", "mask"))
                dve.wait_ge(*fg.after("dve", "mask", i))
                v.tensor_reduce(m3[:, 0:9], b_s[:].rearrange("p g b k -> p (g b) k"), AX, ALU.max).then_inc(*fg.mark("dve", "m3"))
                dve.wait_ge(*fg.after("dve", "m3", i))
                v.tensor_tensor(mm[:, 0:3], m3[:, 1:9:3], m3[:, 2:9:3], ALU.max).then_inc(*fg.mark("dve", "mm"))
                v.tensor_scalar(nmax[:, 0:6:2], m3[:, 0:9:3], -1.0, None, ALU.mult).then_inc(*fg.mark("dve", "n0"))
                dve.wait_ge(*fg.after("dve", "mm", i))
                v.tensor_scalar(nmax[:, 1:6:2], mm[:, 0:3], -1.0, None, ALU.mult).then_inc(*fg.mark("dve", "neg"))
            if j == 5:
                dve.wait_ge(*fg.after("act", "p", i))
                v.reciprocal(rden[:, 0:6], den[:, 0:6]).then_inc(*fg.mark("dve", "rd"))
            if j == 10:
                dve.wait_ge(*fg.after("pe", "o2", i))
                dve.wait_ge(*fg.after("dve", "rd", i))
                o = sc[0][:].rearrange("p (t c) -> p t c", t=T)[:, :, 0:AG * HD].rearrange("p t (g d) -> p t g d", d=HD)
                r = rden[:, 0:6].rearrange("p (g t) -> p t g", t=T)
                v.tensor_tensor(b_o[:], o, over(r, [P, T, AG, HD]), ALU.mult).then_inc(*fg.mark("dve", "on"))
                dve.wait_ge(*fg.after("dve", "on", i))
                z = pb[:, :, bass.ds(i * AG * HD + 3 * BW, AG * HD)].rearrange("p t (h d) -> p t h d", d=HD)
                v.tensor_tensor(z, b_o[:], z, ALU.mult).then_inc(*fg.mark("dve", "u"))

        run(dve, "gate_a", stream(gate_side(phases["gate_a"], y1, True, late(forget))))
        end_phase(dve, "gate_a")
        for n in range(2):
            dve.wait_ge(*me_prep.after("act", f"sq{n}"))
            v.tensor_reduce(ssh[:, :, n * CH:(n + 1) * CH], me_sq[:].rearrange("p t (h d) -> p t h d", d=CD), AX, ALU.add).then_inc(*me_prep.mark("dve", f"ms{n}"))
        dve.wait_ge(*me_prep.after("dve", "ms1"))
        root_mean(me_prep, ssh[:, :, 0:2 * CH], 2 * CH, CD)

        def memory(i, j):
            if j == -1:
                dve.wait_ge(*me_prep.after("dve", "r"))
                for what, dst, src, h0 in (("qn", c_qn, pc, 0), ("kn", c_kn, mk1, CH)):
                    r = ssh[:, :, bass.ds(i + h0, 1)].to_broadcast([P, T, CD])
                    v.tensor_tensor(dst[:], src[:, :, bass.ds(i * CD, CD)], r, ALU.mult).then_inc(*me.mark("dve", what))
            if j == 2:
                dve.wait_ge(*me.after("pe", "s", i))
                v.tensor_reduce(nmax[:, 0:T], sc[0][:].rearrange("p (t m) -> p t m", t=T), AX, ALU.max, negate=True).then_inc(*me.mark("dve", "m"))
            if j == 4:
                dve.wait_ge(*me.after("act", "p", i))
                v.reciprocal(rden[:, 0:T], den[:, 0:T]).then_inc(*me.mark("dve", "rd"))
            if j == 7:
                dve.wait_ge(*me.after("pe", "o", i))
                dve.wait_ge(*me.after("dve", "rd", i))
                o = sc[1][:, 0:T * CD].rearrange("p (t d) -> p t d", t=T)
                v.tensor_tensor(c_qn[:], o, over(rden[:, 0:T], [P, T, CD]), ALU.mult).then_inc(*me.mark("dve", "on"))
                dve.wait_ge(*me.after("dve", "on", i))
                z = pc[:, :, bass.ds(i * CD + CW, CD)]
                v.tensor_tensor(z, c_qn[:], z, ALU.mult).then_inc(*me.mark("dve", "u"))

        body = stream(gate_side(phases["gate_b"], y1, False, for_branch(
            ub_split, lambda k: ol[:, k], lambda k: oh[:, k], [0, 0, 4], late(memory))))
        run(dve, "gate_b", body, first=body)
        end_phase(dve, "gate_b")
        body = stream(gate_side(phases["gate_c"], y1, False, for_branch(
            uc_split, lambda k: ol[:, 6 + k], lambda k: oh[:, 6 + k], [0, 1], None)))
        run(dve, "gate_c", body, first=body)
        end_phase(dve, "gate_c", wait=False)
        y1_lo = stepwise(y1_split, lambda k: ol[:, OUT_SLOTS[k]], lambda k: oh[:, OUT_SLOTS[k]])

        def out_side(i, j):
            ph = phases["out"]
            y1_lo(i, j)
            if j == 4:
                norm_rest(norm_m2, lambda t: mem2_in[:, t], lambda t: mem2_in[:, t])
            if 8 <= j < 16:
                split_lo(norm_m2, lambda k: m2l[:, k], lambda k: m2h[:, k], j - 8, V_MEM2)
            blk, _, _, last = positions(ph)[j]
            if last:
                dve.wait_ge(in_x_again, 16)
                dve.wait_ge(chunk_done, ph.chunk(i, j) + 1)
                for t in range(T):
                    cols = slice(blk * NB, (blk + 1) * NB)
                    v.tensor_tensor(x1[:, t, cols], acc[blk % 2][t][:], x_again[:, t, cols], ALU.add).then_inc(acc_free[blk % 2], 1)
                dve.drain().then_inc(*out1.mark("dve", f"x{blk}"))

        run(dve, "out", stream(out_side))
        end_phase(dve, "out")

        def mem2_side(i, j):
            if j == 0:
                norm_rest(norm_x1, lambda t: x1[:, t], lambda t: x1n[:, t])
            if 6 <= j < 14:
                split_lo(norm_x1, lambda k: xl[:, k], lambda k: xh[:, k], j - 6, V_MIX)

        run(dve, "mem_kv_2", stream(mem2_side))
        end_phase(dve, "mem_kv_2")
        run(dve, "conv_proj", stream(nothing))
        end_phase(dve, "conv_proj")
        run(dve, "mq_proj", stream(nothing))
        end_phase(dve, "mq_proj")

        def hg_side(i, j):
            if j == -1:
                part = lambda n: cv[:, n, :, bass.ds(i * 2 * P, 2 * P)]
                v.tensor_tensor(u_st[:].rearrange("p t a b -> p t (a b)"), part(1), part(2), ALU.mult).then_inc(*conv.mark("dve", "u"))
            if j == 1:
                dve.wait_ge(*conv.after("pe", "u", i))
                w = lambda k, n: vcol[:, V_CONV[0], bass.ds(i * 2 + (V_CONV[1] + 8 * k + n), 1)]
                u = lambda n: tp[0][:, n * S:(n + 1) * S]
                for n in range(2):
                    ins = v.tensor_scalar(v_tm[:, n], u(n), w(2, n), None, ALU.mult)
                ins.then_inc(*conv.mark("dve", "c0"))
                for back in (1, 2):
                    dve.wait_ge(*conv.after("dve", f"c{back - 1}", i))
                    for n in range(2):
                        ins = v.scalar_tensor_tensor(v_tm[:, n, back:S], u(n)[:, 0:S - back], w(2 - back, n), v_tm[:, n, back:S], ALU.mult, ALU.add)
                    ins.then_inc(*conv.mark("dve", f"c{back}"))
                dve.wait_ge(*conv.after("pe", "b", i))
                dve.wait_ge(*conv.after("dve", "c2", i))
                flat = v_tm[:].rearrange("p a b -> p (a b)")
                v.tensor_tensor(flat, flat, tp[1][:], ALU.mult).then_inc(*conv.mark("dve", "y"))
            if j == 4:
                dve.wait_ge(*conv.after("act", "h", i))
                k = bass.ds(i * 2, 2)
                v.tensor_tensor(ol[:, k], v_tm[:], oh[:, k].bitcast(F32), ALU.subtract).then_inc(*conv.mark("dve", "l"))
            if j == 7:
                dve.wait_ge(*ma.after("pe", "s", i))
                v.tensor_reduce(nmax[:, 0:T], sc[0][:].rearrange("p (t m) -> p t m", t=T), AX, ALU.max, negate=True).then_inc(*ma.mark("dve", "m"))
            if j == 9:
                dve.wait_ge(*ma.after("act", "p", i))
                v.reciprocal(rden[:, 0:T], den[:, 0:T]).then_inc(*ma.mark("dve", "rd"))
            if j == 12:
                dve.wait_ge(*ma.after("pe", "o", i))
                dve.wait_ge(*ma.after("dve", "rd", i))
                v.tensor_tensor(mq[:, :, bass.ds(i * MD, MD)], sc[1][:].rearrange("p (t d) -> p t d", t=T),
                                over(rden[:, 0:T], [P, T, MD]), ALU.mult).then_inc(*ma.mark("dve", "u"))

        run(dve, "hg_proj", stream(late(hg_side)))
        end_phase(dve, "hg_proj")
        end_phase(dve, "hg_prep")

        def halves(tensor, s):
            w = tensor.rearrange("p (n two s) -> p n two s", two=2, s=s)
            return w[:, :, 0], w[:, :, 1]

        def gates_of(it, j):
            z = zt[:, bass.ds(it, 1)].rearrange("p a b -> p (a b)")
            if j == 8:
                v.scalar_tensor_tensor(h_a[:], z, -1.0, z, ALU.mult, ALU.max).then_inc(*hp.mark("dve", "a"))
            if j == 9:
                dve.wait_ge(*hp.after("act", "l1", it))
                v.scalar_tensor_tensor(h_ls[:], z, 0.0, h_l[:], ALU.min, ALU.subtract).then_inc(*hp.mark("dve", "ls"))
                dve.wait_ge(*hp.after("dve", "ls", it))
                v.tensor_scalar(h_d[:], h_ls[:], LOG_TINY, None, ALU.subtract).then_inc(*hp.mark("dve", "d0"))
                dve.wait_ge(*hp.after("dve", "d0", it))
                v.scalar_tensor_tensor(h_d[:], h_d[:], -1.0, h_d[:], ALU.mult, ALU.max).then_inc(*hp.mark("dve", "d"))
            if j == 10:
                dve.wait_ge(*hp.after("act", "l2", it))
                v.scalar_tensor_tensor(h_pre[:], h_ls[:], LOG_TINY, h_d[:], ALU.max, ALU.add).then_inc(*hp.mark("dve", "lf"))
                dve.wait_ge(*hp.after("dve", "lf", it))
                v.memset(h_suf[:], 0.0)
                v.tensor_scalar(h_pre[:], h_pre[:], 0.0, None, ALU.min).then_inc(*hp.mark("dve", "lf0"))
                v.tensor_tensor(h_k[:], h_ls[:], z, ALU.subtract).then_inc(*hp.mark("dve", "kz"))
            if j == 11:
                dve.wait_ge(*hp.after("act", "k", it))
                v.tensor_scalar(h_k[:], h_k[:], 1e-30, HK ** -0.5, ALU.subtract, ALU.mult).then_inc(*hp.mark("dve", "k"))

        def recur(first):
            def side(i, j):
                it = i + first
                q = qt[:, bass.ds(it, 1)].rearrange("p a b -> p (a b)")
                if j == 0:
                    dve.wait_ge(*hr.after("pe", "d", it))
                    v.tensor_tensor(h_sc[:], sc[0][:, 0:T * P].rearrange("p (t k) -> p t k", t=T),
                                    ident.unsqueeze(1).to_broadcast([P, T, P]), ALU.mult).then_inc(*hr.mark("dve", "dg"))
                if j < 8:
                    n = j
                    s = (LEVELS + [P])[n]
                    e, g, pre, suf = (halves(w[:], s) for w in (h_e, h_g, h_pre, h_suf))
                    dve.wait_ge(*hr.after("act", f"el{n}", it))
                    if n >= 1:
                        dve.wait_ge(*hr.after("pe", f"s{n - 1}", it))
                    if n == len(LEVELS):
                        dve.wait_ge(*hr.after("dve", f"mk{n - 2}", it))
                    v.tensor_tensor(g[0], e[0], halves(h_k[:], s)[0], ALU.mult).then_inc(*hr.mark("dve", f"gl{n}"))
                    dve.wait_ge(*hr.after("act", f"er{n}", it))
                    v.tensor_tensor(g[1], e[1], halves(q, s)[1], ALU.mult).then_inc(*hr.mark("dve", f"gr{n}"))
                    if n < len(LEVELS):
                        shape = [P, S // (2 * s), s]
                        v.tensor_tensor(suf[0], suf[0], pre[1][:, :, s - 1:s].to_broadcast(shape), ALU.add).then_inc(*hr.mark("dve", f"suf{n}"))
                        dve.wait_ge(*hr.after("dve", f"suf{n}", it))
                        v.tensor_tensor(pre[1], pre[1], pre[0][:, :, s - 1:s].to_broadcast(shape), ALU.add).then_inc(*hr.mark("dve", f"pre{n}"))
                    if n >= 1:
                        v.copy_predicated(h_sc[:], lmask[:, n - 1].unsqueeze(1).to_broadcast([P, T, P]),
                                          sc[n % 2][:, 0:T * P].rearrange("p (t k) -> p t k", t=T)).then_inc(*hr.mark("dve", f"mk{n - 1}"))
                if j == 9:
                    dve.wait_ge(*hr.after("act", "sq1", it))
                    v.tensor_scalar(ssk[:, 0:T], ssk[:, 0:T], 1.0 / HK, EPS, ALU.mult, ALU.add).then_inc(*hr.mark("dve", "e"))
                    dve.wait_ge(*hr.after("act", "rt", it))
                    v.reciprocal(ssk[:, 0:T], ssk[:, 0:T]).then_inc(*hr.mark("dve", "r"))
                    dve.wait_ge(*hr.after("dve", "r", it))
                    o = sc[1][:, 0:T * HK].rearrange("p (t d) -> p t d", t=T)
                    v.tensor_tensor(h_o[:], o, over(ssk[:, 0:T], [P, T, HK]), ALU.mult).then_inc(*hr.mark("dve", "on"))
                    dve.wait_ge(*hr.after("dve", "on", it))
                    u = hg[:, 3, :, bass.ds(it * HK, HK)]
                    v.tensor_tensor(u, h_o[:], u, ALU.mult).then_inc(*hr.mark("dve", "u"))
                if not (isinstance(it, int) and it == HH - 1):
                    gates_of(it + 1, j)
            return side

        for j in range(8, 12):
            gates_of(0, j)

        dve.wait_ge(sig_free, 1)
        run(dve, "gate_conv", stream(gate_side(phases["gate_conv"], y2, True, recur(0))))
        end_phase(dve, "gate_conv")
        body = stream(gate_side(phases["gate_mem"], y2, False, for_branch(
            ym_split, lambda k: ol[:, 16 + k], lambda k: oh[:, 16 + k], [0, 1, 2, 3], recur(4))))
        run(dve, "gate_mem", body, first=body, last=body)
        end_phase(dve, "gate_mem")
        body = stream(gate_side(phases["gate_hg"], y2, False, for_branch(
            yb_split, lambda k: ol[:, 8 + k], lambda k: oh[:, 8 + k], [0, 1, 2, 3], None, V_HG)))
        run(dve, "gate_hg", body, first=body)
        end_phase(dve, "gate_hg", wait=False)
        y2_lo = stepwise(y2_split, lambda k: ol[:, OUT2_SLOTS[k]], lambda k: oh[:, OUT2_SLOTS[k]])

        def gain_block(st, kept, src, gain, b):
            dve.wait_ge(*kept.after("act", f"m{b}{T - 1}"))
            part = src[:, :, b * NB:(b + 1) * NB]
            v.tensor_tensor(part, part, gain[:, b * NB:(b + 1) * NB].unsqueeze(1).to_broadcast([P, T, NB]), ALU.mult).then_inc(*st.mark("dve", f"w{b}"))

        def post(st, ph, src, res):
            dve.wait_ge(acc_free[1], 2 * ph.use(ph.times - 1, ph.blocks - 1) + T)
            v.tensor_reduce(rn[:], ss4[:], AX, ALU.add).then_inc(*st.mark("dve", "ms"))
            dve.wait_ge(*st.after("dve", "ms"))
            root_mean(st, rn[:], T, D)
            dve.wait_ge(*st.after("dve", "r"))
            for q in range(4):
                cols = slice(q * NB, (q + 1) * NB)
                for t in range(T):
                    ins = v.scalar_tensor_tensor(res[:, t, cols], src[:, t, cols], rn[:, t:t + 1], res[:, t, cols], ALU.mult, ALU.add)
                ins.then_inc(*st.mark("dve", f"x{q}"))

        def out2_side(i, j):
            y2_lo(i, j)
            if j in (10, 18, 26):
                dve.wait_ge(in_x1, 32)
                gain_block(post1, mixs, mix, gpost, j // 8 - 1)

        run(dve, "out_2", stream(out2_side))
        gain_block(post1, mixs, mix, gpost, 3)
        post(post1, phases["out_2"], mix, x2)
        x2_lo = stepwise(x2_split, lambda k: xl[:, k], lambda k: xh[:, k], V_FFN)
        x2_scales = scales(x2_norm, rnf)
        end_phase(dve, "out_2", wait=False)

        def first_side(i, j):
            x2_lo(i, j)
            x2_scales(i, j)

        def ffn_conv(i, h):
            dve.wait_ge(*ffs.after("pe", f"g{h}", i))
            for c in (2 * h, 2 * h + 1):
                w = lambda k: vcol[:, V_FW[k][0], bass.ds(i * 4 + (V_FW[k][1] + c), 1)]
                u = tp[h][:, (c % 2) * S:(c % 2 + 1) * S]
                v.tensor_scalar(f_c[:, c], u, w(2), None, ALU.mult).then_inc(*ffs.mark("dve", f"c{c}"))
                dve.wait_ge(*ffs.after("dve", f"c{c}", i))
                for back in (1, 2):
                    v.scalar_tensor_tensor(f_c[:, c, back:S], u[:, 0:S - back], w(2 - back), f_c[:, c, back:S],
                                           ALU.mult, ALU.add).then_inc(*ffs.mark("dve", f"b{c}{back}"))
                    dve.wait_ge(*ffs.after("dve", f"b{c}{back}", i))

        def ffn_mul(i):
            dve.wait_ge(*ffs.after("act", "gelu", i))
            for h in range(2):
                dve.wait_ge(*ffs.after("pe", f"v{h}", i))
                part = f_a[:, 2 * h:2 * h + 2].rearrange("p a b -> p (a b)")
                ins = v.tensor_tensor(part, part, tp[h][:], ALU.mult)
            ins.then_inc(*ffs.mark("dve", "y"))

        def ffn_lo(i):
            dve.wait_ge(*ffs.after("act", "h", i))
            k = bass.ds(i * 4, 4)
            v.tensor_tensor(fl[:, k], f_a[:], fh[:, k].bitcast(F32), ALU.subtract).then_inc(*ffs.mark("dve", "l"))

        def ffn_side(i, j):
            if j in (1, 2):
                ffn_conv(i, j - 1)
            if j == 5:
                ffn_mul(i)
            if j == 6:
                ffn_lo(i)

        run(dve, "ffn_first", stream(first_side))
        dve.wait_ge(out_x2, 16)
        run(dve, "ffn_up", stream(ffn_side))
        last = FT // 4 - 1
        for h in range(2):
            ffn_conv(last, h)
        ffn_mul(last)
        ffn_lo(last)
        end_phase(dve, "ffn_up")
        ph = phases["ffn_down"]

        def down_side(i, j):
            if (i, j) in ((0, 26), (1, 2), (1, 26)):
                dve.wait_ge(in_x2, 32)
                gain_block(post2, ffe, ff, gpost2, 2 * i + j // 24 - 1)

        stream(down_side)(ph, 0)
        stream(down_side, skip_last=True)(ph, 1)
        gain_block(post2, ffe, ff, gpost2, 3)
        post(post2, ph, ff, x2b)

    ctx.close()


def kernel(**inputs):
    import numpy as _np
    import concourse.bacc as _bacc
    from concourse import mybir as _mybir
    from concourse.bass_utils import run_bass_kernel_spmd as _run

    nc = _bacc.Bacc("TRN2", target_bir_lowering=False, num_devices=1)
    constants, level_masks = shape_constants()
    arrays, args = {}, {}
    given = {n: _np.ascontiguousarray(a) for n, a in inputs.items() if n != "hg_lower_bounds_2"}
    for name, a in {**given, "constants": constants, "level_masks": level_masks}.items():
        arrays[f"in_{name}"] = a
        args[name] = nc.dram_tensor(f"in_{name}", a.shape, _mybir.dt.from_np(a.dtype), kind="ExternalInput").ap()
    out = nc.dram_tensor("out_x", (1, S, D), F32, kind="ExternalOutput").ap()
    two_blocks(nc, out=out, **args)
    r = _run(nc, [arrays], core_ids=[0])
    return r.results[0]["out_x"]
```

```python
from contextlib import ExitStack

import numpy as np

import concourse.bass as bass
from concourse import mybir

F32 = mybir.dt.float32
F32R = mybir.dt.float32r
U8 = mybir.dt.uint8
ALU = mybir.AluOpType
ACT = mybir.ActivationFunctionType
AX = mybir.AxisListType.X

P = 128
D = 2048
S = 256
T = S // P
KT = D // P
NB = 512
EPS = 1e-6
NEG = -1e30
RING = 4
LEAD = 3

HD = 64
AH, AKV, AG = 12, 4, 3
BH = 12
CH, CD = 4, 128
AW, AKW, BW, CW = AH * HD, AKV * HD, BH * HD, CH * CD
A_COLS = 2 * AW + 2 * AKW
B_AT = A_COLS
F_AT = B_AT + 4 * BW
C_AT = F_AT + BH
G_AT = C_AT + 2 * CW

BR = D // 2
HH, HK = 8, 128
MH, MD = 4, 256
FF = 5632
FT = FF // P
HQ_AT, MQ_AT, G2_AT = 3 * BR, 7 * BR, 8 * BR
LOG_TINY = float(np.log(np.float32(1e-30)))
LEVELS = [1, 2, 4, 8, 16, 32, 64]

V_NORM, V_MEM, V_MIX, V_MEM2, V_FFN = (0, 0), (0, 16), (0, 32), (0, 48), (0, 64)
V_CONV, V_HG = (0, 80), (0, 104)
V_FW = [(1, 0), (1, FT), (2, 0)]
V_FB = (2, FT)
V_QK = 2 * FT
V_ROWS = [112, V_QK + 6, 2 * FT]

K_ID, K_REL, K_MASK, K_TRI, K_ONE, K_SLOPE = 0, 128, 512, 640, 768, 896
K_COLS = K_SLOPE + AH


def shape_constants():
    p = np.arange(P)
    c = np.zeros((P, K_COLS), np.float32)
    c[:, K_ID:K_ID + P] = np.eye(P)
    own = p[:, None] - p[None, :]
    before = own + P
    far = np.float32(1e34)
    own_rel = np.where(own >= 0, own, far)
    c[:, K_REL:K_REL + P] = own_rel
    c[:, K_REL + P:K_REL + 2 * P] = np.where(before < P, before, far)
    c[:, K_REL + 2 * P:K_REL + 3 * P] = own_rel
    c[:, K_MASK:K_MASK + P] = np.where(own >= 0, 0, NEG)
    c[:, K_TRI:K_TRI + P] = p[:, None] <= p[None, :]
    c[:, K_ONE:K_ONE + P] = 1
    c[:, K_SLOPE:] = -np.exp2(-8.0 * np.arange(1, AH + 1) / AH).astype(np.float32)
    j, i = p[:, None], p[None, :]
    masks = [(j // (2 * s) == i // (2 * s)) & (j // s % 2 == 0) & (i // s % 2 == 1) for s in LEVELS]
    return c, np.concatenate(masks, 1).astype(np.float32)


class Stage:

    def __init__(self, sem, name, **steps):
        self.steps = steps
        self.sems = {e: sem(f"{name}_{e}") for e in steps}
        self.place = {e: 0 for e in steps}

    def after(self, engine, step, it=0):
        n = self.steps[engine]
        return self.sems[engine], it * len(n) + n.index(step) + 1

    def mark(self, engine, step):
        n = self.steps[engine]
        assert n[self.place[engine]] == step, (n[self.place[engine]], step)
        self.place[engine] = (self.place[engine] + 1) % len(n)
        return self.sems[engine], 1


class Phase:

    def __init__(self, name, times, sizes, before):
        self.name, self.times, self.sizes, self.n = name, times, sizes, len(sizes)
        self.c0 = before.c0 + before.n * before.times if before else 0
        self.b0 = before.b0 + before.blocks * before.times if before else 0
        self.blocks = 0

    def chunk(self, i, j):
        return i * self.n + (self.c0 + j)

    def use(self, i, block):
        return i * (self.blocks // 2) + (self.b0 + block) // 2


FULL = [2] * (KT // 2)


def plan():
    gate_a = FULL + [2, 2, 1, 1]
    gate_c = FULL + [1, 1, 1, 1]
    gate_2 = FULL + [2, 2, 2, 2]
    down = [2] * 20 + [1] * 4
    spec = [
        ("a_proj", 2, FULL * 2, 2), ("b_proj", 3, FULL * 2, 2), ("c_proj", 1, FULL * 4, 4),
        ("gate_a", 4, gate_a, 2), ("gate_b", 4, gate_a, 2), ("gate_c", 4, gate_c, 2),
        ("out", 1, FULL * 4, 4), ("mem_kv_2", 1, FULL * 4, 4),
        ("conv_proj", 3, FULL * 2, 2), ("mq_proj", 1, FULL * 2, 2), ("hg_proj", 4, FULL * 2, 2),
        ("gate_conv", 4, gate_2, 2), ("gate_mem", 4, gate_2, 2), ("gate_hg", 4, gate_2, 2),
        ("out_2", 1, FULL * 4, 4), ("ffn_first", 1, FULL * 2, 2), ("ffn_up", FT // 4 - 1, FULL * 2, 2),
        ("ffn_down", 2, down * 2, 2),
    ]
    phases, before = {}, None
    for name, times, sizes, blocks in spec:
        before = Phase(name, times, sizes, before)
        before.blocks = blocks
        phases[name] = before
    return phases, before.c0 + before.n * before.times


def two_blocks(
    nc, x, mem, norm_gain, mem_norm_gain, w_in, b_forget, q_gain_a, k_gain_a, sinks_a, q_gain_b, k_gain_b,
    q_gain_c, k_gain_c, w_mem_kv, w_branch_a, w_branch_b, w_branch_c, w_out, mem_2, w_in_2, conv_mix_w_2,
    hg_norm_w_2, w_mem_kv_2, w_branch_2, w_out_2, norm_mix_pre_2, norm_mix_post_2, norm_mem_2,
    norm_ffn_pre_2, norm_ffn_post_2, w_ffn_up_2, conv_ffn_w_2, conv_ffn_b_2, w_ffn_down_2,
    constants, level_masks, out,
):
    phases, chunks = plan()
    ctx = ExitStack()

    def sem(name):
        return ctx.enter_context(nc.semaphore(name))

    base = (nc.sbuf_base + 31) // 32 * 32
    names = set()

    def at(name, offset, shape, dt=F32):
        assert name not in names
        names.add(name)
        return nc.alloc_sbuf_tensor_at(name, [P, *shape], dt, offset=base + offset)

    CHUNK = 2 * NB * 4
    TK = S * 4
    RAW_AT, HI_AT, LO_AT = 0, RING * CHUNK, 2 * RING * CHUNK
    X_AT = 3 * RING * CHUNK
    CONST_AT = X_AT + 2 * KT * TK
    O_AT = CONST_AT + 11776
    W_AT = O_AT + 48 * TK

    raw = at("raw", RAW_AT, [RING, 2, NB])
    hi = at("hi", HI_AT, [RING, 2, NB], F32R)
    lo = at("lo", LO_AT, [RING, 2, NB], F32R)
    xh = at("xh", X_AT, [KT, S], F32R)
    xl = at("xl", X_AT + KT * TK, [KT, S], F32R)
    oh = at("oh", O_AT, [24, S], F32R)
    ol = at("ol", O_AT + 24 * TK, [24, S], F32R)
    m2h = at("m2h", W_AT + 16384, [KT, S], F32R)
    m2l = at("m2l", W_AT + 32768, [KT, S], F32R)
    fh = at("fh", O_AT, [FT, S], F32R)
    fl = at("fl", O_AT + FT * TK, [FT, S], F32R)

    cursor = [CONST_AT]

    def const(name, shape, dt=F32):
        size = int(np.prod(shape)) * (1 if dt == U8 else 4)
        t = at(name, cursor[0], shape, dt)
        cursor[0] += (size + 31) // 32 * 32
        assert cursor[0] <= O_AT
        return t

    kc = const("kc", [K_COLS])
    lmask = const("lmask", [len(LEVELS), P], U8)
    vcol = const("vcol", [3, P])
    gqk = const("gqk", [3])
    sinks = const("sinks", [AH])
    bfor = const("bfor", [BH])
    wf_raw = const("wf_raw", [KT, BH])
    wf_hi = const("wf_hi", [KT, BH], F32R)
    wf_lo = const("wf_lo", [KT, BH], F32R)
    ss4 = const("ss4", [T, 4])
    rnf = const("rnf", [T])
    rn = const("rn", [T])
    rnx = const("rnx", [T])
    ssh = const("ssh", [T, 2 * BH])
    ssm = const("ssm", [T, 2 * CH])
    nmax = const("nmax", [8])
    m3 = const("m3", [12])
    mm = const("mm", [4])
    es = const("es", [8])
    den = const("den", [8])
    rden = const("rden", [8])
    cq = const("cq", [T, BH])
    logf = const("logf", [T, BH])
    tf = const("tf", [T, BH])
    h_ss = const("h_ss", [HH, T])
    ident = kc[:, K_ID:K_ID + P]

    pa = at("pa", W_AT, [T, A_COLS])
    pb = at("pb", W_AT + 16384, [T, 4 * BW])
    pc = at("pc", W_AT + 40960, [T, 2 * CW])
    mk1 = at("mk1", W_AT + 49152, [T, 2 * CW])
    x_in = at("x_in", W_AT + 16384, [T, D])
    mem_in = [at("mem_in0", O_AT + 16 * TK, [D]), at("mem_in1", O_AT + 40 * TK, [D])]
    vrow = at("vrow", W_AT + 57344, [3, P])
    y1 = at("y1", W_AT, [T, D])
    sig = at("sig", W_AT + 65536, [T, NB])
    lmask_in = at("lmask_in", W_AT + 65536, [len(LEVELS), P])
    a_qn = at("a_qn", W_AT + 40960, [T, AKV, HD])
    a_qt = at("a_qt", W_AT + 43008, [2, S])
    a_kt = at("a_kt", W_AT + 45056, [2, S])
    a_s = at("a_s", W_AT + 47104, [AKV, 3, P])
    a_pt = at("a_pt", W_AT + 53248, [2, 3, P])
    a_o = at("a_o", W_AT + 56320, [T, AKV, HD])
    a_sq = at("a_sq", W_AT + 47104, [T, AW + AKW])
    a_kn = at("a_kn", W_AT + 55296, [T, AKW])
    b_sq = at("b_sq", W_AT + 57344, [2 * BW])
    nck = at("nck", O_AT, [BH, S])
    ct = at("ct", W_AT + 63488, [S])
    B_AT_ = O_AT + 24 * TK
    b_qn = at("b_qn", B_AT_, [T, AG, HD])
    b_kn = at("b_kn", B_AT_ + 1536, [T, AG, HD])
    b_qt = at("b_qt", B_AT_ + 3072, [2, S])
    b_kt = at("b_kt", B_AT_ + 5120, [2, S])
    b_s = at("b_s", B_AT_ + 7168, [AG, 3, P])
    b_pt = at("b_pt", B_AT_ + 11776, [2, 3, P])
    b_o = at("b_o", B_AT_ + 14848, [T, AG, HD])
    c_qn = at("c_qn", W_AT + 57344, [T, CD])
    c_kn = at("c_kn", W_AT + 58368, [T, CD])
    c_qt = at("c_qt", W_AT + 59392, [S])
    c_kt = at("c_kt", W_AT + 60416, [S])
    c_p = at("c_p", W_AT + 61440, [T, S])
    c_pt = at("c_pt", W_AT + 63488, [T, S])
    me_sq = at("me_sq", W_AT + 57344, [T, CW])
    x_again = at("x_again", X_AT, [T, D])
    mem2_in = at("mem2_in", W_AT + 49152, [T, D])
    x1 = at("x1", W_AT, [T, D])
    x1n = at("x1n", W_AT + 49152, [T, D])
    mk2 = at("mk2", O_AT + 8 * TK, [T, BR])
    mv2 = at("mv2", O_AT + 32 * TK, [T, BR])
    hg = at("hg", W_AT, [4, T, BR])
    cv = at("cv", W_AT + 32768, [3, T, BR])
    mq = at("mq", W_AT + 57344, [T, BR])
    u_st = at("u_st", W_AT + 65536, [T, 2, P])
    cb_st = at("cb_st", W_AT + 67584, [T, 2, P])
    v_tm = at("v_tm", O_AT + 16 * TK, [2, S])
    d_q = at("d_q", O_AT + 18 * TK, [T, MD])
    d_k = at("d_k", O_AT + 20 * TK, [T, MD])
    d_qt = at("d_qt", O_AT + 22 * TK, [2, S])
    d_kt = at("d_kt", O_AT + 40 * TK, [2, S])
    d_p = at("d_p", O_AT + 42 * TK, [T, S])
    d_pt = at("d_pt", O_AT + 44 * TK, [T, S])
    qt = at("qt", W_AT + 32768, [HH, S])
    zt = at("zt", W_AT + 40960, [HH, S])
    H_AT, H2_AT = O_AT + 8 * TK, O_AT + 32 * TK
    h_l, h_pre, h_suf, h_k, h_ls, h_d, h_kz, h_e = (
        at(n, H_AT + TK * k, [S]) for k, n in enumerate(("h_l", "h_pre", "h_suf", "h_k", "h_ls", "h_d", "h_kz", "h_e")))
    h_g = at("h_g", H2_AT, [S])
    h_sc = at("h_sc", H2_AT + TK, [T, P])
    h_off = at("h_off", H2_AT + 2 * TK, [P])
    h_sq = at("h_sq", H2_AT + 3 * TK, [T, HK])
    y2 = at("y2", W_AT, [T, D])
    mix = at("mix", W_AT, [T, D])
    x2 = at("x2", W_AT + 16384, [T, D])
    gpost = at("gpost", W_AT + 32768, [D])
    F_W = W_AT + 40960
    f_g = at("f_g", F_W, [T, NB])
    f_v = at("f_v", F_W + 4096, [T, NB])
    f_c = at("f_c", F_W + 8192, [4, S])
    f_a = at("f_a", F_W + 12288, [4, S])
    ff = at("ff", F_W, [T, D])
    x2b = at("x2b", X_AT, [T, D])
    gpost2 = at("gpost2", X_AT + KT * TK, [D])

    acc = [[ctx.enter_context(nc.psum_tensor(f"acc{p}{t}", [P, NB], F32)) for t in range(T)] for p in range(2)]
    tp = [ctx.enter_context(nc.psum_tensor(f"tp{n}", [P, NB], F32)) for n in range(2)]
    sc = [ctx.enter_context(nc.psum_tensor(f"sc{n}", [P, NB], F32)) for n in range(2)]

    nck_d = nc.dram_tensor("nck_d", [BH, S], F32).ap()
    x1_d = nc.dram_tensor("x1_d", [S, D], F32).ap()
    x2_d = nc.dram_tensor("x2_d", [S, D], F32).ap()

    loaded = [sem(f"chunk_loaded{n}") for n in range(RING)]
    hi_ready = sem("hi_ready")
    lo_ready = sem("lo_ready")
    chunk_done = sem("chunk_done")
    acc_free = [sem(f"acc_free{n}") for n in range(2)]
    phase_end = sem("phase_end")
    in_first, in_const, in_mem, in_wf = (sem(n) for n in ("in_first", "in_const", "in_mem", "in_wf"))
    in_x = [sem(f"in_x_half{half}") for half in range(2)]
    in_mem2, in_x_again, out_x1, in_x1 = sem("in_mem2"), sem("in_x_again"), sem("out_x1"), sem("in_x1")
    out_x2, in_x2, out_nck, in_nck, out_y = (sem(n) for n in ("out_x2", "in_x2", "out_nck", "in_nck", "out_y"))

    BANKS = KT // 2

    def split_steps(banks):
        return dict(pe=[f"t{n}" for n in range(banks)], act=[f"h{n}" for n in range(banks)],
                    dve=[f"l{n}" for n in range(banks)])

    def norm_stage(name):
        s = split_steps(BANKS)
        return Stage(sem, name, pe=s["pe"], act=[f"sq{n}" for n in range(4 * T)] + ["rt"] + s["act"], dve=["ms", "e", "r", "n0", "n1"] + s["dve"])

    setup = Stage(sem, "setup", pe=["vn", "v"], act=["wh"], dve=["vn", "v", "qk0", "qk1", "wl"])
    norm_m, norm_m2, norm_x1 = (norm_stage(n) for n in ("norm_m", "norm_m2", "norm_x1"))
    x_split, x2_split = (Stage(sem, n, **split_steps(BANKS)) for n in ("x_split", "x2_split"))
    x_norm, x2_norm = (Stage(sem, n, act=[f"sq{k}" for k in range(4 * T)] + ["rt"], dve=["ms", "e", "r"])
                       for n in ("x_norm", "x2_norm"))
    win_prep = Stage(sem, "win_prep", pe=["k"], act=["sq", "rt", "silu", "k"], dve=["ms", "e", "r", "kn"])
    G4 = range(AKV)
    G3 = range(AG)
    win = Stage(
        sem, "win",
        pe=["q"] + [f"s{g}" for g in G4] + [f"{k}{g}" for g in G4 for k in ("pt", "o")],
        act=["q", "p"] + ["es"] + [f"pt{g}" for g in G4],
        dve=["qn"] + [f"s{g}" for g in G4] + ["m3", "mm", "n0", "n1", "neg", "es", "den", "rd", "on", "u"])
    ua_split = Stage(sem, "ua_split", **split_steps(3))
    fg_prep = Stage(
        sem, "fg_prep", pe=["f", "ft", "c", "ct"], act=["sq0", "sq1", "rt", "silu", "e", "l"],
        dve=["f", "ms0", "ms1", "e", "r", "z", "a", "lf", "c", "ct"])
    fg = Stage(
        sem, "fg",
        pe=["q", "k"] + [f"s{g}" for g in G3] + [f"{k}{g}" for g in G3 for k in ("pt", "o")],
        act=["q", "k", "p"] + [f"pt{g}" for g in G3],
        dve=["qn", "kn"] + [f"s{g}" for g in G3] + ["mask", "m3", "mm", "n0", "neg", "rd", "on", "u"])
    ub_split = Stage(sem, "ub_split", **split_steps(3))
    me_prep = Stage(sem, "me_prep", act=["sq0", "sq1", "rt", "silu"], dve=["ms0", "ms1", "e", "r"])
    me = Stage(sem, "me", pe=["qk", "s", "pt", "o"], act=["q", "k", "p", "pt"], dve=["qn", "kn", "m", "rd", "on", "u"])
    uc_split = Stage(sem, "uc_split", **split_steps(2))
    y1_split = Stage(sem, "y1_split", **split_steps(BANKS))
    y2_split = Stage(sem, "y2_split", **split_steps(BANKS))
    sig_free = sem("sig_free")
    GATES = ("gate_a", "gate_b", "gate_c", "gate_conv", "gate_mem", "gate_hg")
    out1 = Stage(sem, "out1", dve=[f"x{n}" for n in range(4)])
    conv = Stage(sem, "conv", pe=["u", "b"], act=["cb", "h"], dve=["u", "c0", "c1", "c2", "y", "l"])
    ma = Stage(sem, "ma", pe=["q", "k", "s", "pt", "o"], act=["sq", "sk", "q", "k", "p", "pt"], dve=["m", "rd", "u"])
    ym_split = Stage(sem, "ym_split", **split_steps(4))
    hg_prep = Stage(sem, "hg_prep", pe=[f"t{n}" for n in range(8)], act=[f"t{n}" for n in range(8)])
    LV = range(len(LEVELS))
    hp1 = Stage(sem, "hp1", act=["e1", "l1"], dve=["a"])
    hp2 = Stage(sem, "hp2", act=["e2", "k", "l2"], dve=["ls", "d0", "d", "kz", "lf", "lf0", "k"])
    hr_dve = ["dg"]
    for n in range(len(LEVELS) + 1):
        hr_dve += [f"gl{n}", f"gr{n}"]
        if n < len(LEVELS):
            hr_dve += [f"suf{n}", f"pre{n}"]
        if n > 0:
            hr_dve += [f"mk{n - 1}"]
    hr = Stage(
        sem, "hr", pe=["d"] + [f"s{n}" for n in LV] + ["s7", "o"],
        act=[f"e{k}{n}" for n in range(8) for k in "lr"] + ["off", "sq0", "sq1"],
        dve=hr_dve + ["u"])
    hn = Stage(sem, "hn", act=["rt"], dve=["e", "r"] + [f"n{n}" for n in range(4)])
    yb_split = Stage(sem, "yb_split", **split_steps(4))
    mixs, ffe = (Stage(sem, n, act=[f"m{b}{t}" for b in range(4) for t in range(T)]) for n in ("mixs", "ffe"))
    post1 = Stage(sem, "post1", act=["rt"], dve=["w0", "w1", "w2", "ms", "e", "w3", "r", "x0", "x1", "x2", "x3"])
    ffs = Stage(sem, "ffs", pe=["g0", "g1", "v0", "v1"], act=["ev", "gelu0", "gelu1", "h"],
                dve=[f"{k}" for c in range(4) for k in (f"c{c}", f"b{c}1", f"b{c}2")] + ["y", "l"])
    post2 = Stage(sem, "post2", act=["rt"], dve=["w0", "w1", "w2", "ms", "e", "w3", "r", "x0", "x1", "x2", "x3"])

    def w3(w):
        return w.rearrange("(k p) n -> p k n", p=P)

    wi, wi2 = w3(w_in[0]), w3(w_in_2[0])
    w_up, w_down = w3(w_ffn_up_2[0]), w3(w_ffn_down_2[0])
    w_o, w_o2, w_m, w_m2 = w3(w_out[0]), w3(w_out_2[0]), w3(w_mem_kv[0]), w3(w_mem_kv_2[0])
    w_br = {"a": w3(w_branch_a[0]), "b": w3(w_branch_b[0]), "c": w3(w_branch_c[0])}
    w_br2 = [w3(w_branch_2[0, n]) for n in range(3)]

    def weights(name, i, n):
        two = lambda w, col: [(w, col), (w, col + NB)]
        if name == "a_proj":
            return two(wi, i * 2 * NB)
        if name == "b_proj":
            return two(wi, i * 2 * NB + B_AT)
        if name == "c_proj":
            return two(wi, C_AT) + two(w_m, 0)
        if name in ("gate_a", "gate_b", "gate_c"):
            return [(wi, i * NB + (G_AT + "abc".index(name[-1]) * D)), (w_br[name[-1]], n * NB - NB)]
        if name in ("out", "out_2", "mem_kv_2"):
            w = {"out": w_o, "out_2": w_o2, "mem_kv_2": w_m2}[name]
            return two(w, 0) + two(w, 2 * NB)
        if name == "conv_proj":
            return two(wi2, i * 2 * NB)
        if name == "mq_proj":
            return two(wi2, MQ_AT)
        if name == "hg_proj":
            return two(wi2, i * 2 * NB + HQ_AT)
        if name in ("gate_conv", "gate_hg", "gate_mem"):
            g = ("gate_conv", "gate_hg", "gate_mem").index(name)
            return [(wi2, i * NB + (G2_AT + g * D)), (w_br2[g], n * NB - NB)]
        if name == "ffn_first":
            return [(w_up, 0), (w_up, FF)]
        if name == "ffn_up":
            return [(w_up, i * NB + NB), (w_up, i * NB + (FF + NB))]
        if name == "ffn_down":
            return two(w_down, i * 2 * NB)

    def positions(ph):
        per = {"ffn_down": len(ph.sizes) // 2}.get(ph.name, KT // 2)
        res, k, block = [], 0, 0
        for j, size in enumerate(ph.sizes):
            new = j > 0 and (j % per == 0 if not ph.name.startswith("gate") else j == KT // 2)
            if new:
                block, k = block + 1, 0
            res.append([block, k, size, False])
            k += size
        for j, r in enumerate(res):
            r[3] = j + 1 == len(res) or res[j + 1][0] != r[0]
        return res

    HEAD_PAIRS = {1: [0], 2: [1], 3: [2], 4: [3], 5: [4, 5], 6: [6, 7]}
    OUT_SLOTS = [*range(10, 24), 0, 1]
    OUT2_SLOTS = [*range(0, 8), *range(16, 24)]

    def stationary(name, block):
        own = lambda k: k
        if name in ("a_proj", "b_proj", "conv_proj", "mq_proj", "hg_proj", "ffn_first", "ffn_up"):
            return xh, xl, own
        if name == "c_proj":
            return (xh, xl, own) if block < 2 else (oh, ol, own)
        if name.startswith("gate"):
            if block == 0:
                return xh, xl, own
            first = {"gate_a": 16, "gate_b": 0, "gate_c": 6, "gate_conv": 0, "gate_mem": 16, "gate_hg": 8}[name]
            return oh, ol, lambda k: first + k
        if name == "out":
            return oh, ol, lambda k: OUT_SLOTS[k]
        if name == "out_2":
            return oh, ol, lambda k: OUT2_SLOTS[k]
        if name == "mem_kv_2":
            return m2h, m2l, own
        return fh, fl, own

    block_ctx = ctx.enter_context(nc.Block())

    def run(engine, name, body, first=None, last=None, lasts=1):
        ph = phases[name]
        begin, end = 0, ph.times
        if first or ph.c0 == 0:
            (first or body)(ph, 0)
            begin = 1
        if last:
            end -= lasts
        if end - begin == 1:
            body(ph, begin)
        elif end > begin:
            with engine.Fori(begin, end) as i:
                body(ph, i)
        if last:
            for i in range(end, ph.times):
                last(ph, i)

    def late(side):
        return lambda i, j: side(i, j - 1)

    ENDS = ["a_proj", "b_proj", "c_proj", "gate_a", "gate_b", "gate_c", "out", "mem_kv_2", "conv_proj",
            "mq_proj", "hg_proj", "gate_conv", "gate_mem", "gate_hg", "out_2", "ffn_up"]

    def ended(name):
        return phase_end, 3 * (ENDS.index(name) + 1)

    def end_phase(engine, name, wait=True):
        engine.drain().then_inc(phase_end, 1)
        if wait:
            engine.wait_ge(*ended(name))

    def gate_used(name, i):
        return sig_free, 1 + T * (GATES.index(name) * (D // NB) + i + 1)

    @block_ctx.sync
    def _(sp):
        def rows(dst, vec, n, landed=in_const):
            sp.dma_start(dst, vec.rearrange("(r c) -> r c", c=P) if n > 1 else vec).then_inc(landed, 16)

        sp.dma_start(kc[:], constants).then_inc(in_first, 16)
        rows(vrow[V_NORM[1]:V_NORM[1] + KT, V_NORM[0]], norm_gain[0], KT, in_first)
        for half in range(2):
            cols = slice(half * D // 2, (half + 1) * D // 2)
            sp.dma_start(x_in[:, :, cols], x[0].rearrange("(t p) d -> p t d", p=P)[:, :, cols]).then_inc(in_x[half], 16)

        def vectors():
            for (g, r), vec in ((V_MEM, mem_norm_gain), (V_MIX, norm_mix_pre_2),
                                (V_MEM2, norm_mem_2), (V_FFN, norm_ffn_pre_2)):
                rows(vrow[r:r + KT, g], vec[0], KT)
            for k in range(3):
                rows(vrow[V_CONV[1] + 8 * k:V_CONV[1] + 8 * k + 8, 0], conv_mix_w_2[0, k], 8)
                g, r = V_FW[k]
                rows(vrow[r:r + FT, g], conv_ffn_w_2[0, k], FT)
            rows(vrow[V_HG[1]:V_HG[1] + HH, 0], hg_norm_w_2[0], HH)
            rows(vrow[V_FB[1]:V_FB[1] + FT, 2], conv_ffn_b_2[0], FT)
            for k, vec in enumerate((q_gain_a, k_gain_a, q_gain_b, k_gain_b)):
                for half in range(2):
                    sp.dma_start(vrow[V_QK + k:V_QK + k + 1, 1, half * HD:half * HD + HD], vec).then_inc(in_const, 16)
            for k, vec in enumerate((q_gain_c, k_gain_c)):
                sp.dma_start(vrow[V_QK + 4 + k:V_QK + 5 + k, 1, :], vec).then_inc(in_const, 16)
            sp.dma_start(sinks[:], sinks_a.partition_broadcast(P)).then_inc(in_const, 16)
            sp.dma_start(bfor[:], b_forget.partition_broadcast(P)).then_inc(in_const, 16)
            sp.dma_start(lmask_in[:], level_masks.rearrange("p (l c) -> p l c", c=P)).then_inc(in_const, 16)

        def load(ph, i, n=1):
            spec = weights(ph.name, i, n)
            for j, (blk, k, size, _) in enumerate(positions(ph)):
                c = ph.chunk(i, j)
                slot = (ph.c0 + j) % RING
                w, col = spec[blk]
                source = w[:, k:k + size, bass.ds(col, NB)]
                if not (isinstance(c, int) and c < RING):
                    sp.wait_ge(lo_ready, c - (RING - 1))
                sp.dma_start(raw[:, slot, 0:size], source).then_inc(loaded[slot], 16)
                if isinstance(c, int) and c == 2 * RING - 1:
                    vectors()

        ph = phases["a_proj"]
        load(ph, 0)
        load(ph, 1)
        for name in list(phases)[1:]:
            ph = phases[name]
            if ph.times == 1:
                load(ph, 0)
            else:
                with sp.Fori(1, ph.times + 1) as n:
                    load(ph, n - 1, n)
        for q in range(4):
            cols = slice(q * NB, (q + 1) * NB)
            sp.wait_ge(*post2.after("dve", f"x{q}"))
            sp.dma_start(out[0].rearrange("(t p) d -> p t d", p=P)[:, :, cols], x2b[:, :, cols]).then_inc(out_y, 16)
        sp.wait_ge(out_y, 16 * 4)

    N_CONST = 4 + 3 * 2 + 2 + 8 + 2 + 3

    @block_ctx.gpsimd
    def _(pool):
        pool.wait_ge(*x_split.after("dve", f"l{BANKS - 1}"))
        pool.dma_start(wf_raw[:], wi[:, :, F_AT:F_AT + BH]).then_inc(in_wf, 16)
        for t in range(T):
            pool.dma_start(mem_in[t][:], mem[0, t * P:(t + 1) * P]).then_inc(in_mem, 16)
        pool.wait_ge(*fg_prep.after("dve", "ct"))
        pool.dma_start(nck_d, ct[0:BH, :]).then_inc(out_nck, 16)
        pool.wait_ge(out_nck, 16)
        pool.wait_ge(*ended("c_proj"))
        pool.dma_start(nck[:], nck_d.partition_broadcast(P)).then_inc(in_nck, 16)
        pool.wait_ge(*ended("gate_b"))
        pool.dma_start(mem2_in[:], mem_2[0].rearrange("(t p) d -> p t d", p=P)).then_inc(in_mem2, 16)
        pool.wait_ge(*ended("gate_c"))
        pool.dma_start(x_again[:], x[0].rearrange("(t p) d -> p t d", p=P)).then_inc(in_x_again, 16)
        pool.wait_ge(*out1.after("dve", "x3"))
        pool.dma_start(x1_d.rearrange("(t p) d -> p t d", p=P), x1[:]).then_inc(out_x1, 16)
        pool.wait_ge(out_x1, 16)
        pool.wait_ge(*ended("gate_hg"))
        pool.dma_start(x2[:], x1_d.rearrange("(t p) d -> p t d", p=P)).then_inc(in_x1, 16)
        pool.dma_start(gpost[:], norm_mix_post_2[0].partition_broadcast(P)).then_inc(in_x1, 16)
        pool.wait_ge(*post1.after("dve", "x3"))
        pool.dma_start(x2_d.rearrange("(t p) d -> p t d", p=P), x2[:]).then_inc(out_x2, 16)
        pool.wait_ge(out_x2, 16)
        pool.wait_ge(*ended("ffn_up"))
        pool.dma_start(x2b[:], x2_d.rearrange("(t p) d -> p t d", p=P)).then_inc(in_x2, 16)
        pool.dma_start(gpost2[:], norm_ffn_post_2[0].partition_broadcast(P)).then_inc(in_x2, 16)

    @block_ctx.tensor
    def _(pe):
        def mm(o, lhsT, rhs, start=True, stop=True):
            return nc.tensor.matmul(o, lhsT, rhs, start=start, stop=stop)

        def tr(o, in_):
            k = in_.shape[0]
            return nc.tensor.transpose(o, in_, ident[0:k, :])

        def chunk(ph, i, j, pos):
            blk, k0, size, last = pos
            pair = blk % 2
            slot = (ph.c0 + j) % RING
            ah, al, place = stationary(ph.name, blk)
            if k0 == 0 and not (isinstance(i, int) and ph.use(i, blk) == 0):
                pe.wait_ge(acc_free[pair], 2 * ph.use(i, blk))
            pe.wait_ge(lo_ready, ph.chunk(i, j) + 1)
            for kk in range(size):
                ks = place(k0 + kk)
                for t in range(T):
                    tok = slice(t * P, (t + 1) * P)
                    o = acc[pair][t][:]
                    end = last and kk == size - 1
                    mm(o, al[:, ks, tok], hi[:, slot, kk], start=(k0 + kk == 0), stop=False)
                    mm(o, ah[:, ks, tok], hi[:, slot, kk], start=False, stop=False)
                    ins = mm(o, ah[:, ks, tok], lo[:, slot, kk], start=False, stop=end)
            ins.then_inc(chunk_done, 1)

        def stream(side, ready=None):
            def body(ph, i):
                for j, pos in enumerate(positions(ph)):
                    if ready:
                        ready(i, j)
                    chunk(ph, i, j, pos)
                    side(i, j)
            return body

        nothing = lambda i, j: None

        def split(st, src, ready, n, kts=None):
            bank = tp[n % 2]
            if n >= 2:
                pe.wait_ge(*st.after("dve", f"l{n - 2}"))
            if ready:
                pe.wait_ge(*ready)
            for kk in range(2):
                for t in range(T):
                    ins = tr(bank[:, kk * S + t * P:kk * S + (t + 1) * P], src(t, (2 * n + kk) * P))
            ins.then_inc(*st.mark("pe", f"t{n}"))

        def norm_split(st, src, n):
            split(st, src, st.after("dve", "n1"), n)

        def stepwise(st, src, ready, side):
            for n in range(2):
                split(st, src, ready(n), n)

            def ahead(i, j):
                if i == 0 and j + 2 < BANKS:
                    split(st, src, ready(j + 2), j + 2)
                side(i, j)

            def have(i, j):
                if i == 0 and j < BANKS:
                    pe.wait_ge(*st.after("dve", f"l{j}"))
            return stream(ahead, have)

        pe.wait_ge(in_first, 16 * 2)
        nc.tensor.transpose(sc[0][:, 0:KT], vrow[0:KT, V_NORM[0]], ident[0:KT, 0:KT]).then_inc(*setup.mark("pe", "vn"))

        def vectors(i, j):
            if i == 1 and j == 0:
                pe.wait_ge(in_const, 16 * N_CONST)
                pe.wait_ge(*setup.after("dve", "vn"))
                for g in range(3):
                    ins = nc.tensor.transpose(sc[0][:, g * P:g * P + V_ROWS[g]], vrow[0:V_ROWS[g], g], ident[0:V_ROWS[g], 0:V_ROWS[g]])
                ins.then_inc(*setup.mark("pe", "v"))

        run(pe, "a_proj", stepwise(x_split, lambda t, c: x_in[:, t, c:c + P], lambda n: (in_x[n // 4], 16), vectors))
        end_phase(pe, "a_proj", wait=False)

        def window(i, j):
            if isinstance(i, int) and j == -1:
                pe.wait_ge(*win_prep.after("dve", "kn"))
                for t in range(T):
                    for pair in range(2):
                        ins = tr(tp[0][:, pair * S + t * P:pair * S + (t + 1) * P], a_kn[:, t, pair * P:(pair + 1) * P])
                ins.then_inc(*win_prep.mark("pe", "k"))
            if j == 0:
                if isinstance(i, int):
                    pe.wait_ge(*win_prep.after("act", "k"))
                pe.wait_ge(*win.after("dve", "qn", i))
                for t in range(T):
                    for pair in range(2):
                        ins = tr(tp[0][:, pair * S + t * P:pair * S + (t + 1) * P], a_qn[:, t, 2 * pair:2 * pair + 2, :].rearrange("p h d -> p (h d)"))
                ins.then_inc(*win.mark("pe", "q"))
            if j in (1, 2):
                for g in (2 * j - 2, 2 * j - 1):
                    pe.wait_ge(*win.after("act", "q", i))
                    if g >= 2:
                        pe.wait_ge(*win.after("dve", f"s{g - 2}", i))
                    half = slice(64 * (g % 2), 64 * (g % 2) + 64)
                    o = sc[g % 2]
                    mm(o[:, 0:P], a_qt[half, g // 2, 0:P], a_kt[half, g // 2, 0:P])
                    mm(o[:, P:3 * P], a_qt[half, g // 2, P:S], a_kt[half, g // 2, :]).then_inc(*win.mark("pe", f"s{g}"))
            if 7 <= j < 11:
                g = j - 7
                pe.wait_ge(*win.after("act", f"pt{g}", i))
                v = lambda t: pa[:, t, AW + AKW + g * HD:AW + AKW + (g + 1) * HD]
                mm(sc[0][:, g * HD:(g + 1) * HD], a_pt[:, g % 2, 0], v(0))
                o = sc[0][:, S + g * HD:S + (g + 1) * HD]
                mm(o, a_pt[:, g % 2, 1], v(0), stop=False)
                mm(o, a_pt[:, g % 2, 2], v(1), start=False).then_inc(*win.mark("pe", f"o{g}"))
            if 6 <= j < 10:
                g = j - 6
                pe.wait_ge(*win.after("act", "p", i))
                if g >= 2:
                    pe.wait_ge(*win.after("act", f"pt{g - 2}", i))
                for b in range(3):
                    ins = tr(tp[g % 2][:, b * P:(b + 1) * P], a_s[:, g, b])
                ins.then_inc(*win.mark("pe", f"pt{g}"))

        run(pe, "b_proj", stream(late(window)), first=stream(late(window)))
        end_phase(pe, "b_proj", wait=False)

        def c_side(i, j):
            if j == 0:
                pe.wait_ge(*setup.after("dve", "wl"))
                o = sc[1][0:BH, 0:S]
                for k in range(KT):
                    mm(o, wf_lo[:, k], xh[:, k], start=(k == 0), stop=False)
                    mm(o, wf_hi[:, k], xh[:, k], start=False, stop=False)
                    ins = mm(o, wf_hi[:, k], xl[:, k], start=False, stop=(k == KT - 1))
                ins.then_inc(*fg_prep.mark("pe", "f"))
            if j == 1:
                pe.wait_ge(*fg_prep.after("dve", "f"))
                for t in range(T):
                    ins = nc.tensor.transpose(sc[1][:, t * BH:(t + 1) * BH], ct[0:BH, t * P:(t + 1) * P], ident[0:BH, 0:BH])
                ins.then_inc(*fg_prep.mark("pe", "ft"))
            if 8 <= j < 16:
                norm_split(norm_m, lambda t, c: mem_in[t][:, c:c + P], j - 8)
            if j == 13:
                pe.wait_ge(*fg_prep.after("dve", "lf"))
                tri, one = kc[:, K_TRI:K_TRI + P], kc[:, K_ONE:K_ONE + P]
                mm(sc[0][:, 0:BH], tri, logf[:, 0])
                mm(sc[0][:, BH:2 * BH], one, logf[:, 0], stop=False)
                mm(sc[0][:, BH:2 * BH], tri, logf[:, 1], start=False).then_inc(*fg_prep.mark("pe", "c"))
            if j == 15:
                pe.wait_ge(*fg_prep.after("dve", "c"))
                for t in range(T):
                    ins = tr(sc[1][0:BH, t * P:(t + 1) * P], cq[:, t])
                ins.then_inc(*fg_prep.mark("pe", "ct"))
            if 18 <= j < 21:
                split(ua_split, lambda t, c: pa[:, t, AW + 2 * AKW + c:AW + 2 * AKW + c + P], None, j - 18)

        def c_ready(i, j):
            if j >= KT:
                pe.wait_ge(*norm_m.after("dve", f"l{(j - KT) % BANKS}"))

        run(pe, "c_proj", stream(c_side, c_ready))
        end_phase(pe, "c_proj", wait=False)

        def forget(i, j):
            pairs = ((0, P), (1, HD))
            if j == 0:
                for what, src, bank in (("q", b_qn, tp[0]), ("k", b_kn, tp[1])):
                    pe.wait_ge(*fg.after("dve", f"{what}n", i))
                    for n, w in pairs:
                        for t in range(T):
                            ins = tr(bank[0:w, n * S + t * P:n * S + (t + 1) * P], src[:, t].rearrange("p h d -> p (h d)")[:, n * P:n * P + w])
                    ins.then_inc(*fg.mark("pe", what))
            if j in (1, 2):
                for g in ((0, 1) if j == 1 else (2,)):
                    pe.wait_ge(*fg.after("act", "k", i))
                    if g >= 2:
                        pe.wait_ge(*fg.after("dve", f"s{g - 2}", i))
                    half = slice(64 * (g % 2), 64 * (g % 2) + 64)
                    o = sc[g % 2]
                    mm(o[:, 0:P], b_qt[half, g // 2, 0:P], b_kt[half, g // 2, 0:P])
                    mm(o[:, P:3 * P], b_qt[half, g // 2, P:S], b_kt[half, g // 2, :]).then_inc(*fg.mark("pe", f"s{g}"))
            if 7 <= j < 10:
                g = j - 7
                pe.wait_ge(*fg.after("act", f"pt{g}", i))
                v = lambda t: pb[:, t, bass.ds(i * AG * HD + (2 * BW + g * HD), HD)]
                mm(sc[0][:, g * HD:(g + 1) * HD], b_pt[:, g % 2, 0], v(0))
                o = sc[0][:, S + g * HD:S + (g + 1) * HD]
                mm(o, b_pt[:, g % 2, 1], v(0), stop=False)
                mm(o, b_pt[:, g % 2, 2], v(1), start=False).then_inc(*fg.mark("pe", f"o{g}"))
            if 6 <= j < 9:
                g = j - 6
                pe.wait_ge(*fg.after("act", "p", i))
                if g >= 2:
                    pe.wait_ge(*fg.after("act", f"pt{g - 2}", i))
                for b in range(3):
                    ins = tr(tp[g % 2][:, b * P:(b + 1) * P], b_s[:, g, b])
                ins.then_inc(*fg.mark("pe", f"pt{g}"))

        def for_branch(st, src, ready, at_, side, ready_of=None):
            def both(i, j):
                if j in at_:
                    for n in (n for n, k in enumerate(at_) if k == j):
                        split(st, src, ready_of(n) if ready_of else ready, n)
                side(i, j)

            def have(i, j):
                if j == KT // 2:
                    pe.wait_ge(*st.after("dve", f"l{len(at_) - 1}"))
            return stream(both, have)

        pe.wait_ge(*ua_split.after("dve", "l2"))
        run(pe, "gate_a", stream(late(forget)))
        end_phase(pe, "gate_a", wait=False)

        def memory(i, j):
            if j == 0:
                pe.wait_ge(*me.after("dve", "kn", i))
                for n, src in enumerate((c_qn, c_kn)):
                    for t in range(T):
                        ins = tr(tp[0][:, n * S + t * P:n * S + (t + 1) * P], src[:, t])
                ins.then_inc(*me.mark("pe", "qk"))
            if j == 2:
                pe.wait_ge(*me.after("act", "k", i))
                for t in range(T):
                    ins = mm(sc[0][:, t * S:(t + 1) * S], c_qt[:, t * P:(t + 1) * P], c_kt[:])
                ins.then_inc(*me.mark("pe", "s"))
            if j == 5:
                pe.wait_ge(*me.after("act", "p", i))
                for m in range(T):
                    for t in range(T):
                        ins = tr(tp[1][:, m * S + t * P:m * S + (t + 1) * P], c_p[:, t, m * P:(m + 1) * P])
                ins.then_inc(*me.mark("pe", "pt"))
            if j == 7:
                pe.wait_ge(*me.after("act", "pt", i))
                for t in range(T):
                    for m in range(T):
                        ins = mm(sc[1][:, t * CD:(t + 1) * CD], c_pt[:, m, t * P:(t + 1) * P],
                                 mk1[:, m, bass.ds(i * CD + CW, CD)], start=(m == 0), stop=(m == T - 1))
                ins.then_inc(*me.mark("pe", "o"))

        def memory_first(i, j):
            if j == 1:
                pe.wait_ge(*ub_split.after("dve", "l0"))
            if j == 6:
                pe.wait_ge(*ub_split.after("dve", "l1"))
            memory(i, j - 1)

        run(pe, "gate_b", stream(late(memory)),
            first=for_branch(ub_split, lambda t, c: pb[:, t, 3 * BW + c:3 * BW + c + P], fg.after("dve", "u", D // NB - 1),
                             [0, 0, 4], memory_first))
        end_phase(pe, "gate_b", wait=False)
        run(pe, "gate_c", stream(nothing),
            first=for_branch(uc_split, lambda t, c: pc[:, t, CW + c:CW + c + P], me.after("dve", "u", D // NB - 1), [0, 1], nothing))
        end_phase(pe, "gate_c", wait=False)

        def out_side(i, j):
            if 16 <= j < 24:
                norm_split(norm_m2, lambda t, c: mem2_in[:, t, c:c + P], j - 16)

        run(pe, "out", stepwise(y1_split, lambda t, c: y1[:, t, c:c + P], lambda n: gate_used("gate_c", n // 2), out_side))
        end_phase(pe, "out", wait=False)

        def mem2_side(i, j):
            if 8 <= j < 16:
                norm_split(norm_x1, lambda t, c: x1n[:, t, c:c + P], j - 8)

        run(pe, "mem_kv_2", stream(mem2_side))
        end_phase(pe, "mem_kv_2", wait=False)
        run(pe, "conv_proj", stream(nothing))
        end_phase(pe, "conv_proj", wait=False)
        run(pe, "mq_proj", stream(nothing))
        end_phase(pe, "mq_proj", wait=False)

        def hg_side(i, j):
            if j == 0:
                pe.wait_ge(*conv.after("act", "cb", i))
                pe.wait_ge(*conv.after("dve", "u", i))
                for what, src, bank in (("u", u_st, tp[0]), ("b", cb_st, tp[1])):
                    for n in range(2):
                        for t in range(T):
                            ins = tr(bank[:, n * S + t * P:n * S + (t + 1) * P], src[:, t, n])
                    ins.then_inc(*conv.mark("pe", what))
            if j == 5:
                pe.wait_ge(*conv.after("dve", "y", i))
                for what, src, bank in (("q", d_q, tp[0]), ("k", d_k, tp[1])):
                    pe.wait_ge(*ma.after("act", f"s{what}", i))
                    for n in range(2):
                        for t in range(T):
                            ins = tr(bank[:, n * S + t * P:n * S + (t + 1) * P], src[:, t, n * P:(n + 1) * P])
                    ins.then_inc(*ma.mark("pe", what))
            if j == 7:
                pe.wait_ge(*ma.after("act", "k", i))
                for t in range(T):
                    for n in range(2):
                        ins = mm(sc[0][:, t * S:(t + 1) * S], d_qt[:, n, t * P:(t + 1) * P], d_kt[:, n],
                                 start=(n == 0), stop=(n == 1))
                ins.then_inc(*ma.mark("pe", "s"))
            if j == 10:
                pe.wait_ge(*ma.after("act", "p", i))
                for m in range(T):
                    for t in range(T):
                        ins = tr(tp[0][:, m * S + t * P:m * S + (t + 1) * P], d_p[:, t, m * P:(m + 1) * P])
                ins.then_inc(*ma.mark("pe", "pt"))
            if j == 12:
                pe.wait_ge(*ma.after("act", "pt", i))
                for t in range(T):
                    for m in range(T):
                        ins = mm(sc[1][:, t * MD:(t + 1) * MD], d_pt[:, m, t * P:(t + 1) * P],
                                 mv2[:, m, bass.ds(i * MD, MD)], start=(m == 0), stop=(m == T - 1))
                ins.then_inc(*ma.mark("pe", "o"))

        def hg_all(i, j):
            hg_side(i, j - 1)
            if not isinstance(i, int):
                return
            for n in HEAD_PAIRS.get(j, []):
                if n >= 2:
                    pe.wait_ge(*hg_prep.after("act", f"t{n - 2}"))
                else:
                    pe.wait_ge(*ma.after("dve", "u", i - 1))
                    pe.wait_ge(*ma.after("act", "p", i - 1))
                for h in range(2):
                    for t in range(T):
                        c = (2 * (n % 4) + h) * HK
                        ins = tr(sc[n % 2][:, h * S + t * P:h * S + (t + 1) * P], hg[:, n // 4, t, c:c + P])
                ins.then_inc(*hg_prep.mark("pe", f"t{n}"))
            if j == 7:
                pe.wait_ge(*hg_prep.after("act", "t7"))

        run(pe, "hg_proj", stream(hg_all), last=stream(hg_all))
        end_phase(pe, "hg_proj", wait=False)

        def recur(first):
            def side(i, j):
                it = i + first
                if j == 0:
                    pe.wait_ge(*hp2.after("dve", "k", it))
                    for t in range(T):
                        ins = mm(sc[0][:, t * P:(t + 1) * P], h_k[:, t * P:(t + 1) * P],
                                 qt[:, bass.ds(it, 1), t * P:(t + 1) * P].rearrange("p a b -> p (a b)"))
                    ins.then_inc(*hr.mark("pe", "d"))
                if 1 <= j < 8:
                    n = j - 1
                    pe.wait_ge(*hr.after("dve", f"gr{n}", it))
                    if n >= 1:
                        pe.wait_ge(*hr.after("dve", "dg" if n == 1 else f"mk{n - 2}", it))
                    s, half = LEVELS[n], P // 2
                    for t in range(T):
                        g = h_g[:, t * P:(t + 1) * P]
                        right = g.rearrange("p (n two s) -> p n two s", two=2, s=s)[:, :, 1]
                        o = sc[(n + 1) % 2][:, t * half:(t + 1) * half]
                        ins = mm(o.rearrange("p (n s) -> p n s", s=s), g, right)
                    ins.then_inc(*hr.mark("pe", f"s{n}"))
                if j == 8:
                    pe.wait_ge(*hr.after("dve", "gr7", it))
                    pe.wait_ge(*hr.after("dve", "mk5", it))
                    mm(sc[0][:, 0:P], h_g[:, 0:P], h_g[:, P:S]).then_inc(*hr.mark("pe", "s7"))
                if j == 9:
                    pe.wait_ge(*hr.after("act", "off", it))
                    pe.wait_ge(*hr.after("dve", "mk6", it))
                    v = lambda t: hg[:, 2, t, bass.ds(it * HK, HK)]
                    mm(sc[1][:, 0:HK], h_sc[:, 0], v(0))
                    mm(sc[1][:, HK:2 * HK], h_off[:], v(0), stop=False)
                    mm(sc[1][:, HK:2 * HK], h_sc[:, 1], v(1), start=False).then_inc(*hr.mark("pe", "o"))
            return side

        run(pe, "gate_conv", stream(recur(0)))
        end_phase(pe, "gate_conv", wait=False)
        run(pe, "gate_mem", stream(recur(4)), last=stream(recur(4)), lasts=2,
            first=for_branch(ym_split, lambda t, c: mq[:, t, c:c + P], ma.after("dve", "u", HH // 2 - 1), [0, 1, 2, 3], recur(4)))
        end_phase(pe, "gate_mem", wait=False)
        run(pe, "gate_hg", stream(nothing),
            first=for_branch(yb_split, lambda t, c: hg[:, 3, t, c:c + P], None, [2, 3, 4, 5], nothing, lambda n: hn.after("dve", f"n{n}")))
        end_phase(pe, "gate_hg", wait=False)
        run(pe, "out_2", stepwise(y2_split, lambda t, c: y2[:, t, c:c + P], lambda n: gate_used("gate_hg", n // 2), nothing))
        end_phase(pe, "out_2", wait=False)

        def ffn(i, at_, step):
            st, n = ("g", f_g) if step < 2 else ("v", f_v)
            h = step % 2
            pe.wait_ge(*ffs.after("act", "ev", i))
            if step >= 2:
                pe.wait_ge(*ffs.after("dve", f"b{2 * h + 1}2", i))
            for c in range(2):
                for t in range(T):
                    ins = tr(tp[h][:, c * S + t * P:c * S + (t + 1) * P], n[:, t, (2 * h + c) * P:(2 * h + c + 1) * P])
            ins.then_inc(*ffs.mark("pe", f"{st}{h}"))

        def ffn_side(i, j):
            if j in (0, 1):
                ffn(i, j, j)
            if j in (4, 5):
                ffn(i, j, j - 2)

        run(pe, "ffn_first", stepwise(x2_split, lambda t, c: x2[:, t, c:c + P], lambda n: post1.after("dve", f"x{n // 2}"), nothing))
        run(pe, "ffn_up", stream(ffn_side))
        end_phase(pe, "ffn_up", wait=False)

        def down_first(i, j):
            ffn_side(FT // 4 - 1, j)

        def down_ready(i, j):
            if j == (FT - 4) // 2:
                pe.wait_ge(*ffs.after("dve", "l", FT // 4 - 1))
        run(pe, "ffn_down", stream(nothing), first=stream(down_first, down_ready))

    @block_ctx.scalar
    def _(act):
        def go(o, in_, func=ACT.Copy, **kw):
            return nc.scalar.activation(o, in_, func, **kw)

        def convert(c, slot, size, uses):
            act.wait_ge(loaded[slot], 16 * uses)
            if not (isinstance(c, int) and c < RING):
                act.wait_ge(chunk_done, c - (RING - 1))
            go(hi[:, slot, 0:size], raw[:, slot, 0:size]).then_inc(hi_ready, 1)

        def stream(side, skip_last=False):
            def body(ph, i):
                for j in range(ph.n):
                    c = ph.chunk(i, j + LEAD)
                    if not (skip_last and j + LEAD >= ph.n):
                        slot = (ph.c0 + j + LEAD) % RING
                        size = ph.sizes[j + LEAD] if j + LEAD < ph.n else 2
                        convert(c, slot, size, i * (ph.n // RING) + ((ph.c0 + j + LEAD) // RING + 1))
                    side(i, j)
            return body

        def evacuate(ph, i, blk, dst, scale=None, func=None):
            j = max(k for k, p in enumerate(positions(ph)) if p[0] == blk)
            act.wait_ge(chunk_done, ph.chunk(i, j) + 1)
            for t in range(T):
                kw = dict(func=ACT.Identity, scale=scale[:, t:t + 1]) if scale is not None else dict(func=func) if func else {}
                go(dst(t), acc[blk % 2][t][:], **kw).then_inc(acc_free[blk % 2], 1)

        def ends(ph, j):
            p = positions(ph)[j]
            return p[0] if p[3] else None

        def split_hi(st, dst, n, gain=None):
            act.wait_ge(*st.after("pe", f"t{n}"))
            for kk in range(2):
                k = 2 * n + kk
                kw = dict(func=ACT.Identity, scale=vcol[:, gain[0], gain[1] + k:gain[1] + k + 1]) if gain else {}
                ins = go(dst(k), tp[n % 2][:, kk * S:(kk + 1) * S], **kw)
            ins.then_inc(*st.mark("act", f"h{n}"))

        def square(st, src, bank, n):
            t, q = n % T, n // T
            if n > 0:
                act.wait_ge(*st.after("act", f"sq{n - 1}"))
            go(bank[:], src(t)[:, q * NB:(q + 1) * NB], ACT.Square, accum_out=ss4[:, t, q:q + 1]).then_inc(*st.mark("act", f"sq{n}"))

        def scales(st, src, bank, r):
            def side(i, j):
                if i == 0 and 3 <= j < 7:
                    for n in (2 * j - 6, 2 * j - 5):
                        square(st, src, bank, n)
                if i == 0 and j == 7:
                    act.wait_ge(*st.after("dve", "e"))
                    go(r[:], r[:], ACT.Sqrt).then_inc(*st.mark("act", "rt"))
                    act.wait_ge(*st.after("dve", "r"))
            return side

        def stepwise(st, dst, gain=None):
            for n in range(2):
                split_hi(st, dst, n, gain)

            def side(i, j):
                if i == 0 and j + 2 < BANKS:
                    split_hi(st, dst, j + 2, gain)
            return side

        def norm_steps(st, src, bank, i, j):
            if 0 <= j < 4:
                for n in (2 * j, 2 * j + 1):
                    square(st, src, bank, n)
            if j == 5:
                act.wait_ge(*st.after("dve", "e"))
                go(rn[:], rn[:], ACT.Sqrt).then_inc(*st.mark("act", "rt"))

        def head_root(st, n):
            act.wait_ge(*st.after("dve", "e"))
            go(ssh[:, :, 0:n], ssh[:, :, 0:n], ACT.Sqrt).then_inc(*st.mark("act", "rt"))

        def into(dst, scale, func):
            def side(i, j):
                blk = ends(ph_of[0], j)
                if blk is not None:
                    evacuate(ph_of[0], i, blk, lambda t: dst(t, i, blk), scale(blk), func(i))
            return side

        ph_of = [None]

        def go_phase(name, side=None, dst=None, skip_last=False, peel_first=False, peel_last=0, before=None, scale=lambda b: None,
                     func=lambda i: None):
            ph_of[0] = phases[name]
            both = into(dst, scale, func) if dst else (lambda i, j: None)

            def all_(i, j):
                if before:
                    before(i, j)
                both(i, j)
                if side:
                    side(i, j)

            body = stream(all_, skip_last)
            run(act, name, body, first=body if peel_first else None, last=body if peel_last else None, lasts=peel_last)

        act.wait_ge(*setup.after("dve", "vn"))
        x_hi = stepwise(x_split, lambda k: xh[:, k], V_NORM)
        for c in range(LEAD):
            convert(c, c, 2, 1)

        def a_side(i, j):
            x_hi(i, j)
            if i == 1 and j == 0:
                act.wait_ge(in_wf, 16)
                go(wf_hi[:], wf_raw[:]).then_inc(*setup.mark("act", "wh"))

        go_phase("a_proj", a_side, lambda t, i, b: pa[:, t, bass.ds(i * 2 * NB + b * NB, NB)],
                 before=scales(x_norm, lambda t: x_in[:, t], sc[1], rnx), scale=lambda b: rnx)
        end_phase(act, "a_proj")

        go(a_sq[:], pa[:, :, 0:AW + AKW], ACT.Square).then_inc(*win_prep.mark("act", "sq"))
        head_root(win_prep, AH + AKV)
        z = pa[:, :, AW + 2 * AKW:A_COLS]
        go(z, z, ACT.Silu).then_inc(*win_prep.mark("act", "silu"))

        def window(i, j):
            if isinstance(i, int) and j == -1:
                act.wait_ge(*win_prep.after("pe", "k"))
                go(a_kt[:].rearrange("p a b -> p (a b)"), tp[0][:]).then_inc(*win_prep.mark("act", "k"))
            if j == 0:
                act.wait_ge(*win.after("pe", "q", i))
                go(a_qt[:].rearrange("p a b -> p (a b)"), tp[0][:], ACT.Identity, scale=gqk[:, 0:1]).then_inc(*win.mark("act", "q"))
            if j == 4:
                act.wait_ge(*win.after("dve", "neg", i))
                for g in G4:
                    for t in range(T):
                        n = 2 * g + t
                        part = a_s[:, g, t:2 * t + 1].rearrange("p b k -> p (b k)")
                        ins = go(part, part, ACT.Exp, bias=nmax[:, n:n + 1], accum_out=den[:, n:n + 1])
                ins.then_inc(*win.mark("act", "p"))
                act.wait_ge(*win.after("dve", "es", i))
                go(es[:], es[:], ACT.Exp).then_inc(*win.mark("act", "es"))
            if 6 <= j < 10:
                g = j - 6
                act.wait_ge(*win.after("pe", f"pt{g}", i))
                if g >= 2:
                    act.wait_ge(*win.after("pe", f"o{g - 2}", i))
                go(a_pt[:, g % 2].rearrange("p b k -> p (b k)"), tp[g % 2][:, 0:3 * P]).then_inc(*win.mark("act", f"pt{g}"))

        go_phase("b_proj", late(window), lambda t, i, b: pb[:, t, bass.ds(i * 2 * NB + b * NB, NB)], scale=lambda b: rnx,
                 peel_first=True)
        end_phase(act, "b_proj")

        def c_dst(t, i, b):
            return (pc if b < 2 else mk1)[:, t, (b % 2) * NB:(b % 2 + 1) * NB]

        def c_side(i, j):
            if j == 0:
                act.wait_ge(in_mem, 32)
            norm_steps(norm_m, lambda t: mem_in[t][:], sc[0], i, j)
            if 8 <= j < 16:
                split_hi(norm_m, lambda k: oh[:, k], j - 8, V_MEM)
            if j == 2:
                for t in range(T):
                    if t:
                        act.wait_ge(*fg_prep.after("dve", f"ms{t - 1}"))
                    go(b_sq[:], pb[:, t, 0:2 * BW], ACT.Square).then_inc(*fg_prep.mark("act", f"sq{t}"))
                act.wait_ge(*fg_prep.after("dve", "e"))
                go(ssh[:], ssh[:], ACT.Sqrt).then_inc(*fg_prep.mark("act", "rt"))
            if j == 10:
                zz = pb[:, :, 3 * BW:4 * BW]
                go(zz, zz, ACT.Silu).then_inc(*fg_prep.mark("act", "silu"))
            if j == 12:
                act.wait_ge(*fg_prep.after("dve", "a"))
                go(tf[:], tf[:], ACT.Exp, scale=-1.0).then_inc(*fg_prep.mark("act", "e"))
                act.wait_ge(*fg_prep.after("act", "e"))
                go(tf[:], tf[:], ACT.Ln, bias=1.0).then_inc(*fg_prep.mark("act", "l"))
            if 18 <= j < 21:
                split_hi(ua_split, lambda k: oh[:, 16 + k], j - 18)

            if j == 25:
                ph = ph_of[0]
                act.wait_ge(acc_free[0], 2 * ph.use(i, 2) + T)
                for n, src in enumerate((pc, mk1)):
                    if n:
                        act.wait_ge(*me_prep.after("dve", "ms0"))
                    go(me_sq[:], src[:, :, 0:CW], ACT.Square).then_inc(*me_prep.mark("act", f"sq{n}"))
            if j == 27:
                act.wait_ge(*me_prep.after("dve", "e"))
                go(ssm[:], ssm[:], ACT.Sqrt).then_inc(*me_prep.mark("act", "rt"))
            if j == 29:
                act.wait_ge(acc_free[1], 2 * phases["c_proj"].use(i, 1) + T)
                z3 = pc[:, :, CW:2 * CW]
                go(z3, z3, ACT.Silu).then_inc(*me_prep.mark("act", "silu"))

        go_phase("c_proj", c_side, c_dst, scale=lambda b: rnx if b < 2 else None)
        end_phase(act, "c_proj")

        def for_branch(st, dst, at_, side, gain=None):
            def both(i, j):
                if isinstance(i, int) and i == 0 and j in at_:
                    for n in (n for n, k in enumerate(at_) if k == j):
                        split_hi(st, dst, n, gain)
                if side:
                    side(i, j)
            return both

        def gate_side(name, more=None):
            gates_before = GATES.index(name) * (D // NB)

            def side(i, j):
                ph = ph_of[0]
                if more:
                    more(i, j)
                if j == KT // 2 - 1:
                    act.wait_ge(chunk_done, ph.chunk(i, j) + 1)
                    act.wait_ge(sig_free, i * T + (1 + T * gates_before))
                    for t in range(T):
                        kw = dict(scale=rnx[:, t:t + 1]) if name in ("gate_a", "gate_b", "gate_c") else {}
                        go(sig[:, t], acc[0][t][:], ACT.Sigmoid, **kw).then_inc(acc_free[0], 1)
            return side

        def forget(i, j):
            if j == 0:
                for what, dst, bank in (("q", b_qt, tp[0]), ("k", b_kt, tp[1])):
                    act.wait_ge(*fg.after("pe", what, i))
                    kw = lambda w: dict(func=ACT.Identity, scale=gqk[0:w, 1:2]) if what == "q" else {}
                    go(dst[:, 0], bank[:, 0:S], **kw(P))
                    go(dst[0:HD, 1], bank[0:HD, S:2 * S], **kw(HD)).then_inc(*fg.mark("act", what))
            if j == 4:
                act.wait_ge(*fg.after("dve", "neg", i))
                for g in G3:
                    for t in range(T):
                        n = 2 * g + t
                        part = b_s[:, g, t:2 * t + 1].rearrange("p b k -> p (b k)")
                        ins = go(part, part, ACT.Exp, bias=nmax[:, n:n + 1], accum_out=den[:, n:n + 1])
                ins.then_inc(*fg.mark("act", "p"))
            if 6 <= j < 9:
                g = j - 6
                act.wait_ge(*fg.after("pe", f"pt{g}", i))
                if g >= 2:
                    act.wait_ge(*fg.after("pe", f"o{g - 2}", i))
                go(b_pt[:, g % 2].rearrange("p b k -> p (b k)"), tp[g % 2][:, 0:3 * P]).then_inc(*fg.mark("act", f"pt{g}"))

        go_phase("gate_a", gate_side("gate_a", late(forget)))
        end_phase(act, "gate_a")
        def memory(i, j):
            if j == 0:
                act.wait_ge(*me.after("pe", "qk", i))
                go(c_qt[:], tp[0][:, 0:S], ACT.Identity, scale=gqk[:, 2:3]).then_inc(*me.mark("act", "q"))
                go(c_kt[:], tp[0][:, S:2 * S]).then_inc(*me.mark("act", "k"))
            if j == 3:
                act.wait_ge(*me.after("dve", "m", i))
                for t in range(T):
                    ins = go(c_p[:, t], sc[0][:, t * S:(t + 1) * S], ACT.Exp, bias=nmax[:, t:t + 1], accum_out=den[:, t:t + 1])
                ins.then_inc(*me.mark("act", "p"))
            if j == 5:
                act.wait_ge(*me.after("pe", "pt", i))
                go(c_pt[:].rearrange("p a b -> p (a b)"), tp[1][:]).then_inc(*me.mark("act", "pt"))

        go_phase("gate_b", gate_side("gate_b", for_branch(ub_split, lambda k: oh[:, k], [0, 0, 4], late(memory))), peel_first=True)
        end_phase(act, "gate_b")
        go_phase("gate_c", gate_side("gate_c", for_branch(uc_split, lambda k: oh[:, 6 + k], [0, 1], None)), peel_first=True)
        end_phase(act, "gate_c", wait=False)
        y1_hi = stepwise(y1_split, lambda k: oh[:, OUT_SLOTS[k]])

        def out_side(i, j):
            y1_hi(i, j)
            if j == 8:
                act.wait_ge(in_mem2, 16)
            norm_steps(norm_m2, lambda t: mem2_in[:, t], sc[0], i, j - 8)
            if 16 <= j < 24:
                split_hi(norm_m2, lambda k: m2h[:, k], j - 16, V_MEM2)

        go_phase("out", out_side)
        end_phase(act, "out")

        def mem2_side(i, j):
            norm_steps(norm_x1, lambda t: x1[:, t], sc[0], i, j)
            if 8 <= j < 16:
                split_hi(norm_x1, lambda k: xh[:, k], j - 8, V_MIX)

        go_phase("mem_kv_2", mem2_side, lambda t, i, b: (mk2 if b < 2 else mv2)[:, t, (b % 2) * NB:(b % 2 + 1) * NB])
        end_phase(act, "mem_kv_2")
        go_phase("conv_proj", dst=lambda t, i, b: cv[:, i, t, b * NB:(b + 1) * NB])
        end_phase(act, "conv_proj")
        go_phase("mq_proj", dst=lambda t, i, b: mq[:, t, b * NB:(b + 1) * NB])
        end_phase(act, "mq_proj")

        def hg_side(i, j):
            if j == -1:
                go(cb_st[:], cv[:, 0, :, bass.ds(i * 2 * P, 2 * P)]).then_inc(*conv.mark("act", "cb"))
            if j == 4:
                act.wait_ge(*conv.after("dve", "y", i))
                for n in range(2):
                    ins = go(oh[:, bass.ds(i * 2 + n, 1)].rearrange("p a b -> p (a b)"), v_tm[:, n])
                ins.then_inc(*conv.mark("act", "h"))
                go(d_q[:], mq[:, :, bass.ds(i * MD, MD)], ACT.Copy, scale=MD ** -0.5).then_inc(*ma.mark("act", "sq"))
                go(d_k[:], mk2[:, :, bass.ds(i * MD, MD)]).then_inc(*ma.mark("act", "sk"))
            if j == 5:
                for what, dst, bank in (("q", d_qt, tp[0]), ("k", d_kt, tp[1])):
                    act.wait_ge(*ma.after("pe", what, i))
                    go(dst[:].rearrange("p a b -> p (a b)"), bank[:]).then_inc(*ma.mark("act", what))
            if j == 8:
                act.wait_ge(*ma.after("dve", "m", i))
                for t in range(T):
                    ins = go(d_p[:, t], sc[0][:, t * S:(t + 1) * S], ACT.Exp, bias=nmax[:, t:t + 1], accum_out=den[:, t:t + 1])
                ins.then_inc(*ma.mark("act", "p"))
            if j == 10:
                act.wait_ge(*ma.after("pe", "pt", i))
                go(d_pt[:].rearrange("p a b -> p (a b)"), tp[0][:]).then_inc(*ma.mark("act", "pt"))

        act.wait_ge(out_x1, 16)
        def gates_first(it, step):
            if step == "e1":
                act.wait_ge(*hp1.after("dve", "a", it))
                go(h_l[:], h_l[:], ACT.Exp, scale=-1.0).then_inc(*hp1.mark("act", "e1"))
            else:
                act.wait_ge(*hp1.after("act", "e1", it))
                go(h_l[:], h_l[:], ACT.Ln, bias=1.0).then_inc(*hp1.mark("act", "l1"))

        def gates_second(it, step):
            if step == "e2":
                act.wait_ge(*hp2.after("dve", "d", it))
                go(h_d[:], h_d[:], ACT.Exp, scale=-1.0).then_inc(*hp2.mark("act", "e2"))
            elif step == "k":
                act.wait_ge(*hp2.after("dve", "kz", it))
                go(h_kz[:], h_kz[:], ACT.Exp).then_inc(*hp2.mark("act", "k"))
            else:
                act.wait_ge(*hp2.after("act", "e2", it))
                go(h_d[:], h_d[:], ACT.Ln, bias=1.0).then_inc(*hp2.mark("act", "l2"))

        def hg_all(i, j):
            hg_side(i, j - 1)
            if not isinstance(i, int):
                return
            for n in HEAD_PAIRS.get(j, []):
                if n == 0:
                    act.wait_ge(*conv.after("dve", "u", i))
                act.wait_ge(*hg_prep.after("pe", f"t{n}"))
                dst = (qt if n < 4 else zt)[:, 2 * (n % 4):2 * (n % 4) + 2].rearrange("p a b -> p (a b)")
                go(dst, sc[n % 2][:], ACT.Silu if n < 4 else ACT.Copy).then_inc(*hg_prep.mark("act", f"t{n}"))
            if j == 10:
                gates_first(0, "e1")
                gates_first(0, "l1")
            if j == 12:
                for step in ("e2", "k", "l2"):
                    gates_second(0, step)
            if j == 14:
                gates_first(1, "e1")
                gates_first(1, "l1")

        go_phase("hg_proj", hg_all, lambda t, i, b: hg[:, i, t, b * NB:(b + 1) * NB], peel_last=1,
                 func=lambda i: ACT.Silu if isinstance(i, int) else None)
        end_phase(act, "hg_proj")

        def halves(tensor, s):
            v = tensor.rearrange("p (n two s) -> p n two s", two=2, s=s)
            return v[:, :, 0], v[:, :, 1]

        def recur(first):
            def side(i, j):
                it = i + first
                if j < 8:
                    n = j
                    s = (LEVELS + [P])[n]
                    e, pre, suf = halves(h_e[:], s), halves(h_pre[:], s), halves(h_suf[:], s)
                    if n == 0:
                        act.wait_ge(*hp2.after("dve", "lf0", it))
                    else:
                        act.wait_ge(*hr.after("dve", f"pre{n - 1}", it))
                    go(e[0], suf[0], ACT.Exp).then_inc(*hr.mark("act", f"el{n}"))
                    go(e[1], pre[1], ACT.Exp).then_inc(*hr.mark("act", f"er{n}"))
                if j == 8:
                    act.wait_ge(*hr.after("pe", "s7", it))
                    go(h_off[:], sc[0][:, 0:P]).then_inc(*hr.mark("act", "off"))
                if j == 9:
                    act.wait_ge(*hr.after("pe", "o", it))
                    for t in range(T):
                        go(h_sq[:, t], sc[1][:, t * HK:(t + 1) * HK], ACT.Square,
                           accum_out=h_ss[:, bass.ds(it, 1), t:t + 1].rearrange("p a b -> p (a b)")).then_inc(*hr.mark("act", f"sq{t}"))
                after = lambda n: not (isinstance(it, int) and it + n >= HH)
                if j == 3 and after(2):
                    gates_first(it + 2, "e1")
                if j == 4 and after(1):
                    gates_second(it + 1, "e2")
                if j == 5 and after(1):
                    gates_second(it + 1, "k")
                if j == 8 and after(1):
                    gates_second(it + 1, "l2")
                if j == 8 and after(2):
                    gates_first(it + 2, "l1")
            return side

        go_phase("gate_conv", gate_side("gate_conv", recur(0)))
        end_phase(act, "gate_conv")
        go_phase("gate_mem", gate_side("gate_mem", for_branch(ym_split, lambda k: oh[:, 16 + k], [0, 1, 2, 3], recur(4))),
                 peel_first=True, peel_last=2)
        end_phase(act, "gate_mem")
        def norm_heads(i, j):
            if isinstance(i, int) and j == 0:
                act.wait_ge(*hn.after("dve", "e"))
                go(h_ss[:], h_ss[:], ACT.Sqrt).then_inc(*hn.mark("act", "rt"))

        go_phase("gate_hg", gate_side("gate_hg", for_branch(yb_split, lambda k: oh[:, 8 + k], [2, 3, 4, 5], norm_heads, V_HG)), peel_first=True)
        end_phase(act, "gate_hg", wait=False)
        y2_hi = stepwise(y2_split, lambda k: oh[:, OUT2_SLOTS[k]])

        def keep(st, dst):
            def side(i, j):
                ph = ph_of[0]
                blk = ends(ph, j)
                if blk is None:
                    return
                act.wait_ge(chunk_done, ph.chunk(i, j) + 1)
                if i or blk:
                    last = (i, blk - 1) if blk else (i - 1, ph.blocks - 1)
                    act.wait_ge(acc_free[last[1] % 2], 2 * ph.use(*last) + T)
                for t in range(T):
                    col = i * 2 + blk
                    go(dst[:, t, bass.ds(col * NB, NB)], acc[blk % 2][t][:]).then_inc(*st.mark("act", f"m{col}{t}"))
                    if t:
                        act.wait_ge(acc_free[blk % 2], 2 * ph.use(i, blk) + t)
                    go(sc[0][:], acc[blk % 2][t][:], ACT.Square, accum_out=ss4[:, t, bass.ds(col, 1)]).then_inc(acc_free[blk % 2], 1)
            return side

        go_phase("out_2", keep(mixs, mix), before=y2_hi)
        act.wait_ge(*post1.after("dve", "e"))
        go(rn[:], rn[:], ACT.Sqrt).then_inc(*post1.mark("act", "rt"))
        x2_hi = stepwise(x2_split, lambda k: xh[:, k], V_FFN)
        x2_scales = scales(x2_norm, lambda t: x2[:, t], sc[0], rnf)
        end_phase(act, "out_2", wait=False)

        def ffn_ev(i, blk, ph):
            act.wait_ge(chunk_done, ph.chunk(i, KT // 2 * (blk + 1) - 1) + 1)
            for t in range(T):
                go((f_g, f_v)[blk][:, t], acc[blk][t][:], ACT.Identity, scale=rnf[:, t:t + 1]).then_inc(acc_free[blk], 1)

        def ffn_up(first, ph):
            def side(i, j):
                if not first:
                    x2_scales(i, j)
                    x2_hi(i, j)
                if first and j in (3, 4):
                    ffn_act(i, j - 3)
                if first and j == 8:
                    ffn_hi(i)
                if j == 7:
                    ffn_ev(i, 0, ph)
                if j == 15:
                    ffn_ev(i, 1, ph)
                    act.drain().then_inc(*ffs.mark("act", "ev"))
            return side

        def ffn_act(i, h):
            act.wait_ge(*ffs.after("dve", f"b{2 * h + 1}2", i))
            for c in (2 * h, 2 * h + 1):
                ins = go(f_a[:, c], f_c[:, c], ACT.Gelu_apprx_tanh, bias=vcol[:, V_FB[0], bass.ds(i * 4 + (V_FB[1] + c), 1)])
            ins.then_inc(*ffs.mark("act", f"gelu{h}"))

        def ffn_hi(i):
            act.wait_ge(*ffs.after("dve", "y", i))
            go(fh[:, bass.ds(i * 4, 4)], f_a[:]).then_inc(*ffs.mark("act", "h"))

        run(act, "ffn_first", stream(ffn_up(0, phases["ffn_first"])))
        act.wait_ge(out_x2, 16)
        run(act, "ffn_up", stream(ffn_up(1, phases["ffn_up"])))
        end_phase(act, "ffn_up")
        ph_of[0] = ph = phases["ffn_down"]
        k = keep(ffe, ff)

        def down_first(i, j):
            if j in (3, 4):
                ffn_act(FT // 4 - 1, j - 3)
            if j == 8:
                ffn_hi(FT // 4 - 1)
            if j == 12:
                act.wait_ge(*ffs.after("dve", "l", FT // 4 - 1))
            k(i, j)

        stream(down_first)(ph, 0)
        stream(k, skip_last=True)(ph, 1)
        act.wait_ge(*post2.after("dve", "e"))
        go(rn[:], rn[:], ACT.Sqrt).then_inc(*post2.mark("act", "rt"))

    @block_ctx.vector
    def _(dve):
        v = nc.vector

        def convert(c, slot, size):
            dve.wait_ge(hi_ready, c + 1)
            v.tensor_tensor(lo[:, slot, 0:size], raw[:, slot, 0:size], hi[:, slot, 0:size].bitcast(F32),
                            ALU.subtract).then_inc(lo_ready, 1)

        def stream(side, skip_last=False):
            def body(ph, i):
                for j in range(ph.n):
                    if not (skip_last and j + LEAD >= ph.n):
                        size = ph.sizes[j + LEAD] if j + LEAD < ph.n else 2
                        convert(ph.chunk(i, j + LEAD), (ph.c0 + j + LEAD) % RING, size)
                    side(i, j)
            return body

        nothing = lambda i, j: None

        def split_lo(st, dst, hi_of, n, gain=None):
            dve.wait_ge(*st.after("act", f"h{n}"))
            for kk in range(2):
                k = 2 * n + kk
                src, h = tp[n % 2][:, kk * S:(kk + 1) * S], hi_of(k).bitcast(F32)
                if gain:
                    g = vcol[:, gain[0], gain[1] + k:gain[1] + k + 1]
                    ins = v.scalar_tensor_tensor(dst(k), src, g, h, ALU.mult, ALU.subtract)
                else:
                    ins = v.tensor_tensor(dst(k), src, h, ALU.subtract)
            ins.then_inc(*st.mark("dve", f"l{n}"))

        def root_mean(st, part, n, mean):
            v.tensor_scalar(part, part, 1.0 / mean, EPS, ALU.mult, ALU.add).then_inc(*st.mark("dve", "e"))
            dve.wait_ge(*st.after("act", "rt"))
            v.reciprocal(part, part).then_inc(*st.mark("dve", "r"))

        def norm_steps(st, src, dst, i, j):
            if j == 4:
                dve.wait_ge(*st.after("act", f"sq{4 * T - 1}"))
                v.tensor_reduce(rn[:], ss4[:], AX, ALU.add).then_inc(*st.mark("dve", "ms"))
                dve.wait_ge(*st.after("dve", "ms"))
                v.tensor_scalar(rn[:], rn[:], 1.0 / D, EPS, ALU.mult, ALU.add).then_inc(*st.mark("dve", "e"))
            if j == 5:
                dve.wait_ge(*st.after("act", "rt"))
                v.reciprocal(rn[:], rn[:]).then_inc(*st.mark("dve", "r"))
                dve.wait_ge(*st.after("dve", "r"))
            if j in (6, 7):
                t = j - 6
                v.tensor_scalar(dst(t), src(t), rn[:, t:t + 1], None, ALU.mult).then_inc(*st.mark("dve", f"n{t}"))

        def over(ap, shape):
            return ap.unsqueeze(len(ap.shape)).to_broadcast(shape)

        def scales(st, r):
            def side(i, j):
                if i == 0 and j == 6:
                    dve.wait_ge(*st.after("act", f"sq{4 * T - 1}"))
                    v.tensor_reduce(r[:], ss4[:], AX, ALU.add).then_inc(*st.mark("dve", "ms"))
                    dve.wait_ge(*st.after("dve", "ms"))
                    v.tensor_scalar(r[:], r[:], 1.0 / D, EPS, ALU.mult, ALU.add).then_inc(*st.mark("dve", "e"))
                if i == 0 and j == 7:
                    dve.wait_ge(*st.after("act", "rt"))
                    v.reciprocal(r[:], r[:]).then_inc(*st.mark("dve", "r"))
            return side

        def stepwise(st, dst, hi_of, gain=None):
            for n in range(2):
                split_lo(st, dst, hi_of, n, gain)

            def side(i, j):
                if i == 0 and j + 2 < BANKS:
                    split_lo(st, dst, hi_of, j + 2, gain)
            return side

        dve.wait_ge(*setup.after("pe", "vn"))
        v.tensor_copy(vcol[:, V_NORM[0], 0:KT], sc[0][:, 0:KT]).then_inc(*setup.mark("dve", "vn"))
        x_lo = stepwise(x_split, lambda k: xl[:, k], lambda k: xh[:, k], V_NORM)
        x_scales = scales(x_norm, rnx)
        for c in range(LEAD):
            convert(c, c, 2)

        def a_side(i, j):
            x_lo(i, j)
            x_scales(i, j)
            if i == 1 and j == 1:
                vectors()

        def vectors():
            dve.wait_ge(*setup.after("pe", "v"))
            for g in range(3):
                ins = v.tensor_copy(vcol[:, g, 0:V_ROWS[g]], sc[0][:, g * P:g * P + V_ROWS[g]])
            ins.then_inc(*setup.mark("dve", "v"))
            dve.wait_ge(*setup.after("dve", "v"))
            v.tensor_tensor(gqk[:], vcol[:, 1, V_QK:V_QK + 6:2], vcol[:, 1, V_QK + 1:V_QK + 6:2], ALU.mult).then_inc(*setup.mark("dve", "qk0"))
            dve.wait_ge(*setup.after("dve", "qk0"))
            v.tensor_scalar(gqk[:, 0:2], gqk[:, 0:2], HD ** -0.5, None, ALU.mult)
            v.tensor_scalar(gqk[:, 2:3], gqk[:, 2:3], CD ** -0.5, None, ALU.mult).then_inc(*setup.mark("dve", "qk1"))
            dve.wait_ge(*setup.after("act", "wh"))
            v.tensor_tensor(wf_lo[:], wf_raw[:], wf_hi[:].bitcast(F32), ALU.subtract).then_inc(*setup.mark("dve", "wl"))
            dve.wait_ge(in_const, 16 * N_CONST)
            v.tensor_copy(lmask[:], lmask_in[:]).then_inc(sig_free, 1)

        run(dve, "a_proj", stream(a_side))
        end_phase(dve, "a_proj")

        dve.wait_ge(*win_prep.after("act", "sq"))
        heads = ssh[:, :, 0:AH + AKV]
        v.tensor_reduce(heads, a_sq[:].rearrange("p t (h d) -> p t h d", d=HD), AX, ALU.add).then_inc(*win_prep.mark("dve", "ms"))
        dve.wait_ge(*win_prep.after("dve", "ms"))
        root_mean(win_prep, heads, AH + AKV, HD)
        dve.wait_ge(*win_prep.after("dve", "r"))
        v.tensor_tensor(a_kn[:].rearrange("p t (h d) -> p t h d", d=HD),
                        pa[:, :, AW:AW + AKW].rearrange("p t (h d) -> p t h d", d=HD),
                        over(ssh[:, :, AH:AH + AKV], [P, T, AKV, HD]), ALU.mult).then_inc(*win_prep.mark("dve", "kn"))

        def window(i, j):
            by_g = lambda ap, n: ap.rearrange("p t (g n d) -> p t g n d", n=AG, d=n)[:, :, :, i, :]
            if j == -1:
                r = ssh[:, :, 0:AH].rearrange("p t (g n) -> p t g n", n=AG)[:, :, :, i]
                v.tensor_tensor(a_qn[:], by_g(pa[:, :, 0:AW], HD), over(r, [P, T, AKV, HD]), ALU.mult).then_inc(*win.mark("dve", "qn"))
            if j in (1, 2):
                for g in (2 * j - 2, 2 * j - 1):
                    dve.wait_ge(*win.after("pe", f"s{g}", i))
                    v.scalar_tensor_tensor(a_s[:, g].rearrange("p b k -> p (b k)"), kc[:, K_REL:K_REL + 3 * P],
                                           kc[:, bass.ds(i + (K_SLOPE + AG * g), 1)], sc[g % 2][:, 0:3 * P],
                                           ALU.mult, ALU.add).then_inc(*win.mark("dve", f"s{g}"))
            if j == 3:
                dve.wait_ge(*win.after("dve", "s3", i))
                v.tensor_reduce(m3[:], a_s[:].rearrange("p g b k -> p (g b) k"), AX, ALU.max).then_inc(*win.mark("dve", "m3"))
                dve.wait_ge(*win.after("dve", "m3", i))
                v.tensor_tensor(mm[:], m3[:, 1:12:3], m3[:, 2:12:3], ALU.max).then_inc(*win.mark("dve", "mm"))
                sink = sinks[:].rearrange("p (g n) -> p g n", n=AG)[:, :, i]
                v.tensor_tensor(nmax[:, 0:8:2], m3[:, 0:12:3], sink, ALU.max).then_inc(*win.mark("dve", "n0"))
                dve.wait_ge(*win.after("dve", "mm", i))
                v.tensor_tensor(nmax[:, 1:8:2], mm[:], sink, ALU.max).then_inc(*win.mark("dve", "n1"))
                dve.wait_ge(*win.after("dve", "n1", i))
                v.tensor_scalar(nmax[:], nmax[:], -1.0, None, ALU.mult).then_inc(*win.mark("dve", "neg"))
                dve.wait_ge(*win.after("dve", "neg", i))
                v.tensor_tensor(es[:].rearrange("p (g t) -> p g t", t=T), nmax[:].rearrange("p (g t) -> p g t", t=T),
                                over(sink, [P, AKV, T]), ALU.add).then_inc(*win.mark("dve", "es"))
            if j == 4:
                dve.wait_ge(*win.after("act", "es", i))
                v.tensor_tensor(den[:], den[:], es[:], ALU.add).then_inc(*win.mark("dve", "den"))
                dve.wait_ge(*win.after("dve", "den", i))
                v.reciprocal(rden[:], den[:]).then_inc(*win.mark("dve", "rd"))
            if j == 11:
                dve.wait_ge(*win.after("pe", "o3", i))
                r = rden[:].rearrange("p (g t) -> p t g", t=T)
                v.tensor_tensor(a_o[:], sc[0][:].rearrange("p (t g d) -> p t g d", t=T, g=AKV), over(r, [P, T, AKV, HD]),
                                ALU.mult).then_inc(*win.mark("dve", "on"))
                dve.wait_ge(*win.after("dve", "on", i))
                z = by_g(pa[:, :, AW + 2 * AKW:A_COLS], HD)
                v.tensor_tensor(z, a_o[:], z, ALU.mult).then_inc(*win.mark("dve", "u"))

        run(dve, "b_proj", stream(late(window)))
        end_phase(dve, "b_proj")

        def c_side(i, j):
            norm_steps(norm_m, lambda t: mem_in[t][:], lambda t: mem_in[t][:], i, j)
            if 8 <= j < 16:
                split_lo(norm_m, lambda k: ol[:, k], lambda k: oh[:, k], j - 8, V_MEM)
            if j == 1:
                dve.wait_ge(*fg_prep.after("pe", "f"))
                v.tensor_copy(ct[0:BH], sc[1][0:BH, 0:S]).then_inc(*fg_prep.mark("dve", "f"))
            if j == 2:
                for t in range(T):
                    dve.wait_ge(*fg_prep.after("act", f"sq{t}"))
                    v.tensor_reduce(ssh[:, t], b_sq[:].rearrange("p (h d) -> p h d", d=HD), AX, ALU.add).then_inc(*fg_prep.mark("dve", f"ms{t}"))
                dve.wait_ge(*fg_prep.after("dve", "ms1"))
                root_mean(fg_prep, ssh[:], 2 * BH, HD)
                dve.wait_ge(*fg_prep.after("pe", "ft"))
                for t in range(T):
                    ins = v.scalar_tensor_tensor(logf[:, t], sc[1][:, t * BH:(t + 1) * BH], rnx[:, t:t + 1], bfor[:], ALU.mult, ALU.add)
                ins.then_inc(*fg_prep.mark("dve", "z"))
                dve.wait_ge(*fg_prep.after("dve", "z"))
                v.scalar_tensor_tensor(tf[:], logf[:], -1.0, logf[:], ALU.mult, ALU.max).then_inc(*fg_prep.mark("dve", "a"))
            if j == 12:
                dve.wait_ge(*fg_prep.after("act", "l"))
                v.scalar_tensor_tensor(logf[:], logf[:], 0.0, tf[:], ALU.min, ALU.subtract).then_inc(*fg_prep.mark("dve", "lf"))
            if j == 14:
                dve.wait_ge(*fg_prep.after("pe", "c"))
                v.tensor_copy(cq[:].rearrange("p t h -> p (t h)"), sc[0][:, 0:T * BH]).then_inc(*fg_prep.mark("dve", "c"))
            if j == 16:
                dve.wait_ge(*fg_prep.after("pe", "ct"))
                v.tensor_scalar(ct[0:BH], sc[1][0:BH, 0:S], -1.0, None, ALU.mult).then_inc(*fg_prep.mark("dve", "ct"))
            if 18 <= j < 21:
                split_lo(ua_split, lambda k: ol[:, 16 + k], lambda k: oh[:, 16 + k], j - 18)

            if j == 25:
                for n in range(2):
                    dve.wait_ge(*me_prep.after("act", f"sq{n}"))
                    v.tensor_reduce(ssm[:, :, n * CH:(n + 1) * CH], me_sq[:].rearrange("p t (h d) -> p t h d", d=CD), AX, ALU.add).then_inc(*me_prep.mark("dve", f"ms{n}"))
            if j == 27:
                dve.wait_ge(*me_prep.after("dve", "ms1"))
                root_mean(me_prep, ssm[:], 2 * CH, CD)

        run(dve, "c_proj", stream(c_side))
        end_phase(dve, "c_proj")

        def for_branch(st, dst, hi_of, at_, side, gain=None):
            def both(i, j):
                if isinstance(i, int) and i == 0 and j in at_:
                    for n in (n for n, k in enumerate(at_) if k == j):
                        split_lo(st, dst, hi_of, n, gain)
                if side:
                    side(i, j)
            return both

        def gate_side(ph, y, first, more=None):
            def side(i, j):
                if more:
                    more(i, j)
                if j != ph.n - 1:
                    return
                dve.wait_ge(acc_free[0], 2 * ph.use(i, 0) + T)
                dve.wait_ge(chunk_done, ph.chunk(i, j) + 1)
                for t in range(T):
                    v.tensor_tensor(sig[:, t], sig[:, t], acc[1][t][:], ALU.mult).then_inc(acc_free[1], 1)
                for t in range(T):
                    dve.wait_ge(acc_free[1], 2 * ph.use(i, 1) + t + 1)
                    col = y[:, t, bass.ds(i * NB, NB)]
                    if first:
                        v.tensor_copy(col, sig[:, t]).then_inc(sig_free, 1)
                    else:
                        v.tensor_tensor(col, col, sig[:, t], ALU.add).then_inc(sig_free, 1)
            return side

        def forget(i, j):
            if j == -1:
                for what, dst, col, h0 in (("qn", b_qn, 0, 0), ("kn", b_kn, BW, BH)):
                    src = pb[:, :, bass.ds(i * AG * HD + col, AG * HD)].rearrange("p t (h d) -> p t h d", d=HD)
                    v.tensor_tensor(dst[:], src, over(ssh[:, :, bass.ds(i * AG + h0, AG)], [P, T, AG, HD]), ALU.mult).then_inc(*fg.mark("dve", what))
            if j in (1, 2):
                dve.wait_ge(in_nck, 16)
                for g in ((0, 1) if j == 1 else (2,)):
                    dve.wait_ge(*fg.after("pe", f"s{g}", i))
                    h = bass.ds(i * AG + g, 1)
                    flat = lambda ap: ap.rearrange("p a b -> p (a b)")
                    v.scalar_tensor_tensor(b_s[:, g, 0], sc[g % 2][:, 0:P], cq[:, 0, h], flat(nck[:, h, 0:P]), ALU.add, ALU.add)
                    v.scalar_tensor_tensor(flat(b_s[:, g, 1:3]), sc[g % 2][:, P:3 * P], cq[:, 1, h], flat(nck[:, h, :]),
                                           ALU.add, ALU.add).then_inc(*fg.mark("dve", f"s{g}"))
            if j == 3:
                dve.wait_ge(*fg.after("dve", "s2", i))
                own = b_s[:, :, 0:3:2, :]
                mask = kc[:, K_MASK:K_MASK + P].unsqueeze(1).unsqueeze(1).to_broadcast([P, AG, 2, P])
                v.tensor_tensor(own, own, mask, ALU.add).then_inc(*fg.mark("dve", "mask"))
                dve.wait_ge(*fg.after("dve", "mask", i))
                v.tensor_reduce(m3[:, 0:9], b_s[:].rearrange("p g b k -> p (g b) k"), AX, ALU.max).then_inc(*fg.mark("dve", "m3"))
                dve.wait_ge(*fg.after("dve", "m3", i))
                v.tensor_tensor(mm[:, 0:3], m3[:, 1:9:3], m3[:, 2:9:3], ALU.max).then_inc(*fg.mark("dve", "mm"))
                v.tensor_scalar(nmax[:, 0:6:2], m3[:, 0:9:3], -1.0, None, ALU.mult).then_inc(*fg.mark("dve", "n0"))
                dve.wait_ge(*fg.after("dve", "mm", i))
                v.tensor_scalar(nmax[:, 1:6:2], mm[:, 0:3], -1.0, None, ALU.mult).then_inc(*fg.mark("dve", "neg"))
            if j == 5:
                dve.wait_ge(*fg.after("act", "p", i))
                v.reciprocal(rden[:, 0:6], den[:, 0:6]).then_inc(*fg.mark("dve", "rd"))
            if j == 10:
                dve.wait_ge(*fg.after("pe", "o2", i))
                dve.wait_ge(*fg.after("dve", "rd", i))
                o = sc[0][:].rearrange("p (t c) -> p t c", t=T)[:, :, 0:AG * HD].rearrange("p t (g d) -> p t g d", d=HD)
                r = rden[:, 0:6].rearrange("p (g t) -> p t g", t=T)
                v.tensor_tensor(b_o[:], o, over(r, [P, T, AG, HD]), ALU.mult).then_inc(*fg.mark("dve", "on"))
                dve.wait_ge(*fg.after("dve", "on", i))
                z = pb[:, :, bass.ds(i * AG * HD + 3 * BW, AG * HD)].rearrange("p t (h d) -> p t h d", d=HD)
                v.tensor_tensor(z, b_o[:], z, ALU.mult).then_inc(*fg.mark("dve", "u"))

        run(dve, "gate_a", stream(gate_side(phases["gate_a"], y1, True, late(forget))))
        end_phase(dve, "gate_a")
        def memory(i, j):
            if j == -1:
                dve.wait_ge(*me_prep.after("dve", "r"))
                for what, dst, src, h0 in (("qn", c_qn, pc, 0), ("kn", c_kn, mk1, CH)):
                    r = ssm[:, :, bass.ds(i + h0, 1)].to_broadcast([P, T, CD])
                    v.tensor_tensor(dst[:], src[:, :, bass.ds(i * CD, CD)], r, ALU.mult).then_inc(*me.mark("dve", what))
            if j == 2:
                dve.wait_ge(*me.after("pe", "s", i))
                v.tensor_reduce(nmax[:, 0:T], sc[0][:].rearrange("p (t m) -> p t m", t=T), AX, ALU.max, negate=True).then_inc(*me.mark("dve", "m"))
            if j == 4:
                dve.wait_ge(*me.after("act", "p", i))
                v.reciprocal(rden[:, 0:T], den[:, 0:T]).then_inc(*me.mark("dve", "rd"))
            if j == 7:
                dve.wait_ge(*me.after("pe", "o", i))
                dve.wait_ge(*me.after("dve", "rd", i))
                o = sc[1][:, 0:T * CD].rearrange("p (t d) -> p t d", t=T)
                v.tensor_tensor(c_qn[:], o, over(rden[:, 0:T], [P, T, CD]), ALU.mult).then_inc(*me.mark("dve", "on"))
                dve.wait_ge(*me.after("dve", "on", i))
                z = pc[:, :, bass.ds(i * CD + CW, CD)]
                v.tensor_tensor(z, c_qn[:], z, ALU.mult).then_inc(*me.mark("dve", "u"))

        body = stream(gate_side(phases["gate_b"], y1, False, for_branch(
            ub_split, lambda k: ol[:, k], lambda k: oh[:, k], [0, 0, 4], late(memory))))
        run(dve, "gate_b", body, first=body)
        end_phase(dve, "gate_b")
        body = stream(gate_side(phases["gate_c"], y1, False, for_branch(
            uc_split, lambda k: ol[:, 6 + k], lambda k: oh[:, 6 + k], [0, 1], None)))
        run(dve, "gate_c", body, first=body)
        end_phase(dve, "gate_c", wait=False)
        y1_lo = stepwise(y1_split, lambda k: ol[:, OUT_SLOTS[k]], lambda k: oh[:, OUT_SLOTS[k]])

        def out_side(i, j):
            ph = phases["out"]
            y1_lo(i, j)
            norm_steps(norm_m2, lambda t: mem2_in[:, t], lambda t: mem2_in[:, t], i, j - 8)
            if 16 <= j < 24:
                split_lo(norm_m2, lambda k: m2l[:, k], lambda k: m2h[:, k], j - 16, V_MEM2)
            blk, _, _, last = positions(ph)[j]
            if last:
                dve.wait_ge(in_x_again, 16)
                dve.wait_ge(chunk_done, ph.chunk(i, j) + 1)
                for t in range(T):
                    cols = slice(blk * NB, (blk + 1) * NB)
                    v.tensor_tensor(x1[:, t, cols], acc[blk % 2][t][:], x_again[:, t, cols], ALU.add).then_inc(acc_free[blk % 2], 1)
                dve.drain().then_inc(*out1.mark("dve", f"x{blk}"))

        run(dve, "out", stream(out_side))
        end_phase(dve, "out")

        def mem2_side(i, j):
            norm_steps(norm_x1, lambda t: x1[:, t], lambda t: x1n[:, t], i, j)
            if 8 <= j < 16:
                split_lo(norm_x1, lambda k: xl[:, k], lambda k: xh[:, k], j - 8, V_MIX)

        run(dve, "mem_kv_2", stream(mem2_side))
        end_phase(dve, "mem_kv_2")
        run(dve, "conv_proj", stream(nothing))
        end_phase(dve, "conv_proj")
        run(dve, "mq_proj", stream(nothing))
        end_phase(dve, "mq_proj")

        def hg_side(i, j):
            if j == -1:
                part = lambda n: cv[:, n, :, bass.ds(i * 2 * P, 2 * P)]
                v.tensor_tensor(u_st[:].rearrange("p t a b -> p t (a b)"), part(1), part(2), ALU.mult).then_inc(*conv.mark("dve", "u"))
            if j == 1:
                dve.wait_ge(*conv.after("pe", "u", i))
                w = lambda k, n: vcol[:, V_CONV[0], bass.ds(i * 2 + (V_CONV[1] + 8 * k + n), 1)]
                u = lambda n: tp[0][:, n * S:(n + 1) * S]
                for n in range(2):
                    ins = v.tensor_scalar(v_tm[:, n], u(n), w(2, n), None, ALU.mult)
                ins.then_inc(*conv.mark("dve", "c0"))
                for back in (1, 2):
                    dve.wait_ge(*conv.after("dve", f"c{back - 1}", i))
                    for n in range(2):
                        ins = v.scalar_tensor_tensor(v_tm[:, n, back:S], u(n)[:, 0:S - back], w(2 - back, n), v_tm[:, n, back:S], ALU.mult, ALU.add)
                    ins.then_inc(*conv.mark("dve", f"c{back}"))
                dve.wait_ge(*conv.after("pe", "b", i))
                dve.wait_ge(*conv.after("dve", "c2", i))
                flat = v_tm[:].rearrange("p a b -> p (a b)")
                v.tensor_tensor(flat, flat, tp[1][:], ALU.mult).then_inc(*conv.mark("dve", "y"))
            if j == 4:
                dve.wait_ge(*conv.after("act", "h", i))
                k = bass.ds(i * 2, 2)
                v.tensor_tensor(ol[:, k], v_tm[:], oh[:, k].bitcast(F32), ALU.subtract).then_inc(*conv.mark("dve", "l"))
            if j == 7:
                dve.wait_ge(*ma.after("pe", "s", i))
                v.tensor_reduce(nmax[:, 0:T], sc[0][:].rearrange("p (t m) -> p t m", t=T), AX, ALU.max, negate=True).then_inc(*ma.mark("dve", "m"))
            if j == 9:
                dve.wait_ge(*ma.after("act", "p", i))
                v.reciprocal(rden[:, 0:T], den[:, 0:T]).then_inc(*ma.mark("dve", "rd"))
            if j == 12:
                dve.wait_ge(*ma.after("pe", "o", i))
                dve.wait_ge(*ma.after("dve", "rd", i))
                v.tensor_tensor(mq[:, :, bass.ds(i * MD, MD)], sc[1][:].rearrange("p (t d) -> p t d", t=T),
                                over(rden[:, 0:T], [P, T, MD]), ALU.mult).then_inc(*ma.mark("dve", "u"))


        def halves(tensor, s):
            w = tensor.rearrange("p (n two s) -> p n two s", two=2, s=s)
            return w[:, :, 0], w[:, :, 1]

        def gates_first(it):
            z = zt[:, bass.ds(it, 1)].rearrange("p a b -> p (a b)")
            v.scalar_tensor_tensor(h_l[:], z, -1.0, z, ALU.mult, ALU.max).then_inc(*hp1.mark("dve", "a"))

        def gates_second(it):
            z = zt[:, bass.ds(it, 1)].rearrange("p a b -> p (a b)")
            dve.wait_ge(*hp1.after("act", "l1", it))
            v.scalar_tensor_tensor(h_ls[:], z, 0.0, h_l[:], ALU.min, ALU.subtract).then_inc(*hp2.mark("dve", "ls"))
            dve.wait_ge(*hp2.after("dve", "ls", it))
            v.tensor_scalar(h_d[:], h_ls[:], LOG_TINY, None, ALU.subtract).then_inc(*hp2.mark("dve", "d0"))
            dve.wait_ge(*hp2.after("dve", "d0", it))
            v.scalar_tensor_tensor(h_d[:], h_d[:], -1.0, h_d[:], ALU.mult, ALU.max).then_inc(*hp2.mark("dve", "d"))
            v.tensor_tensor(h_kz[:], h_ls[:], z, ALU.subtract).then_inc(*hp2.mark("dve", "kz"))

        def gates_third(it):
            dve.wait_ge(*hp2.after("act", "l2", it))
            v.scalar_tensor_tensor(h_pre[:], h_ls[:], LOG_TINY, h_d[:], ALU.max, ALU.add).then_inc(*hp2.mark("dve", "lf"))
            dve.wait_ge(*hp2.after("dve", "lf", it))
            v.memset(h_suf[:], 0.0)
            v.tensor_scalar(h_pre[:], h_pre[:], 0.0, None, ALU.min).then_inc(*hp2.mark("dve", "lf0"))
            v.tensor_scalar(h_k[:], h_kz[:], 1e-30, HK ** -0.5, ALU.subtract, ALU.mult).then_inc(*hp2.mark("dve", "k"))

        def hg_all(i, j):
            hg_side(i, j - 1)
            if not isinstance(i, int):
                return
            if j == 9:
                dve.wait_ge(*hg_prep.after("act", "t7"))
                dve.wait_ge(*ma.after("pe", "k", i))
                gates_first(0)
            if j == 11:
                gates_second(0)
            if j == 13:
                gates_first(1)
                gates_third(0)

        body = stream(hg_all)
        run(dve, "hg_proj", body, last=body)
        end_phase(dve, "hg_proj")

        def recur(first):
            def side(i, j):
                it = i + first
                q = qt[:, bass.ds(it, 1)].rearrange("p a b -> p (a b)")
                if j == 0:
                    dve.wait_ge(*hr.after("pe", "d", it))
                    v.tensor_tensor(h_sc[:], sc[0][:, 0:T * P].rearrange("p (t k) -> p t k", t=T),
                                    ident.unsqueeze(1).to_broadcast([P, T, P]), ALU.mult).then_inc(*hr.mark("dve", "dg"))
                if j < 8:
                    n = j
                    s = (LEVELS + [P])[n]
                    e, g, pre, suf = (halves(w[:], s) for w in (h_e, h_g, h_pre, h_suf))
                    dve.wait_ge(*hr.after("act", f"el{n}", it))
                    if n >= 1:
                        dve.wait_ge(*hr.after("pe", f"s{n - 1}", it))
                    if n == len(LEVELS):
                        dve.wait_ge(*hr.after("dve", f"mk{n - 2}", it))
                    v.tensor_tensor(g[0], e[0], halves(h_k[:], s)[0], ALU.mult).then_inc(*hr.mark("dve", f"gl{n}"))
                    dve.wait_ge(*hr.after("act", f"er{n}", it))
                    v.tensor_tensor(g[1], e[1], halves(q, s)[1], ALU.mult).then_inc(*hr.mark("dve", f"gr{n}"))
                    if n < len(LEVELS):
                        shape = [P, S // (2 * s), s]
                        v.tensor_tensor(suf[0], suf[0], pre[1][:, :, s - 1:s].to_broadcast(shape), ALU.add).then_inc(*hr.mark("dve", f"suf{n}"))
                        dve.wait_ge(*hr.after("dve", f"suf{n}", it))
                        v.tensor_tensor(pre[1], pre[1], pre[0][:, :, s - 1:s].to_broadcast(shape), ALU.add).then_inc(*hr.mark("dve", f"pre{n}"))
                    if n >= 1:
                        s = LEVELS[n - 1]
                        shape = [P, T, P // (2 * s), s]
                        v.copy_predicated(h_sc[:].rearrange("p t (n two s) -> p t n two s", two=2, s=s)[:, :, :, 1],
                                          halves(lmask[:, n - 1], s)[1].unsqueeze(1).to_broadcast(shape),
                                          sc[n % 2][:, 0:T * P // 2].rearrange("p (t n s) -> p t n s", t=T, s=s)).then_inc(*hr.mark("dve", f"mk{n - 1}"))
                after = lambda n: not (isinstance(it, int) and it + n >= HH)
                if j == 1 and after(1):
                    gates_second(it + 1)
                if j == 2 and after(2):
                    gates_first(it + 2)
                if j == 9:
                    dve.wait_ge(*hr.after("act", "sq1", it))
                    u = hg[:, 3, :, bass.ds(it * HK, HK)]
                    v.tensor_tensor(u, sc[1][:, 0:T * HK].rearrange("p (t d) -> p t d", t=T), u, ALU.mult).then_inc(*hr.mark("dve", "u"))
                if j == 10 and after(1):
                    gates_third(it + 1)
            return side

        dve.wait_ge(sig_free, 1)
        run(dve, "gate_conv", stream(gate_side(phases["gate_conv"], y2, True, recur(0))))
        end_phase(dve, "gate_conv")
        body = stream(gate_side(phases["gate_mem"], y2, False, for_branch(
            ym_split, lambda k: ol[:, 16 + k], lambda k: oh[:, 16 + k], [0, 1, 2, 3], recur(4))))
        run(dve, "gate_mem", body, first=body, last=body, lasts=2)
        end_phase(dve, "gate_mem")
        def norm_heads(i, j):
            if not isinstance(i, int):
                return
            if j == 0:
                v.tensor_scalar(h_ss[:], h_ss[:], 1.0 / HK, EPS, ALU.mult, ALU.add).then_inc(*hn.mark("dve", "e"))
                dve.wait_ge(*hn.after("act", "rt"))
                v.reciprocal(h_ss[:], h_ss[:]).then_inc(*hn.mark("dve", "r"))
                dve.wait_ge(*hn.after("dve", "r"))
            if 1 <= j < 5:
                n = j - 1
                u = hg[:, 3, :, n * 2 * HK:(n + 1) * 2 * HK].rearrange("p t (h d) -> p t h d", d=HK)
                r = h_ss[:, 2 * n:2 * n + 2].rearrange("p h t -> p t h")
                v.tensor_tensor(u, u, over(r, [P, T, 2, HK]), ALU.mult).then_inc(*hn.mark("dve", f"n{n}"))

        body = stream(gate_side(phases["gate_hg"], y2, False, for_branch(
            yb_split, lambda k: ol[:, 8 + k], lambda k: oh[:, 8 + k], [2, 3, 4, 5], norm_heads, V_HG)))
        run(dve, "gate_hg", body, first=body)
        end_phase(dve, "gate_hg", wait=False)
        y2_lo = stepwise(y2_split, lambda k: ol[:, OUT2_SLOTS[k]], lambda k: oh[:, OUT2_SLOTS[k]])

        def gain_block(st, kept, src, gain, b):
            dve.wait_ge(*kept.after("act", f"m{b}{T - 1}"))
            part = src[:, :, b * NB:(b + 1) * NB]
            v.tensor_tensor(part, part, gain[:, b * NB:(b + 1) * NB].unsqueeze(1).to_broadcast([P, T, NB]), ALU.mult).then_inc(*st.mark("dve", f"w{b}"))

        def post_scale(st, kept, ph, src, gain):
            dve.wait_ge(acc_free[1], 2 * ph.use(ph.times - 1, ph.blocks - 1) + T)
            v.tensor_reduce(rn[:], ss4[:], AX, ALU.add).then_inc(*st.mark("dve", "ms"))
            dve.wait_ge(*st.after("dve", "ms"))
            v.tensor_scalar(rn[:], rn[:], 1.0 / D, EPS, ALU.mult, ALU.add).then_inc(*st.mark("dve", "e"))
            gain_block(st, kept, src, gain, 3)
            dve.wait_ge(*st.after("act", "rt"))
            v.reciprocal(rn[:], rn[:]).then_inc(*st.mark("dve", "r"))
            dve.wait_ge(*st.after("dve", "r"))

        def post(st, src, res, q):
            cols = slice(q * NB, (q + 1) * NB)
            for t in range(T):
                ins = v.scalar_tensor_tensor(res[:, t, cols], src[:, t, cols], rn[:, t:t + 1], res[:, t, cols], ALU.mult, ALU.add)
            ins.then_inc(*st.mark("dve", f"x{q}"))

        def out2_side(i, j):
            y2_lo(i, j)
            if j in (10, 18, 26):
                dve.wait_ge(in_x1, 32)
                gain_block(post1, mixs, mix, gpost, j // 8 - 1)

        run(dve, "out_2", stream(out2_side))
        post_scale(post1, mixs, phases["out_2"], mix, gpost)
        for q in range(2):
            post(post1, mix, x2, q)
        x2_lo = stepwise(x2_split, lambda k: xl[:, k], lambda k: xh[:, k], V_FFN)
        x2_scales = scales(x2_norm, rnf)
        end_phase(dve, "out_2", wait=False)

        def first_side(i, j):
            if j in (0, 2):
                post(post1, mix, x2, j // 2 + 2)
            x2_lo(i, j)
            x2_scales(i, j)

        def ffn_conv(i, h):
            dve.wait_ge(*ffs.after("pe", f"g{h}", i))
            for c in (2 * h, 2 * h + 1):
                w = lambda k: vcol[:, V_FW[k][0], bass.ds(i * 4 + (V_FW[k][1] + c), 1)]
                u = tp[h][:, (c % 2) * S:(c % 2 + 1) * S]
                v.tensor_scalar(f_c[:, c], u, w(2), None, ALU.mult).then_inc(*ffs.mark("dve", f"c{c}"))
                dve.wait_ge(*ffs.after("dve", f"c{c}", i))
                for back in (1, 2):
                    v.scalar_tensor_tensor(f_c[:, c, back:S], u[:, 0:S - back], w(2 - back), f_c[:, c, back:S],
                                           ALU.mult, ALU.add).then_inc(*ffs.mark("dve", f"b{c}{back}"))
                    dve.wait_ge(*ffs.after("dve", f"b{c}{back}", i))

        def ffn_mul(i):
            dve.wait_ge(*ffs.after("act", "gelu1", i))
            for h in range(2):
                dve.wait_ge(*ffs.after("pe", f"v{h}", i))
                part = f_a[:, 2 * h:2 * h + 2].rearrange("p a b -> p (a b)")
                ins = v.tensor_tensor(part, part, tp[h][:], ALU.mult)
            ins.then_inc(*ffs.mark("dve", "y"))

        def ffn_lo(i):
            dve.wait_ge(*ffs.after("act", "h", i))
            k = bass.ds(i * 4, 4)
            v.tensor_tensor(fl[:, k], f_a[:], fh[:, k].bitcast(F32), ALU.subtract).then_inc(*ffs.mark("dve", "l"))

        def ffn_side(i, j):
            if j in (1, 2):
                ffn_conv(i, j - 1)
            if j == 6:
                ffn_mul(i)
            if j == 9:
                ffn_lo(i)

        run(dve, "ffn_first", stream(first_side))
        dve.wait_ge(out_x2, 16)
        run(dve, "ffn_up", stream(ffn_side))
        end_phase(dve, "ffn_up")
        ph = phases["ffn_down"]

        def down_side(i, j):
            if i == 0:
                ffn_side(FT // 4 - 1, j)
            if (i, j) in ((0, 26), (1, 2), (1, 26)):
                dve.wait_ge(in_x2, 32)
                gain_block(post2, ffe, ff, gpost2, 2 * i + j // 24 - 1)

        stream(down_side)(ph, 0)
        stream(down_side, skip_last=True)(ph, 1)
        post_scale(post2, ffe, ph, ff, gpost2)
        for q in range(4):
            post(post2, ff, x2b, q)

    ctx.close()


def kernel(**inputs):
    import numpy as _np
    import concourse.bacc as _bacc
    from concourse import mybir as _mybir
    from concourse.bass_utils import run_bass_kernel_spmd as _run

    nc = _bacc.Bacc("TRN2", target_bir_lowering=False, num_devices=1)
    constants, level_masks = shape_constants()
    arrays, args = {}, {}
    given = {n: _np.ascontiguousarray(a) for n, a in inputs.items() if n != "hg_lower_bounds_2"}
    for name, a in {**given, "constants": constants, "level_masks": level_masks}.items():
        arrays[f"in_{name}"] = a
        args[name] = nc.dram_tensor(f"in_{name}", a.shape, _mybir.dt.from_np(a.dtype), kind="ExternalInput").ap()
    out = nc.dram_tensor("out_x", (1, S, D), F32, kind="ExternalOutput").ap()
    two_blocks(nc, out=out, **args)
    r = _run(nc, [arrays], core_ids=[0])
    return r.results[0]["out_x"]
```
